# Optimizing a Trainium2 kernel written in Bass

```python
import jax, jax.numpy as jnp
from jax import lax
import numpy as np

D_MODEL = 1024
BATCH = 1
SEQ = 128
DEPTH = 2
DEC_BATCH = 1
DEC_SEQ = 1024
PAST_LEN = 128

GRID_W = 64
N_EVEN = (DEPTH + 1) // 2
N_ODD = DEPTH // 2
EPS = 1e-6
W_A = D_MODEL
H_A = 8
BW_A = W_A // H_A
CONV_W = 4
LRU_C = 8.0
W_B = D_MODEL
G_B = 8
GW_B = W_B // G_B
IN_E = 2 * W_A + 2 * W_B
OUT_E = W_A + W_B
H_C = 8
DK_C = D_MODEL // H_C
DV_C = 2 * D_MODEL // H_C
QK_C = H_C * DK_C
W_C = H_C * DV_C
IN_O = 2 * QK_C + 3 * W_C + 4 * H_C
CHUNK = 128

kernel_name = 'hybrid_rglru_fourier_mlstm_step'

def rms_norm(x, g):
    xf = x.astype(jnp.float32)
    y = xf * lax.rsqrt(jnp.mean(xf * xf, axis=-1, keepdims=True) + EPS)
    return (y * g.astype(jnp.float32)).astype(x.dtype)

def ada_mod(cond, w, b):
    m = jax.nn.silu(cond) @ w + b
    return jnp.split(m[:, None, :], 3, axis=-1)

def centred_dwconv(x, w, b):
    y = lax.conv_general_dilated(
        x, w[:, None, :].astype(x.dtype), window_strides=(1,),
        padding=[(CONV_W // 2, CONV_W - 1 - CONV_W // 2)],
        dimension_numbers=('NWC', 'WIO', 'NWC'), feature_group_count=x.shape[-1])
    return y + b

def block_diag(x, w):
    bsz, L, _ = x.shape
    nb, bi, bo = w.shape
    return jnp.einsum('blhi,hij->blhj', x.reshape(bsz, L, nb, bi), w).reshape(bsz, L, nb * bo)

def _lin_combine(e1, e2):
    a1, b1 = e1
    a2, b2 = e2
    return a1 * a2, a2 * b1 + b2

def rglru(x, w_r, b_r, w_i, b_i, lam, h0):
    r = jax.nn.sigmoid(block_diag(x, w_r) + b_r)
    i = jax.nn.sigmoid(block_diag(x, w_i) + b_i)
    log_a = -LRU_C * r * jax.nn.softplus(-lam)
    a = jnp.exp(log_a)
    u = jnp.sqrt(-jnp.expm1(2.0 * log_a)) * (i * x)
    u = u.at[:, 0].add(a[:, 0] * h0)
    _, h = lax.associative_scan(_lin_combine, (a, u), axis=1)
    return h, h[:, -1]

def mixer_ab(h, h0, w_in, conv_w, conv_b, w_r, b_r, w_i, b_i, lam, w_four, b_four, w_out):
    f32 = jnp.float32
    bsz, L, _ = h.shape
    proj = h @ w_in
    xa, za, xb, zb = jnp.split(proj, [W_A, 2 * W_A, 2 * W_A + W_B], axis=-1)
    xa = centred_dwconv(xa, conv_w, conv_b).astype(f32)
    ya = 0.0
    finals = []
    for d in range(2):
        xd = jnp.flip(xa, 1) if d else xa
        hd, hT = rglru(xd, w_r[d].astype(f32), b_r[d].astype(f32), w_i[d].astype(f32),
                       b_i[d].astype(f32), lam[d].astype(f32), h0[:, d].astype(f32))
        ya = ya + (jnp.flip(hd, 1) if d else hd)
        finals.append(hT)
    xg = xb.astype(f32).reshape(bsz, L, G_B, GW_B)
    fr = jnp.fft.fft2(xg, axes=(1, 3), norm='ortho').real
    yb = jnp.einsum('blgi,gij->blgj', fr, w_four.astype(f32)).reshape(bsz, L, W_B) + b_four.astype(f32)
    y = jnp.concatenate([ya.astype(h.dtype) * jax.nn.silu(za),
                         yb.astype(h.dtype) * jax.nn.silu(zb)], axis=-1)
    return y @ w_out, jnp.stack(finals, axis=1)

def mlstm_chunkwise(q, k, v, i_pre, f_pre, C0, n0, m0):
    bsz, L = q.shape[:2]
    nc = L // CHUNK

    def chunks(t):
        t = t.reshape((bsz, nc, CHUNK) + t.shape[2:])
        return jnp.moveaxis(t, (1, 3), (0, 2))

    mask = jnp.tril(jnp.ones((CHUNK, CHUNK), dtype=bool))

    def step(carry, xs):
        C, n, m = carry
        qc, kc, vc, ic, lfc = xs
        b = jnp.cumsum(lfc, axis=-1)
        dmat = jnp.where(mask, b[..., :, None] - b[..., None, :] + ic[..., None, :], -jnp.inf)
        m_inter = b + m[..., None]
        m_row = jnp.maximum(m_inter, jnp.max(dmat, axis=-1))
        s = jnp.einsum('bhtd,bhsd->bhts', qc, kc) * jnp.exp(dmat - m_row[..., None])
        w_inter = jnp.exp(m_inter - m_row)
        num = (jnp.einsum('bhts,bhsv->bhtv', s, vc)
               + w_inter[..., None] * jnp.einsum('bhtd,bhdv->bhtv', qc, C))
        den = jnp.sum(s, axis=-1) + w_inter * jnp.einsum('bhtd,bhd->bht', qc, n)
        hc = num / jnp.maximum(jnp.abs(den), jnp.exp(-m_row))[..., None]
        b_end = b[..., -1]
        g = b_end[..., None] - b + ic
        m_new = jnp.maximum(b_end + m, jnp.max(g, axis=-1))
        wk = jnp.exp(g - m_new[..., None])
        decay = jnp.exp(b_end + m - m_new)
        C_new = decay[..., None, None] * C + jnp.einsum('bhs,bhsd,bhsv->bhdv', wk, kc, vc)
        n_new = decay[..., None] * n + jnp.einsum('bhs,bhsd->bhd', wk, kc)
        return (C_new, n_new, m_new), hc

    xs = (chunks(q), chunks(k), chunks(v), chunks(i_pre), chunks(jax.nn.log_sigmoid(f_pre)))
    (C, n, m), h = lax.scan(step, (C0, n0, m0), xs)
    h = jnp.transpose(h, (1, 0, 3, 2, 4)).reshape(bsz, L, H_C * DV_C)
    return h, C, n, m

def mixer_c(h, C0, n0, m0, w_in, b_if, w_out):
    f32 = jnp.float32
    bsz, L, _ = h.shape
    proj = h @ w_in
    q, k, v, o, z, gp = jnp.split(
        proj, [QK_C, 2 * QK_C, 2 * QK_C + W_C, 2 * QK_C + 2 * W_C, 2 * QK_C + 3 * W_C], axis=-1)
    q = q.astype(f32).reshape(bsz, L, H_C, DK_C) * (DK_C ** -0.5)
    k = k.astype(f32).reshape(bsz, L, H_C, DK_C)
    v = v.astype(f32).reshape(bsz, L, H_C, DV_C)
    gp = gp.astype(f32).reshape(bsz, L, 2, 2, H_C) + b_if.astype(f32)
    hsum = 0.0
    Cs, ns, ms = [], [], []
    for d in range(2):
        fl = (lambda t: jnp.flip(t, 1)) if d else (lambda t: t)
        hd, Cd, nd, md = mlstm_chunkwise(fl(q), fl(k), fl(v), fl(gp[:, :, d, 0]), fl(gp[:, :, d, 1]),
                                         C0[:, d].astype(f32), n0[:, d].astype(f32), m0[:, d].astype(f32))
        hsum = hsum + fl(hd)
        Cs.append(Cd)
        ns.append(nd)
        ms.append(md)
    y = jax.nn.sigmoid(o) * hsum.astype(h.dtype) * jax.nn.silu(z)
    return y @ w_out, jnp.stack(Cs, axis=1), jnp.stack(ns, axis=1), jnp.stack(ms, axis=1)

def run_trunk(x, cond, lru0, C0, n0, m0, w_mod, b_mod, g_pre, g_post, ab, cw):
    lru_f, C_f, n_f, m_f = [], [], [], []
    for l in range(DEPTH):
        shift, scale, gate = ada_mod(cond, w_mod[l], b_mod[l])
        h = rms_norm(x, g_pre[l]) * (1.0 + scale) + shift
        if l % 2 == 0:
            e = l // 2
            y, s = mixer_ab(h, lru0[:, e], *[p[e] for p in ab])
            lru_f.append(s)
        else:
            j = l // 2
            y, Cj, nj, mj = mixer_c(h, C0[:, j], n0[:, j], m0[:, j], *[p[j] for p in cw])
            C_f.append(Cj)
            n_f.append(nj)
            m_f.append(mj)
        x = x + gate * rms_norm(y, g_post[l])
    return x, jnp.stack(lru_f, 1), jnp.stack(C_f, 1), jnp.stack(n_f, 1), jnp.stack(m_f, 1)

def setup_inputs(seed: int = 0) -> dict:
    key = jax.random.key(seed)
    ks = jax.random.split(key, 32)
    f32 = jnp.float32

    def nrm(k, shape, s):
        return jax.random.normal(k, shape, f32) * s

    u = jax.random.uniform(ks[0], (N_EVEN, 2, W_A), f32, 0.9, 0.999)
    a = u ** (1.0 / LRU_C)
    lru_lambda = jnp.log(a) - jnp.log1p(-a)
    b_if = jnp.concatenate([nrm(ks[1], (N_ODD, 2, 1, H_C), 0.1),
                            3.0 + 3.0 * jax.random.uniform(ks[2], (N_ODD, 2, 1, H_C), f32)], axis=2)
    return {
        'x_prompt': nrm(ks[3], (BATCH, SEQ, D_MODEL), 1.0),
        'x_sample': nrm(ks[4], (DEC_BATCH, DEC_SEQ, D_MODEL), 1.0),
        'c': nrm(ks[5], (DEC_BATCH, D_MODEL), 1.0),
        'state_lru': nrm(ks[6], (DEC_BATCH, N_EVEN, 2, W_A), 0.5),
        'state_mlstm_C': nrm(ks[7], (DEC_BATCH, N_ODD, 2, H_C, DK_C, DV_C), 0.05),
        'state_mlstm_n': nrm(ks[8], (DEC_BATCH, N_ODD, 2, H_C, DK_C), 0.5),
        'state_mlstm_m': jax.random.uniform(ks[9], (DEC_BATCH, N_ODD, 2, H_C), f32, 0.0, 2.0),
        'c_ctx': nrm(ks[10], (D_MODEL,), 1.0),
        'w_mod': nrm(ks[11], (DEPTH, D_MODEL, 3 * D_MODEL), 0.5 * D_MODEL ** -0.5),
        'b_mod': nrm(ks[12], (DEPTH, 3 * D_MODEL), 0.02),
        'g_pre': 1.0 + nrm(ks[13], (DEPTH, D_MODEL), 0.02),
        'g_post': 1.0 + nrm(ks[14], (DEPTH, D_MODEL), 0.02),
        'w_in_e': nrm(ks[15], (N_EVEN, D_MODEL, IN_E), D_MODEL ** -0.5),
        'conv_w': nrm(ks[16], (N_EVEN, CONV_W, W_A), CONV_W ** -0.5),
        'conv_b': nrm(ks[17], (N_EVEN, W_A), 0.02),
        'w_rg': nrm(ks[18], (N_EVEN, 2, H_A, BW_A, BW_A), BW_A ** -0.5),
        'b_rg': nrm(ks[19], (N_EVEN, 2, W_A), 0.02),
        'w_ig': nrm(ks[20], (N_EVEN, 2, H_A, BW_A, BW_A), BW_A ** -0.5),
        'b_ig': nrm(ks[21], (N_EVEN, 2, W_A), 0.02),
        'lru_lambda': lru_lambda,
        'w_four': nrm(ks[22], (N_EVEN, G_B, GW_B, GW_B), GW_B ** -0.5),
        'b_four': nrm(ks[23], (N_EVEN, W_B), 0.02),
        'w_out_e': nrm(ks[24], (N_EVEN, OUT_E, D_MODEL), OUT_E ** -0.5),
        'w_in_o': nrm(ks[25], (N_ODD, D_MODEL, IN_O), D_MODEL ** -0.5),
        'b_if': b_if,
        'w_out_o': nrm(ks[26], (N_ODD, W_C, D_MODEL), W_C ** -0.5),
    }

def reference(x_prompt, x_sample, c, state_lru, state_mlstm_C, state_mlstm_n, state_mlstm_m,
              c_ctx, w_mod, b_mod, g_pre, g_post, w_in_e, conv_w, conv_b, w_rg, b_rg, w_ig, b_ig,
              lru_lambda, w_four, b_four, w_out_e, w_in_o, b_if, w_out_o):
    f32 = jnp.float32
    ab = (w_in_e, conv_w, conv_b, w_rg, b_rg, w_ig, b_ig, lru_lambda, w_four, b_four, w_out_e)
    cw = (w_in_o, b_if, w_out_o)
    bp = x_prompt.shape[0]
    cond_ctx = jnp.broadcast_to(c_ctx[None, :], (bp, c_ctx.shape[0]))
    y_prompt, new_lru, new_C, new_n, new_m = run_trunk(
        x_prompt, cond_ctx,
        jnp.zeros((bp, N_EVEN, 2, W_A), f32),
        jnp.zeros((bp, N_ODD, 2, H_C, DK_C, DV_C), f32),
        jnp.zeros((bp, N_ODD, 2, H_C, DK_C), f32),
        jnp.zeros((bp, N_ODD, 2, H_C), f32),
        w_mod, b_mod, g_pre, g_post, ab, cw)
    y_sample, _, _, _, _ = run_trunk(
        x_sample, c, state_lru, state_mlstm_C, state_mlstm_n, state_mlstm_m,
        w_mod, b_mod, g_pre, g_post, ab, cw)
    return (y_prompt, y_sample, new_lru, new_C, new_n, new_m)


_drawn_inputs = setup_inputs


def setup_inputs(seed=0):
    import zlib

    import numpy as np

    out = dict(_drawn_inputs(seed))
    spreads = {}
    factors = {'state_mlstm_C': 8.0,
     'state_mlstm_n': 2.807,
     'state_mlstm_m': 4.761,
     'b_rg': 8.0,
     'b_ig': 6.779,
     'b_four': 6.792}
    for name, (base, spread) in spreads.items():
        noise = np.random.default_rng([zlib.crc32(name.encode()), seed]).standard_normal(out[name].shape)
        drawn = base * np.exp(spread * noise) if base else spread * noise
        out[name] = __import__('jax').numpy.asarray(drawn.astype(out[name].dtype))
    for name, factor in factors.items():
        out[name] = (out[name] * factor).astype(out[name].dtype)
    return out
```

```python
import numpy as np

import concourse.bass as bass
from concourse import mybir

F32, F32R = mybir.dt.float32, mybir.dt.float32r
ALU = mybir.AluOpType
ACT = mybir.ActivationFunctionType
ds = bass.ds

P = 128
D = 1024
KC = D // P
NCTX, NLAT = 128, 1024
T = NCTX + NLAT
NT = T // P
NJ, JW = 3, T // 3
H = 8
EPS = 1e-6
GAP = 3
TP = T + GAP
JP = TP // 3
LAT = NCTX + GAP
FFT_A = NLAT // P
TAP, CB, HBR, HBI, NEG, POS, H0 = 0, 4, 5, 6, 7, 8, 9
NPRM = 15


class Chain:

    def __init__(self, eng, sem, base=0):
        self.eng, self.sem, self.base, self.n = eng, sem, base, 0

    def link(self, ins):
        ins.then_inc(self.sem, 1)
        self.n += 1
        self.eng.wait_ge(self.sem, self.base + self.n)


def build(nc, a, out):
    sem = nc.alloc_semaphore
    bottom = [(nc.sbuf_base + 31) // 32 * 32]

    def sb(name, shape, dt=F32, at=None):
        at = bottom if at is None else at
        t = nc.alloc_sbuf_tensor_at(name, list(shape), dt, offset=at[0])
        at[0] += (int(np.prod(shape[1:])) * 4 + 31) // 32 * 32
        assert at[0] <= nc.sbuf_usable_end, (name, at[0])
        return t

    HHI = sb("h_hi", [P, KC, T], F32R)
    HLO = sb("h_lo", [P, KC, T], F32R)
    WRAW = sb("w_raw", [P, 2, KC * P])
    WHI = sb("w_hi", [P, 2, KC * P], F32R)
    WLO = sb("w_lo", [P, 2, KC * P], F32R)
    IDENT = sb("ident", [P, P])
    ONES = sb("ones", [P, P])
    AM = sb("mod_scale", [P, 2, KC, 2])
    SH = sb("mod_shift", [P, 2, KC, 2])
    GP = sb("mod_gate", [P, 2, KC, 2])
    zone = bottom[0]
    PS = nc.alloc_psum_tensor("psum_groups", [P, 2, 3, 512], F32)
    PX = nc.alloc_psum_tensor("psum_extra", [P, 2, 512], F32)
    y_dram = nc.dram_tensor("y_scratch", (16, P, T), F32).ap()
    x_dram = nc.dram_tensor("x_scratch", (KC, P, T), F32).ap()

    SEGS = ((0, NCTX, 1), (NCTX, T, 0))

    w_loaded = [sem("w_loaded_0"), sem("w_loaded_1")]
    w_hi, w_lo, w_used = sem("w_hi_ready"), sem("w_lo_ready"), sem("w_used")

    def w_load(sp, pair, slot, src):
        if not isinstance(pair, int) or pair >= 1:
            sp.wait_ge(w_lo, pair * 2 + slot - 1)
        sp.dma_start(WRAW[:, slot, :].rearrange("p (k n) -> p k n", k=src.shape[1]), src).then_inc(w_loaded[slot], 16)

    def w_split_hi(act, pair, slot):
        act.wait_ge(w_loaded[slot], (pair + 1) * 16)
        if not isinstance(pair, int) or pair >= 1:
            act.wait_ge(w_used, pair * 2 + slot - 1)
        act.activation(WHI[:, slot, :], WRAW[:, slot, :], ACT.Copy).then_inc(w_hi, 1)

    def w_split_lo(dve, pair, slot):
        dve.wait_ge(w_hi, pair * 2 + slot + 1)
        dve.tensor_tensor(WLO[:, slot, :], WRAW[:, slot, :], WHI[:, slot, :].bitcast(F32), ALU.subtract).then_inc(w_lo, 1)

    def in_tile(w, col):
        return w.rearrange("(k p) n -> p k n", p=P)[:, :, ds(col, P)]

    def project(pe, pair, slot, group, hi, lo, k0=0, start=True, stop=True, ready=None):
        pe.wait_ge(w_lo, pair * 2 + slot + 1)
        for k in range(KC):
            if ready:
                ready(k0 + k)
            for m, (w, h) in enumerate(((WHI, hi), (WHI, lo), (WLO, hi))):
                for j in range(NJ):
                    ins = pe.matmul(PS[:, group, j, 0:JW], w[:, slot, k * P:(k + 1) * P],
                                    h(k0 + k)[:, j * JW:(j + 1) * JW],
                                    start=start and k == 0 and m == 0, stop=stop and k == KC - 1 and m == 2)
        ins.then_inc(w_used, 1)

    def projected(eng, pair, slot):
        eng.wait_ge(w_used, pair * 2 + slot + 1)

    def out_tile(w, half, col):
        return w.rearrange("(h k p) n -> h p k n", h=2, p=P)[half][:, :, ds(col, P)]

    hhi, hlo = (lambda k: HHI[:, k, :]), (lambda k: HLO[:, k, :])

    def by_bank(ap, w=JW):
        return ap.rearrange("p (j n) -> p j n", n=w)

    norm_zone = [zone]
    XT = sb("xT", [P, KC, T], at=norm_zone)
    TMP = sb("norm_tmp", [P, 2, T], at=norm_zone)
    SQ = sb("squares", [P, 2, T], at=norm_zone)
    RSTD = sb("rstd_rows", [96, JW], at=norm_zone)
    sq_ready, sq_used = sem("squares_ready"), sem("squares_summed")
    var_ready, std_ready = sem("variance_ready"), sem("std_ready")
    rstd_ready, rstd_spread = sem("rstd_ready"), sem("rstd_spread")

    def stats_act(act, n, x_of, SQ, x_ready=None):
        for k in range(KC):
            if x_ready:
                act.wait_ge(x_ready, k + 1)
            if k >= 2 or n:
                act.wait_ge(sq_used, KC * n + k - 1)
            act.activation(SQ[:, k % 2, :], x_of(k), ACT.Square).then_inc(sq_ready, 1)
        act.wait_ge(var_ready, n + 1)
        act.activation(RSTD[:], RSTD[:], ACT.Sqrt).then_inc(std_ready, 1)

    def stats_pe(pe, n, SQ):
        for k in range(KC):
            pe.wait_ge(sq_ready, KC * n + k + 1)
            for j in range(NJ):
                ins = pe.matmul(PX[32 * j:32 * j + 32, 1, 0:JW], ONES[:, 0:32], SQ[:, k % 2, j * JW:(j + 1) * JW],
                                start=k == 0, stop=k == KC - 1)
            ins.then_inc(sq_used, 1)
        pe.wait_ge(rstd_ready, n + 1)
        for j in range(NJ):
            ins = pe.matmul(PS[:, 0, j, 0:JW], ONES[32 * j:32 * j + 1, :], RSTD[32 * j:32 * j + 1, :],
                            start=True, stop=True)
        ins.then_inc(rstd_spread, 1)

    def stats_dve(dve, n):
        dve.wait_ge(sq_used, KC * (n + 1))
        dve.tensor_scalar(RSTD[:], PX[0:96, 1, 0:JW], 1.0 / D, EPS, ALU.mult, ALU.add).then_inc(var_ready, 1)
        dve.wait_ge(std_ready, n + 1)
        dve.reciprocal(RSTD[:], RSTD[:]).then_inc(rstd_ready, 1)

    normed, modulated, h_hi, h_lo = sem("x_normed"), sem("h_modulated"), sem("h_hi_ready"), sem("h_lo_ready")

    def h_dve(dve, l, x_of, TMP):
        dve.wait_ge(rstd_spread, 2 * l + 1)
        for k in range(KC + 1):
            if k < KC:
                if k >= 2:
                    dve.wait_ge(h_lo, KC * l + k - 1)
                dve.tensor_tensor(by_bank(TMP[:, k % 2, :]), by_bank(x_of(k)), PS[:, 0, :, 0:JW],
                                  ALU.mult).then_inc(normed, 1)
            if k:
                dve.wait_ge(h_hi, KC * l + k)
                dve.tensor_tensor(HLO[:, k - 1, :], TMP[:, (k - 1) % 2, :], HHI[:, k - 1, :].bitcast(F32),
                                  ALU.subtract).then_inc(h_lo, 1)

    def h_act(act, l, TMP):
        for k in range(KC):
            act.wait_ge(normed, KC * l + k + 1)
            for t0, t1, c in SEGS:
                act.activation(TMP[:, k % 2, t0:t1], TMP[:, k % 2, t0:t1], ACT.Identity,
                               scale=AM[:, l, k, c:c + 1], bias=SH[:, l, k, c:c + 1]).then_inc(modulated, 1)
            act.wait_ge(modulated, 2 * (KC * l + k + 1))
            act.activation(HHI[:, k, :], TMP[:, k % 2, :], ACT.Copy).then_inc(h_hi, 1)

    def setup():
        z = list(norm_zone)
        XR = sb("x_rows", [P, 2, D], at=z)
        WM = sb("w_mod_rows", [P, 2, 3 * D], at=z)
        CD = sb("cond", [P, 2, KC], at=z)
        SC = sb("cond_silu", [P, 2, KC], at=z)
        BM = sb("b_mod", [P, 2, 24], at=z)
        GN = sb("norm_gains", [P, 2, 2, KC], at=z)
        MD = sb("mod", [P, 24, 2], at=z)
        ZERO = sb("zeros", [P, 48], at=z)
        const_in, cond_in, gains_in = sem("const_loaded"), sem("cond_loaded"), sem("gains_loaded")
        x_in = [sem("x_loaded_0"), sem("x_loaded_1")]
        wm_in = [sem("w_mod_loaded_0"), sem("w_mod_loaded_1")]
        x_turned, xT_dve, xT_act, x_spilled = (sem(s) for s in ("x_turned", "xT_by_dve", "xT_by_act", "x_spilled"))
        cond_tanh, cond_ready, zero_ready = sem("cond_tanh"), sem("cond_ready"), sem("zeros_ready")
        mod_done, mod_ready, wm_used = sem("mod_summed"), sem("mod_ready"), sem("w_mod_used")
        act_chain, dve_chain = sem("setup_act_chain"), sem("setup_dve_chain")
        wm_src = a["w_mod"].rearrange("l (k p) n -> (l k) p n", p=P)
        block = nc.Block()
        block.__enter__()

        @block.sync
        def _(sp):
            sp.dma_start(IDENT[:], a["ident"]).then_inc(const_in, 16)
            sp.dma_start(ONES[:], a["ones"]).then_inc(const_in, 16)

            def x_rows(t):
                if t >= 2:
                    sp.wait_ge(x_turned, t - 1)
                src = a["x_prompt"][0] if t == 0 else a["x_sample"][0, (t - 1) * P:t * P, :]
                sp.dma_start(XR[:, t % 2, :], src).then_inc(x_in[t % 2], 16)

            def w_mod_rows(n):
                if n >= 2:
                    sp.wait_ge(wm_used, n - 1)
                sp.dma_start(WM[:, n % 2, :], wm_src[n]).then_inc(wm_in[n % 2], 16)

            x_rows(0)
            x_rows(1)
            with nc.allow_non_contiguous_dma("vectors, one element per partition"):
                sp.dma_start(CD[:, 0, :], a["c"].rearrange("b (k p) -> p (b k)", p=P)).then_inc(cond_in, 16)
                sp.dma_start(CD[:, 1, :], a["c_ctx"].rearrange("(k p) -> p k", p=P)).then_inc(cond_in, 16)
                for l in range(2):
                    sp.dma_start(BM[:, l, :], a["b_mod"][l].rearrange("(j p) -> p j", p=P)).then_inc(gains_in, 16)
                    sp.dma_start(GN[:, 0, l, :], a["g_pre"][l].rearrange("(k p) -> p k", p=P)).then_inc(gains_in, 16)
                    sp.dma_start(GN[:, 1, l, :], a["g_post"][l].rearrange("(k p) -> p k", p=P)).then_inc(gains_in, 16)
            for t in range(2, NT):
                x_rows(t)
            for n in range(KC):
                w_mod_rows(n)
            for n in range(2):
                w_load(sp, 0, n, in_tile(a["w_in_e"][0], n * D))
            for n in range(KC, 2 * KC):
                w_mod_rows(n)
            sp.wait_ge(xT_dve, 5)
            sp.wait_ge(xT_act, 4)
            sp.dma_start(x_dram.rearrange("k p t -> p k t"), XT[:]).then_inc(x_spilled, 16)
            sp.wait_ge(x_spilled, 16)

        @block.tensor
        def _(pe):
            pe.wait_ge(const_in, 32)
            for t in range(NT):
                pe.wait_ge(x_in[t % 2], 16 * (t // 2 + 1))
                if t >= 2:
                    pe.wait_ge(xT_act if t % 2 else xT_dve, t // 2)
                for k in range(KC):
                    ins = pe.transpose(PS[:, t % 2, k // 4, (k % 4) * P:(k % 4 + 1) * P],
                                       XR[:, t % 2, k * P:(k + 1) * P], IDENT[:])
                ins.then_inc(x_turned, 1)

            def modulation(l):
                if l == 0:
                    pe.wait_ge(zero_ready, 1)
                    pe.wait_ge(cond_ready, 1)
                else:
                    pe.wait_ge(mod_ready, 1)
                pe.matmul(PX[:, 0, 0:48], ONES[:], ZERO[:], start=True, stop=False, skip_group_check=True)
                for k in range(KC):
                    pe.wait_ge(wm_in[k % 2], 16 * ((KC * l + k) // 2 + 1))
                    for j in range(24):
                        ins = pe.matmul(PX[:, 0, 2 * j:2 * j + 2], WM[:, k % 2, j * P:(j + 1) * P], SC[:, :, k],
                                        start=False, stop=k == KC - 1, skip_group_check=True)
                    ins.then_inc(wm_used, 1)
                    if k == KC - 1:
                        pe.wait_ge(wm_used, KC * (l + 1))
                        pe.sem_inc(mod_done, 1)

            stats_pe(pe, 0, SQ)
            modulation(0)
            modulation(1)

        @block.scalar
        def _(act):
            act.wait_ge(cond_in, 32)
            act.activation(SC[:], CD[:], ACT.Tanh, scale=0.5).then_inc(cond_tanh, 1)
            for t in range(1, NT, 2):
                act.wait_ge(x_turned, t + 1)
                act.activation(XT[:, :, t * P:(t + 1) * P],
                               PS[:, 1, 0:2, :].rearrange("p b (k n) -> p (b k) n", n=P), ACT.Copy).then_inc(xT_act, 1)
            act.wait_ge(xT_act, 4)
            act.wait_ge(xT_dve, 5)
            stats_act(act, 0, lambda k: XT[:, k, :], SQ)
            w_split_hi(act, 0, 0)
            act.wait_ge(mod_ready, 1)
            h_act(act, 0, TMP)

        @block.vector
        def _(dve):
            ch = Chain(dve, dve_chain)
            dve.memset(ZERO[:], 0.0).then_inc(zero_ready, 1)
            dve.wait_ge(cond_tanh, 1)
            ch.link(dve.scalar_tensor_tensor(SC[:], SC[:], 1.0, CD[:], ALU.add, ALU.mult))
            dve.tensor_scalar(SC[:], SC[:], 0.5, None, ALU.mult).then_inc(cond_ready, 1)
            for t in range(0, NT, 2):
                dve.wait_ge(x_turned, t + 1)
                dve.tensor_copy(XT[:, :, t * P:(t + 1) * P],
                                PS[:, 0, 0:2, :].rearrange("p b (k n) -> p (b k) n", n=P)).then_inc(xT_dve, 1)
            stats_dve(dve, 0)

            def modulation(l):
                dve.wait_ge(mod_done, l + 1)
                dve.wait_ge(gains_in, 16 * 6)
                ch.link(dve.tensor_tensor(MD[:], PX[:, 0, 0:48].rearrange("p (j c) -> p j c", c=2),
                                          BM[:, l, :].unsqueeze(2).to_broadcast([P, 24, 2]), ALU.add))
                dve.tensor_copy(SH[:, l], MD[:, 0:8, :])
                ch.link(dve.tensor_scalar(AM[:, l], MD[:, 8:16, :], 1.0, None, ALU.add))
                ch.link(dve.tensor_tensor(AM[:, l], AM[:, l], GN[:, 0, l, :].unsqueeze(2).to_broadcast([P, 8, 2]),
                                          ALU.mult))
                dve.tensor_tensor(GP[:, l], MD[:, 16:24, :], GN[:, 1, l, :].unsqueeze(2).to_broadcast([P, 8, 2]),
                                  ALU.mult).then_inc(mod_ready, 1)

            modulation(0)
            w_split_lo(dve, 0, 0)
            dve.wait_ge(xT_act, 4)
            h_dve(dve, 0, lambda k: XT[:, k, :], TMP)
            modulation(1)

        block.__exit__(None, None, None)


    def log1p(dve, ch, E, S, S2):
        ch.link(dve.tensor_scalar(S, E, 2.0, None, ALU.add))
        ch.link(dve.reciprocal(S, S))
        ch.link(dve.tensor_tensor(S, S, E, ALU.mult))
        ch.link(dve.tensor_tensor(S2, S, S, ALU.mult))
        ch.link(dve.tensor_scalar(E, S2, 1.0 / 17, None, ALU.mult))
        for m in range(7, 0, -1):
            ch.link(dve.scalar_tensor_tensor(E, E, 1.0 / (2 * m + 1), S2, ALU.add, ALU.mult))
        ch.link(dve.scalar_tensor_tensor(E, E, 1.0, S, ALU.add, ALU.mult))
        ch.link(dve.tensor_scalar(S, E, 2.0, None, ALU.mult))

    def lru():
        z = [zone]
        PRM = sb("lru_params", [P, KC, NPRM], at=z)
        LAM = sb("lru_lambda", [P, 2, KC], at=z)
        LT = sb("lru_softplus", [P, 3, 2 * KC], at=z)
        GW = sb("gate_weights", [P, 4, P], at=z)
        XA = sb("xa_padded", [P, TP + 3], at=z)
        XC = sb("xa_convolved", [P, TP], at=z)
        GZ = sb("za_silu", [P, T], at=z)
        ZH = sb("za_half", [P, T], at=z)
        T1 = sb("gate_r", [P, 2, TP], at=z)
        T2 = sb("gate_i", [P, 2, TP], at=z)
        A = sb("decay", [P, 2, TP], at=z)
        HT = sb("tanh_then_state", [P, 2, TP], at=z)
        YT = sb("lru_y", [P, T], at=z)
        FIN = sb("lru_final", [P, 2, KC], at=z)
        prm_in, gw_in = sem("lru_params_loaded"), sem("gate_weights_loaded")
        mm = sem("lru_products")
        r_out, i_out, z_out, x_out = sem("r_evacuated"), sem("i_evacuated"), sem("za_evacuated"), sem("xa_evacuated")
        pads, conv, gated, squared, var1, root, y_ready, y_out = (sem(s) for s in (
            "pads_zero", "xa_conv_ready", "za_tanh_ready", "decay_ready", "one_minus_a2_ready", "root_ready",
            "lru_y_ready", "lru_y_stored"))
        lam_exp, prm_ready, fin_out = sem("lambda_exp"), sem("lru_params_ready"), sem("lru_final_stored")
        r_tanh = sem("gate_r_read")
        dve_chain = sem("lru_dve_chain")
        s_in = [sem("lru_lam_abs")]
        block = nc.Block()
        block.__enter__()

        def gate_weights(sp, i):
            sp.dma_start(GW[:, 0:2, :], a["w_rg"][0][:, ds(i, 1)].rearrange("d a p n -> p (d a) n")).then_inc(gw_in, 16)
            sp.dma_start(GW[:, 2:4, :], a["w_ig"][0][:, ds(i, 1)].rearrange("d a p n -> p (d a) n")).then_inc(gw_in, 16)

        @block.sync
        def _(sp):
            with nc.allow_non_contiguous_dma("vectors, one element per partition"):
                by_channel = "(k p) -> p k"
                for j in range(4):
                    sp.dma_start(PRM[:, :, TAP + j], a["conv_w"][0, j].rearrange(by_channel, p=P)).then_inc(prm_in, 16)
                sp.dma_start(PRM[:, :, CB], a["conv_b"][0].rearrange(by_channel, p=P)).then_inc(prm_in, 16)
                for d in range(2):
                    for col, src in ((HBR, a["b_rg"][0, d]), (HBI, a["b_ig"][0, d]), (H0, a["state_lru"][0, 0, d])):
                        sp.dma_start(PRM[:, :, 5 * d + col], src.rearrange(by_channel, p=P)).then_inc(prm_in, 16)
                    sp.dma_start(LAM[:, d, :], a["lru_lambda"][0, d].rearrange(by_channel, p=P)).then_inc(prm_in, 16)
            gate_weights(sp, 0)
            with sp.Fori(0, KC - 1) as i:
                w_load(sp, i + 1, 0, in_tile(a["w_in_e"][0], i * P + P))
                w_load(sp, i + 1, 1, in_tile(a["w_in_e"][0], i * P + P + D))
                sp.wait_ge(mm, i * 4 + 4)
                gate_weights(sp, i + 1)
                sp.wait_ge(y_ready, i + 1)
                sp.dma_start(y_dram[ds(i, 1)].rearrange("a p t -> p (a t)"), YT[:]).then_inc(y_out, 16)
            for slot in range(2):
                w_load(sp, KC, slot, in_tile(a["w_in_e"][0], (2 + slot) * D))
            sp.wait_ge(y_ready, KC)
            sp.dma_start(y_dram[KC - 1], YT[:]).then_inc(y_out, 16)
            with nc.allow_non_contiguous_dma("final states, one element per partition"):
                for d in range(2):
                    sp.dma_start(out["new_lru"][0, 0, d].rearrange("(k p) -> p k", p=P), FIN[:, d, :]).then_inc(fin_out, 16)
            sp.wait_ge(y_out, 16 * KC)
            sp.wait_ge(fin_out, 32)

        @block.tensor
        def _(pe):
            def block_of(i, first):
                if not first:
                    pe.wait_ge(r_out, i * 2)
                project(pe, i, 0, 0, hhi, hlo)
                if not first:
                    pe.wait_ge(i_out, i * 2)
                project(pe, i, 1, 1, hhi, hlo)
                pe.wait_ge(gw_in, i * 32 + 32)
                pe.wait_ge(conv, i + 1)
                for d in range(2):
                    for what in range(2):
                        if what == 0:
                            pe.wait_ge(*((r_out, i * 2 + 1) if d else (x_out, i + 1)))
                        else:
                            pe.wait_ge(*((i_out, i * 2 + 1) if d else (z_out, i + 1)))
                        for j in range(NJ):
                            ins = pe.matmul(PS[:, what, j, 0:JP], GW[:, 2 * what + d, :], XC[:, j * JP:(j + 1) * JP],
                                            start=True, stop=True)
                        ins.then_inc(mm, 1)

            block_of(0, True)
            with pe.Fori(1, KC) as i:
                block_of(i, False)

        def prm(i, col):
            return PRM[:, ds(i, 1), col]

        @block.scalar
        def _(act):
            act.wait_ge(prm_in, 16 * 13)
            act.activation(LT[:, 0, :], LAM[:].rearrange("p d k -> p (d k)"), ACT.Abs).then_inc(s_in[0], 1)
            act.wait_ge(s_in[0], 1)
            act.activation(LT[:, 0, :], LT[:, 0, :], ACT.Exp, scale=-1.0).then_inc(lam_exp, 1)
            act.wait_ge(pads, 1)
            act.wait_ge(prm_ready, 1)
            def block_of(i, first):
                w_split_hi(act, i, 1)
                projected(act, i, 0)
                if not first:
                    act.wait_ge(conv, i)
                act.activation(XA[:, 2:2 + NCTX], PS[:, 0, 0, 0:NCTX], ACT.Copy)
                act.activation(XA[:, 2 + LAT:2 + JW + GAP], PS[:, 0, 0, NCTX:JW], ACT.Copy)
                act.activation(by_bank(XA[:, 2 + JW + GAP:2 + TP]), PS[:, 0, 1:3, 0:JW], ACT.Copy).then_inc(x_out, 1)
                w_split_hi(act, i + 1, 0)
                projected(act, i, 1)
                if not first:
                    act.wait_ge(y_ready, i)
                act.activation(by_bank(GZ[:]), PS[:, 1, :, 0:JW], ACT.Tanh, scale=0.5)
                act.activation(by_bank(ZH[:]), PS[:, 1, :, 0:JW], ACT.Copy, scale=0.5).then_inc(z_out, 1)
                for d in range(2):
                    act.wait_ge(mm, i * 4 + 1 + 2 * d)
                    act.activation(by_bank(T1[:, d, :], JP), PS[:, 0, :, 0:JP], ACT.Tanh, scale=0.5,
                                   bias=prm(i, HBR + 5 * d)).then_inc(r_out, 1)
                    act.wait_ge(mm, i * 4 + 2 + 2 * d)
                    act.activation(by_bank(T2[:, d, :], JP), PS[:, 1, :, 0:JP], ACT.Tanh, scale=0.5,
                                   bias=prm(i, HBI + 5 * d)).then_inc(i_out, 1)
                    act.wait_ge(r_out, i * 2 + 1 + d)
                    act.activation(A[:, d, :], T1[:, d, :], ACT.Exp, scale=prm(i, NEG + 5 * d),
                                   bias=prm(i, NEG + 5 * d)).then_inc(r_tanh, 1)
                    act.activation(HT[:, d, :], T1[:, d, :], ACT.Tanh, scale=prm(i, POS + 5 * d),
                                   bias=prm(i, POS + 5 * d)).then_inc(r_tanh, 1)
                    act.wait_ge(r_tanh, i * 4 + 2 + 2 * d)
                    act.activation(T1[:, d, :], A[:, d, :], ACT.Square).then_inc(squared, 1)
                for d in range(2):
                    act.wait_ge(var1, i * 2 + 1 + d)
                    act.activation(T1[:, d, :], T1[:, d, :], ACT.Sqrt, scale=0.25).then_inc(root, 1)

            block_of(0, True)
            with act.Fori(1, KC) as i:
                block_of(i, False)

        @block.vector
        def _(dve):
            ch = Chain(dve, dve_chain)
            dve.memset(XA[:], 0.0).then_inc(pads, 1)
            dve.wait_ge(prm_in, 16 * 13)
            dve.wait_ge(lam_exp, 1)
            log1p(dve, ch, LT[:, 0, :], LT[:, 1, :], LT[:, 2, :])
            lam = LAM[:].rearrange("p d k -> p (d k)")
            ch.link(dve.tensor_scalar(LT[:, 0, :], lam, -1.0, 0.0, ALU.mult, ALU.max))
            ch.link(dve.tensor_tensor(LT[:, 1, :], LT[:, 0, :], LT[:, 1, :], ALU.add))
            for d in range(2):
                sp_d = LT[:, 1, KC * d:KC * d + KC]
                dve.tensor_scalar(PRM[:, :, NEG + 5 * d], sp_d, -4.0, None, ALU.mult)
                dve.tensor_scalar(PRM[:, :, POS + 5 * d], sp_d, 4.0, None, ALU.mult)
                for col in (HBR, HBI):
                    ins = dve.tensor_scalar(PRM[:, :, col + 5 * d], PRM[:, :, col + 5 * d], 0.5, None, ALU.mult)
            ins.then_inc(prm_ready, 1)
            dve.wait_ge(prm_ready, 1)
            before, LINKS = ch.n, 12

            def block_of(i, first):
                w_split_lo(dve, i, 1)
                dve.wait_ge(x_out, i + 1)
                if not first:
                    dve.wait_ge(mm, i * 4)
                ch.link(dve.tensor_scalar(XC[:], XA[:, 0:TP], prm(i, TAP), prm(i, CB), ALU.mult, ALU.add))
                for j in range(1, 4):
                    ins = dve.scalar_tensor_tensor(XC[:], XA[:, j:j + TP], prm(i, TAP + j), XC[:], ALU.mult, ALU.add)
                    if j < 3:
                        ch.link(ins)
                ins.then_inc(conv, 1)
                w_split_lo(dve, i + 1, 0)
                dve.wait_ge(z_out, i + 1)
                ch.link(dve.scalar_tensor_tensor(GZ[:], GZ[:], 1.0, ZH[:], ALU.add, ALU.mult))
                dve.wait_ge(conv, i + 1)
                for d in range(2):
                    dve.wait_ge(i_out, i * 2 + 1 + d)
                    dve.scalar_tensor_tensor(T2[:, d, :], T2[:, d, :], 1.0, XC[:], ALU.add, ALU.mult)
                    dve.wait_ge(squared, i * 2 + 1 + d)
                    dve.scalar_tensor_tensor(T1[:, d, :], T1[:, d, :], 1.0, HT[:, d, :], ALU.add,
                                             ALU.mult).then_inc(var1, 1)
                for d in range(2):
                    dve.wait_ge(root, i * 2 + 1 + d)
                    ch.link(dve.tensor_tensor(T2[:, d, :], T2[:, d, :], T1[:, d, :], ALU.mult))
                    for t0, t1, h0 in ((0, NCTX, 0.0), (LAT, TP, prm(i, H0 + 5 * d))):
                        w = slice(t0, t1) if d == 0 else slice(t1 - 1, None if t0 == 0 else t0 - 1, -1)
                        ins = dve.tensor_tensor_scan(HT[:, d, w], A[:, d, w], T2[:, d, w], h0, op0=ALU.mult, op1=ALU.add)
                    ch.link(ins)
                    dve.tensor_copy(FIN[:, d, ds(i, 1)], HT[:, d, NCTX - 1:NCTX] if d == 0 else HT[:, d, 0:1])
                for n, (t0, t1, p0) in enumerate(((0, NCTX, 0), (NCTX, T, LAT))):
                    ch.link(dve.tensor_tensor(HT[:, 0, p0:p0 + t1 - t0], HT[:, 0, p0:p0 + t1 - t0],
                                              HT[:, 1, p0:p0 + t1 - t0], ALU.add))
                if not first:
                    dve.wait_ge(y_out, i * 16)
                ch.link(dve.tensor_tensor(YT[:, 0:NCTX], HT[:, 0, 0:NCTX], GZ[:, 0:NCTX], ALU.mult))
                ch.link(dve.tensor_tensor(YT[:, NCTX:T], HT[:, 0, LAT:TP], GZ[:, NCTX:T], ALU.mult))
                dve.sem_inc(y_ready, 1)

            block_of(0, True)
            assert ch.n == before + LINKS, ch.n - before
            with dve.Fori(1, KC) as i:
                ch.base, ch.n = before + i * LINKS, 0
                block_of(i, False)

        block.__exit__(None, None, None)

    def fourier():
        z = [zone]
        CH = sb("channel_dft", [P, 2, P], at=z)
        TB = sb("token_dft", [P, 8, 2, P], at=z)
        WF = sb("w_four", [P, 2, P], at=z)
        CW = sb("channel_weights", [P, 2, P], at=z)
        B4 = sb("b_four", [P, KC], at=z)
        XB = sb("xb", [P, T], at=z)
        GZ = sb("zb_silu", [P, T], at=z)
        ZH = sb("zb_half", [P, T], at=z)
        Z = sb("token_major", [P, NT, 2, P], at=z)
        S = sb("butterfly", [P, 2, 4, 2, P], at=z)
        M = sb("butterfly_mid", [P, 4, 2, P], at=z)
        TF = sb("transformed", [P, 8, 2, P], at=z)
        YT = sb("fourier_y", [P, T], at=z)
        table_in = sem("tables_loaded")
        wf_in = [sem("w_four_loaded_0"), sem("w_four_loaded_1")]
        cw_done, cw_out = sem("cw_product"), sem("cw_ready")
        f_done, ua_done, ub_done = sem("dft_product"), sem("ua_product"), sem("ub_product")
        xb_out, ua_out, ub_out, zb_out, y_ready, y_out = (sem(s) for s in (
            "xb_ready", "ua_ready", "ub_ready", "zb_ready", "fourier_y_ready", "fourier_y_stored"))
        tf_ready = sem("token_transform_ready")
        dve_chain = sem("fourier_dve_chain")
        half = 1.0 / np.sqrt(2.0)
        block = nc.Block()
        block.__enter__()

        @block.sync
        def _(sp):
            sp.dma_start(CH[:], a["channel_dft"]).then_inc(table_in, 16)
            sp.dma_start(TB[:], a["token_dft"]).then_inc(table_in, 16)
            with nc.allow_non_contiguous_dma("a vector, one element per partition"):
                sp.dma_start(B4[:], a["b_four"][0].rearrange("(k p) -> p k", p=P)).then_inc(table_in, 16)
            with sp.Fori(0, KC - 1) as i:
                w_load(sp, i + KC + 1, 0, in_tile(a["w_in_e"][0], i * P + P + 2 * D))
                w_load(sp, i + KC + 1, 1, in_tile(a["w_in_e"][0], i * P + P + 3 * D))
                sp.wait_ge(y_ready, i + 1)
                sp.dma_start(y_dram[ds(i + KC, 1)].rearrange("a p t -> p (a t)"), YT[:]).then_inc(y_out, 16)
            for slot in range(2):
                w_load(sp, 2 * KC, slot, out_tile(a["w_out_e"][0], slot, 0))
            sp.wait_ge(y_ready, KC)
            sp.dma_start(y_dram[2 * KC - 1], YT[:]).then_inc(y_out, 16)
            sp.wait_ge(y_out, 16 * KC)

        @block.gpsimd
        def _(pool):
            for slot in range(2):
                pool.dma_start(WF[:, slot, :], a["w_four"][0, slot]).then_inc(wf_in[slot], 16)
            with pool.Fori(0, KC // 2 - 1) as m:
                for slot in range(2):
                    pool.wait_ge(cw_done, m * 2 + 1 + slot)
                    pool.dma_start(WF[:, slot, :], a["w_four"][0][ds(m * 2 + 2 + slot, 1)].rearrange("a p n -> p (a n)")
                                   ).then_inc(wf_in[slot], 16)

        @block.tensor
        def _(pe):
            pe.wait_ge(table_in, 48)

            def channel_weights(m, slot):
                pe.wait_ge(wf_in[slot], m * 16 + 16)
                pe.wait_ge(cw_out, m * 2 + slot)
                pe.wait_ge(ub_out, m * 2 + slot)
                for part in range(2):
                    ins = pe.matmul(PX[:, 1, 256 + part * P:256 + (part + 1) * P], CH[:, part, :], WF[:, slot, :],
                                    start=True, stop=True, skip_group_check=True)
                ins.then_inc(cw_done, 1)

            def to_tokens(first, last, bank, done):
                for t in range(first, last):
                    ins = pe.matmul(bank(t - first), XB[:, t * P:(t + 1) * P], CW[:].rearrange("p a n -> p (a n)"),
                                    start=True, stop=True, skip_group_check=True)
                ins.then_inc(done, 1)

            def token_transform(i):
                pe.wait_ge(tf_ready, i + 1)
                pe.wait_ge(zb_out, i + 1)
                for k1 in range(8):
                    for part in range(2):
                        pe.matmul(PS[:, 1, k1 // 4, (k1 % 4) * P:(k1 % 4 + 1) * P], TF[:, k1, part, :],
                                  TB[:, k1, part, :], start=part == 0, stop=part == 1, skip_group_check=True)
                for part in range(2):
                    ins = pe.matmul(PS[:, 1, 2, 0:P], Z[:, 0, part, :], TB[:, 0, part, :],
                                    start=part == 0, stop=part == 1)
                ins.then_inc(f_done, 1)

            def group(i, m, slot, first):
                channel_weights(m, slot)
                if not first:
                    pe.wait_ge(ua_out, i)
                project(pe, i + KC, 0, 0, hhi, hlo)
                if not first:
                    token_transform(i - 1)
                pe.wait_ge(xb_out, i + 1)
                pe.wait_ge(cw_out, m * 2 + slot + 1)
                if not first:
                    pe.wait_ge(ub_out, i)
                to_tokens(0, 6, lambda t: PS[:, 0, t // 2, t % 2 * 256:t % 2 * 256 + 256], ua_done)
                to_tokens(6, 9, lambda t: PX[:, t // 2, t % 2 * 256:t % 2 * 256 + 256], ub_done)
                if not first:
                    pe.wait_ge(y_ready, i)
                project(pe, i + KC, 1, 1, hhi, hlo)

            group(0, 0, 0, True)
            group(1, 0, 1, False)
            with pe.Fori(1, KC // 2) as m:
                for slot in range(2):
                    group(m * 2 + slot, m, slot, False)
            token_transform(KC - 1)

        @block.scalar
        def _(act):
            def group(i, first):
                w_split_hi(act, i + KC, 1)
                act.wait_ge(cw_done, i + 1)
                if not first:
                    act.wait_ge(ub_done, i)
                act.activation(CW[:].rearrange("p a n -> p (a n)"), PX[:, 1, 256:512], ACT.Copy).then_inc(cw_out, 1)
                projected(act, i + KC, 0)
                act.activation(by_bank(XB[:]), PS[:, 0, :, 0:JW], ACT.Copy).then_inc(xb_out, 1)
                w_split_hi(act, i + KC + 1, 0)
                act.wait_ge(ua_done, i + 1)
                flat = PS[:, 0].rearrange("p b (t r n) -> p (b t) r n", t=2, r=2)
                act.activation(Z[:, 0], flat[:, 0], ACT.Copy, scale=float(np.sqrt(NLAT / NCTX)))
                act.activation(Z[:, 1:6], flat[:, 1:6], ACT.Copy).then_inc(ua_out, 1)
                act.wait_ge(ub_done, i + 1)
                act.activation(Z[:, 6:8], PX[:, 0, :].rearrange("p (t r n) -> p t r n", t=2, r=2), ACT.Copy)
                act.activation(Z[:, 8], PX[:, 1, 0:256].rearrange("p (r n) -> p r n", r=2), ACT.Copy).then_inc(ub_out, 1)
                projected(act, i + KC, 1)
                act.activation(by_bank(GZ[:]), PS[:, 1, :, 0:JW], ACT.Tanh, scale=0.5)
                act.activation(by_bank(ZH[:]), PS[:, 1, :, 0:JW], ACT.Copy, scale=0.5).then_inc(zb_out, 1)

            group(0, True)
            with act.Fori(1, KC) as i:
                group(i, False)

        @block.vector
        def _(dve):
            ch = Chain(dve, dve_chain)

            def tt(o, x, y, op):
                return dve.tensor_tensor(o, x, y, op)

            def eight_points(i):
                add, sub = ALU.add, ALU.subtract
                dve.wait_ge(ub_out, i + 1)
                tt(S[:, 0], Z[:, 1:5], Z[:, 5:9], add)
                ch.link(tt(S[:, 1], Z[:, 1:5], Z[:, 5:9], sub))
                odd = S[:, 1]
                tt(M[:, 0:2], S[:, 0, 0:2], S[:, 0, 2:4], add)
                ch.link(tt(M[:, 2:4], S[:, 0, 0:2], S[:, 0, 2:4], sub))
                tt(TF[:, 0], M[:, 0], M[:, 1], add)
                tt(TF[:, 4], M[:, 0], M[:, 1], sub)
                tt(TF[:, 2, 0], M[:, 2, 0], M[:, 3, 1], add)
                tt(TF[:, 2, 1], M[:, 2, 1], M[:, 3, 0], sub)
                tt(TF[:, 6, 0], M[:, 2, 0], M[:, 3, 1], sub)
                ch.link(tt(TF[:, 6, 1], M[:, 2, 1], M[:, 3, 0], add))
                ch.link(dve.tensor_scalar(odd[:, 1::2], odd[:, 1::2], float(half), None, ALU.mult))
                tt(S[:, 0, 0:2, 0], odd[:, 1::2, 0], odd[:, 1::2, 1], add)
                tt(S[:, 0, 0:2, 1], odd[:, 1::2, 1], odd[:, 1::2, 0], sub)
                tt(M[:, 0, 0], odd[:, 0, 0], odd[:, 2, 1], add)
                tt(M[:, 0, 1], odd[:, 0, 1], odd[:, 2, 0], sub)
                tt(M[:, 2, 0], odd[:, 0, 0], odd[:, 2, 1], sub)
                ch.link(tt(M[:, 2, 1], odd[:, 0, 1], odd[:, 2, 0], add))
                tt(M[:, 1, 0], S[:, 0, 0, 0], S[:, 0, 1, 1], add)
                tt(M[:, 1, 1], S[:, 0, 0, 1], S[:, 0, 1, 0], sub)
                tt(M[:, 3, 0], S[:, 0, 0, 0], S[:, 0, 1, 1], sub)
                ch.link(tt(M[:, 3, 1], S[:, 0, 0, 1], S[:, 0, 1, 0], add))
                tt(TF[:, 1], M[:, 0], M[:, 1], add)
                tt(TF[:, 5], M[:, 0], M[:, 1], sub)
                tt(TF[:, 3, 0], M[:, 2, 0], M[:, 3, 1], add)
                tt(TF[:, 3, 1], M[:, 2, 1], M[:, 3, 0], sub)
                tt(TF[:, 7, 0], M[:, 2, 0], M[:, 3, 1], sub)
                tt(TF[:, 7, 1], M[:, 2, 1], M[:, 3, 0], add).then_inc(tf_ready, 1)

            def gate(i):
                dve.wait_ge(zb_out, i + 1)
                ch.link(dve.scalar_tensor_tensor(GZ[:], GZ[:], 1.0, ZH[:], ALU.add, ALU.mult))

            def outputs(i, first):
                dve.wait_ge(f_done, i + 1)
                if not first:
                    dve.wait_ge(y_out, i * 16)
                b4 = B4[:, ds(i, 1)]
                by_k1 = "p (k2 k1) -> p k1 k2"
                dve.scalar_tensor_tensor(YT[:, 0:NCTX], PS[:, 1, 2, 0:P], b4, GZ[:, 0:NCTX], ALU.add, ALU.mult)
                ch.link(dve.scalar_tensor_tensor(
                    YT[:, NCTX:T].rearrange(by_k1, k1=8), PS[:, 1, 0:2, :].rearrange("p b (k n) -> p (b k) n", n=P), b4,
                    GZ[:, NCTX:T].rearrange(by_k1, k1=8), ALU.add, ALU.mult))
                dve.sem_inc(y_ready, 1)

            def group(i):
                w_split_lo(dve, i + KC, 1)
                if not isinstance(i, int) or i:
                    outputs(i - 1, isinstance(i, int))
                w_split_lo(dve, i + KC + 1, 0)
                eight_points(i)
                gate(i)

            dve.wait_ge(table_in, 48)
            group(0)
            before, LINKS = ch.n, 8
            group(1)
            assert ch.n == before + LINKS, ch.n - before
            with dve.Fori(2, KC) as i:
                ch.base, ch.n = before + (i - 1) * LINKS, 0
                group(i)
            ch.base, ch.n = before + (KC - 1) * LINKS, 0
            outputs(KC - 1, False)

        block.__exit__(None, None, None)

    def outputs(l, w_out, pair0, next_tiles):
        z = [zone]
        YHI = sb(f"y_hi_{l}", [P, 2 * KC, T], F32R, at=z)
        OUT = sb(f"out_{l}", [P, KC, T], at=z)
        z = list(norm_zone)
        ROWS = sb(f"out_rows_{l}", [P, 2, D], at=z)
        y_in = [sem(f"y_loaded_{l}_{q}") for q in range(4)]
        y_hi, y_lo, out_ready = sem(f"y_hi_ready_{l}"), sem(f"y_lo_ready_{l}"), sem(f"out_ready_{l}")
        x_in, scaled, x_ready, x_out = (sem(f"{s}_{l}") for s in ("residual_loaded", "out_normed", "x_ready", "x_stored"))
        sq_free, turned = sem(f"stats_read_{l}"), sem(f"rows_turned_{l}")
        rows_dve, rows_act = sem(f"rows_by_dve_{l}"), sem(f"rows_by_act_{l}")
        row_out = [sem(f"rows_stored_{l}_0"), sem(f"rows_stored_{l}_1")]
        last = pair0 + KC
        block = nc.Block()
        block.__enter__()

        def ylo(k):
            return (HHI if k < KC else HLO)[:, k % KC, :]

        @block.sync
        def _(sp):
            for q in range(4):
                dst = (HHI if q < 2 else HLO)[:, 4 * (q % 2):4 * (q % 2) + 4, :].bitcast(F32)
                sp.dma_start(dst, y_dram[4 * q:4 * q + 4].rearrange("k p t -> p k t")).then_inc(y_in[q], 16)
            with sp.Fori(0, KC - 1) as o:
                for half in range(2):
                    w_load(sp, o + pair0 + 1, half, out_tile(w_out, half, o * P + P))
            if next_tiles:
                for slot in range(2):
                    w_load(sp, last, slot, next_tiles[slot])
            projected(sp, last - 1, 1)
            sp.dma_start(XT[:], x_dram.rearrange("k p t -> p k t")).then_inc(x_in, 16)
            if l == 0:
                sp.wait_ge(x_ready, KC)
                sp.dma_start(x_dram.rearrange("k p t -> p k t"), XT[:]).then_inc(x_out, 16)
                sp.wait_ge(x_out, 16)
            else:
                for t in range(NT):
                    sp.wait_ge(rows_act if t % 2 else rows_dve, t // 2 + 1)
                    dst = out["y_prompt"][0] if t == 0 else out["y_sample"][0, (t - 1) * P:t * P, :]
                    sp.dma_start(dst, ROWS[:, t % 2, :]).then_inc(row_out[t % 2], 16)
                sp.wait_ge(row_out[0], 16 * 5)
                sp.wait_ge(row_out[1], 16 * 4)

        @block.tensor
        def _(pe):
            def out_block(o, group, free, ready=None):
                if free is not None:
                    pe.wait_ge(out_ready, free)
                for half in range(2):
                    project(pe, o + pair0, half, group, lambda k: YHI[:, k, :], ylo, k0=half * KC,
                            start=half == 0, stop=half == 1, ready=ready)

            out_block(0, 0, None, lambda k: pe.wait_ge(y_lo, k + 1))
            out_block(1, 1, None)
            with pe.Fori(1, KC // 2) as m:
                for b in range(2):
                    out_block(m * 2 + b, b, m * 2 + b - 1)
            stats_pe(pe, 2 * l + 1, SQ)
            if l == 0:
                stats_pe(pe, 2, SQ)
            else:
                for t in range(NT):
                    if t == 0:
                        pe.wait_ge(x_ready, KC)
                    else:
                        if t >= 2:
                            pe.wait_ge(rows_act if t % 2 else rows_dve, t // 2)
                    for k in range(KC):
                        ins = pe.transpose(PS[:, t % 2, k // 4, (k % 4) * P:(k % 4 + 1) * P],
                                           XT[:, k, t * P:(t + 1) * P], IDENT[:])
                    ins.then_inc(turned, 1)

        @block.scalar
        def _(act):
            for k in range(2 * KC):
                if k % 4 == 0:
                    act.wait_ge(y_in[k // 4], 16)
                act.activation(YHI[:, k, :], ylo(k).bitcast(F32), ACT.Copy).then_inc(y_hi, 1)
                if k == 3:
                    w_split_hi(act, pair0, 1)

            def evacuate(o, group):
                projected(act, o + pair0, 1)
                act.activation(OUT[:, ds(o, 1), :].rearrange("p a (j n) -> p (a j) n", n=JW), PS[:, group, :, 0:JW],
                               ACT.Copy).then_inc(out_ready, 1)

            def out_block(o, group):
                w_split_hi(act, o + pair0 + 1, 0)
                w_split_hi(act, o + pair0 + 1, 1)
                evacuate(o, group)

            with act.Fori(0, KC // 2 - 1) as m:
                for b in range(2):
                    out_block(m * 2 + b, b)
            out_block(KC - 2, 0)
            if next_tiles:
                w_split_hi(act, last, 0)
            evacuate(KC - 1, 1)
            act.wait_ge(out_ready, KC)
            stats_act(act, 2 * l + 1, lambda k: OUT[:, k, :], SQ)
            if l == 0:
                stats_act(act, 2, lambda k: XT[:, k, :], SQ, x_ready)
                h_act(act, 1, TMP)
            else:
                for t in range(1, NT, 2):
                    act.wait_ge(turned, t + 1)
                    if t >= 3:
                        act.wait_ge(row_out[1], 16 * (t // 2))
                    act.activation(ROWS[:, 1, :], PS[:, 1, 0:2, :].rearrange("p b n -> p (b n)"),
                                   ACT.Copy).then_inc(rows_act, 1)

        @block.vector
        def _(dve):
            for k in range(2 * KC):
                dve.wait_ge(y_hi, k + 1)
                dve.tensor_tensor(ylo(k), ylo(k).bitcast(F32), YHI[:, k, :].bitcast(F32), ALU.subtract).then_inc(y_lo, 1)
                if k == 3:
                    w_split_lo(dve, pair0, 1)
            with dve.Fori(0, KC - 1) as o:
                for half in range(2):
                    w_split_lo(dve, o + pair0 + 1, half)
            if next_tiles:
                w_split_lo(dve, last, 0)
            stats_dve(dve, 2 * l + 1)
            dve.wait_ge(rstd_spread, 2 * l + 2)
            dve.wait_ge(x_in, 16)
            for k in range(KC + 1):
                if k < KC:
                    dve.tensor_tensor(by_bank(OUT[:, k, :]), by_bank(OUT[:, k, :]), PS[:, 0, :, 0:JW],
                                      ALU.mult).then_inc(scaled, 1)
                if k:
                    dve.wait_ge(scaled, k)
                    for t0, t1, c in SEGS:
                        ins = dve.scalar_tensor_tensor(XT[:, k - 1, t0:t1], OUT[:, k - 1, t0:t1],
                                                       GP[:, l, k - 1, c:c + 1], XT[:, k - 1, t0:t1], ALU.mult, ALU.add)
                    ins.then_inc(x_ready, 1)
            if l == 0:
                stats_dve(dve, 2)
                h_dve(dve, 1, lambda k: XT[:, k, :], TMP)
            else:
                for t in range(0, NT, 2):
                    dve.wait_ge(turned, t + 1)
                    if t >= 2:
                        dve.wait_ge(row_out[0], 16 * (t // 2))
                    dve.tensor_copy(ROWS[:, 0, :], PS[:, 0, 0:2, :].rearrange("p b n -> p (b n)")).then_inc(rows_dve, 1)

        block.__exit__(None, None, None)

    ROWS_N = 40
    head_zone = [zone]
    TOK = sb("token_scalars", [P, 3, 2, H, NT], at=head_zone)
    DEC = sb("chunk_decay", [P, 2, H, NT], at=head_zone)
    rows_dram = nc.dram_tensor("gate_rows", (2, 2, H, T), F32).ap()
    dec_dram = nc.dram_tensor("decay_rows", (2, H, NT), F32).ap()

    def gates():
        z = list(head_zone)
        GWR = sb("gate_w_raw", [P, KC * P], at=z)
        GWH = sb("gate_w_hi", [P, KC * P], F32R, at=z)
        GWL = sb("gate_w_lo", [P, KC * P], F32R, at=z)
        G = sb("gate_products", [P, T], at=z)
        IG, FG, B, A, M, E, S, S2, RST, DEL, WI, WK = (sb("rows_" + n, [ROWS_N, T], at=z) for n in (
            "i", "f", "b", "a", "m", "e", "s", "s2", "reset", "shift", "carry", "keep"))
        BI, BF, M0 = (sb("row_" + n, [ROWS_N, 1], at=z) for n in ("b_i", "b_f", "m0"))
        MP, ME, DR, NM = (sb("chunk_" + n, [ROWS_N, NT], at=z) for n in ("m_before", "m_end", "decay", "m_new"))
        gw_in, small_in, gw_hi, gw_lo, product, rows_sb = (sem(s) for s in (
            "gate_w_loaded", "gate_small_loaded", "gate_w_hi_ready", "gate_w_lo_ready", "gates_product", "gates_in_sbuf"))
        cleared, moved, f_ready, exp_ready, args_ready, exps_ready, neg_ready = (sem(s) for s in (
            "rows_cleared", "rows_moved", "f_rows_ready", "exp_f_ready", "exponents_ready", "exponentials_ready",
            "rows_out_ready"))
        f_abs, turned, stored, m_out, dec_in, act_e = (sem(s) for s in (
            "f_abs_ready", "tokens_turned", "gate_rows_stored", "new_m_stored", "decay_spread", "decay_exp_ready"))
        chain = sem("gates_dve_chain")
        parts = ((0, 0), (1, 32))
        block = nc.Block()
        block.__enter__()

        @block.sync
        def _(sp):
            sp.dma_start(GWR[:].rearrange("p (k n) -> p k n", k=KC),
                         in_tile(a["w_in_o"][0], a["w_in_o"].shape[2] - P)).then_inc(gw_in, 16)
            sp.dma_start(RST[:], a["reset"]).then_inc(small_in, 16)
            sp.wait_ge(cleared, 1)
            with nc.allow_non_contiguous_dma("vectors, one element per partition"):
                for d, r in parts:
                    sp.dma_start(BI[r:r + H, :], a["b_if"][0, d, 0].rearrange("(h o) -> h o", o=1)).then_inc(small_in, 16)
                    sp.dma_start(BF[r:r + H, :], a["b_if"][0, d, 1].rearrange("(h o) -> h o", o=1)).then_inc(small_in, 16)
                    sp.dma_start(M0[r:r + H, :], a["state_mlstm_m"][0, 0, d].rearrange("(h o) -> h o", o=1)
                                 ).then_inc(small_in, 16)
            sp.wait_ge(rows_sb, 1)
            for d, r in parts:
                for n, dst in enumerate((IG, FG)):
                    first = P - 4 * H + (2 * d + n) * H
                    sp.dma_start(dst[r:r + H, :], G[first:first + H, :]).then_inc(moved, 16)
            sp.wait_ge(neg_ready, 1)
            for d, r in parts:
                sp.dma_start(rows_dram[0, d], M[r:r + H, :]).then_inc(stored, 16)
                with nc.allow_non_contiguous_dma("one element per partition"):
                    sp.dma_start(out["new_m"][0, 0, d].rearrange("(h o) -> h o", o=1), NM[r:r + H, 0:1]).then_inc(m_out, 16)
            sp.wait_ge(exps_ready, 4)
            for d, r in parts:
                sp.dma_start(rows_dram[1, d], WI[r:r + H, :]).then_inc(stored, 16)
                sp.dma_start(dec_dram[d], DR[r:r + H, :]).then_inc(stored, 16)
            sp.wait_ge(stored, 16 * 6)
            sp.dma_start(DEC[:].rearrange("p d h c -> p (d h c)"),
                         dec_dram.rearrange("d h c -> (d h c)").partition_broadcast(P)).then_inc(dec_in, 16)
            sp.wait_ge(dec_in, 16)
            sp.wait_ge(m_out, 32)

        @block.tensor
        def _(pe):
            pe.wait_ge(gw_lo, 1)
            for k in range(KC):
                for m, (w, h) in enumerate(((GWH, HHI), (GWH, HLO), (GWL, HHI))):
                    for j in range(NJ):
                        ins = pe.matmul(PS[:, 0, j, 0:JW], w[:, k * P:(k + 1) * P], h[:, k, j * JW:(j + 1) * JW],
                                        start=k == 0 and m == 0, stop=k == KC - 1 and m == 2)
            ins.then_inc(product, 1)
            pe.wait_ge(exps_ready, 4)
            for q, rows in enumerate((A, E, WK)):
                for c in range(NT):
                    ins = pe.transpose(PS[:, 1, q, c * ROWS_N:(c + 1) * ROWS_N], rows[:, c * P:(c + 1) * P],
                                       IDENT[0:ROWS_N, 0:ROWS_N])
            ins.then_inc(turned, 1)

        @block.scalar
        def _(act):
            act.wait_ge(gw_in, 16)
            act.activation(GWH[:], GWR[:], ACT.Copy).then_inc(gw_hi, 1)
            act.wait_ge(product, 1)
            act.activation(by_bank(G[96:128, :]), PS[96:128, 0, :, 0:JW], ACT.Copy).then_inc(rows_sb, 1)
            act.wait_ge(f_ready, 1)
            act.activation(E[:], FG[:], ACT.Abs).then_inc(f_abs, 1)
            act.wait_ge(f_abs, 1)
            act.activation(E[:], E[:], ACT.Exp, scale=-1.0).then_inc(exp_ready, 1)
            act.wait_ge(args_ready, 1)
            act.activation(WI[:], WI[:], ACT.Exp).then_inc(exps_ready, 1)
            act.activation(E[:], S2[:], ACT.Exp, scale=-1.0).then_inc(exps_ready, 1)
            act.activation(WK[:], WK[:], ACT.Exp).then_inc(exps_ready, 1)
            act.activation(DR[:], DR[:], ACT.Exp).then_inc(exps_ready, 1)

        @block.vector
        def _(dve):
            ch = Chain(dve, chain)
            for t in (IG, FG, BI, BF, M0, DEL, M, B):
                ins = dve.memset(t[:], 0.0)
            ch.link(ins)
            dve.sem_inc(cleared, 1)
            dve.wait_ge(gw_hi, 1)
            dve.tensor_tensor(GWL[:], GWR[:], GWH[:].bitcast(F32), ALU.subtract).then_inc(gw_lo, 1)
            dve.wait_ge(moved, 64)
            dve.wait_ge(small_in, 16 * 7)
            dve.tensor_scalar(FG[:], FG[:], BF[:, 0:1], None, ALU.add).then_inc(f_ready, 1)
            ch.link(dve.tensor_scalar(IG[:], IG[:], BI[:, 0:1], None, ALU.add))
            dve.wait_ge(f_ready, 1)
            dve.wait_ge(exp_ready, 1)
            log1p(dve, ch, E[:], S[:], S2[:])
            ch.link(dve.scalar_tensor_tensor(S[:], FG[:], 0.0, S[:], ALU.min, ALU.subtract))
            dve.tensor_tensor_scan(B[0:H, :], RST[0:H, :], S[0:H, :], 0.0, op0=ALU.mult, op1=ALU.add)
            ch.link(dve.tensor_tensor_scan(B[32:40, ::-1], RST[32:40, ::-1], S[32:40, ::-1], 0.0, op0=ALU.mult, op1=ALU.add))
            ch.link(dve.tensor_tensor(A[:], IG[:], B[:], ALU.subtract))
            dve.tensor_copy(DEL[0:H, 256::P], B[0:H, 255:T - 1:P])
            ch.link(dve.tensor_copy(DEL[32:40, 255:T - 1:P], B[32:40, 256::P]))
            for t0, t1 in ((0, NCTX), (NCTX, T)):
                for d, r in parts:
                    w = slice(t0, t1) if d == 0 else slice(t1 - 1, None if t0 == 0 else t0 - 1, -1)
                    first = 0.0 if t0 == 0 else M0[r:r + H, 0:1]
                    ins = dve.tensor_tensor_scan(M[r:r + H, w], DEL[r:r + H, w], A[r:r + H, w], first,
                                                 op0=ALU.add, op1=ALU.max)
            ch.link(ins)
            ch.link(dve.tensor_tensor(S2[:], B[:], M[:], ALU.add))
            ch.link(dve.memset(MP[:], 0.0))
            dve.memset(ME[:], 0.0)
            ch.link(dve.memset(NM[:], 0.0))
            dve.tensor_copy(MP[0:H, 1:2], M0[0:H, :])
            dve.tensor_copy(MP[32:40, 8:9], M0[32:40, :])
            dve.tensor_copy(MP[0:H, 2:9], S2[0:H, 255:T - 1:P])
            dve.tensor_copy(MP[32:40, 1:8], S2[32:40, 256::P])
            dve.tensor_copy(ME[0:H, :], M[0:H, P - 1::P])
            dve.tensor_copy(ME[32:40, :], M[32:40, 0::P])
            dve.tensor_copy(NM[0:H, 0:1], S2[0:H, P - 1:P])
            ch.link(dve.tensor_copy(NM[32:40, 0:1], S2[32:40, 0:1]))
            rows3 = "r (c n) -> r c n"
            spread = [ROWS_N, NT, P]
            dve.tensor_tensor(WI[:].rearrange(rows3, n=P), MP[:].unsqueeze(2).to_broadcast(spread),
                              M[:].rearrange(rows3, n=P), ALU.subtract)
            dve.tensor_tensor(WK[:].rearrange(rows3, n=P), A[:].rearrange(rows3, n=P),
                              ME[:].unsqueeze(2).to_broadcast(spread), ALU.subtract)
            ch.link(dve.tensor_tensor(DR[:], MP[:], ME[:], ALU.subtract))
            dve.sem_inc(args_ready, 1)
            ch.link(dve.tensor_scalar(M[:], M[:], -1.0, None, ALU.mult))
            dve.sem_inc(neg_ready, 1)
            dve.wait_ge(turned, 1)
            for q in range(3):
                for d, r in parts:
                    dve.tensor_copy(TOK[:, q, d], PS[:, 1, q, 0:NT * ROWS_N].rearrange("p (c r) -> p r c", r=ROWS_N)[:, r:r + H, :])

        block.__exit__(None, None, None)

    w_o = a["w_in_o"][0]

    DK, DV = P, 2 * P
    DV1 = DV + 1
    QCOL, KCOL, VCOL, OCOL, ZCOL = 0, D, 2 * D, 4 * D, 6 * D
    PAIR0 = 3 * KC

    def mlstm():
        z = list(head_zone)
        QT = sb("q_t", [P, 2, T], at=z)
        KT = sb("k_t", [P, 2, T], at=z)
        V = sb("v_rows", [P, 2, NT, DV1], at=z)
        G = sb("out_gate", [P, 2, 2 * T], at=z)
        DM = sb("decay_matrix", [P, 2, T], at=z)
        QW = sb("q_carry", [P, 2, T], at=z)
        KW = sb("k_rows", [P, 2, T], at=z)
        HS = sb("h_rows", [P, NT, DV], at=z)
        TO = sb("o_tanh", [P, T], at=z)
        TZ = sb("z_tanh", [P, T], at=z)
        C = sb("state", [P, 2, DV1], at=z)
        CC = sb("context_state", [P, 2, DV1], at=z)
        MK = sb("causal", [P, 2, P], at=z)
        TK = sb("head_scalars", [P, 3, 2, NT], at=z)
        DC = sb("head_decay", [P, 2, NT], at=z)
        R = sb("inverse_den", [P, 2], at=z)

        BANK = [PS[:, 1, 0], PS[:, 1, 1], PS[:, 1, 2], PX[:, 0], PX[:, 1]]
        NUM, KV = BANK[0:2], BANK[3:5]
        KS_BANK = [BANK[2], BANK[3], BANK[4], BANK[0], BANK[1], BANK[2]]
        ROUNDS = [(0, 4), (4, 8), (8, 9)]

        mask_in, ones_ready = sem("causal_loaded"), sem("v_ones_ready")
        rows_in, carry_in, c_in = sem("max_rows_loaded"), sem("carry_rows_loaded"), sem("state_loaded")
        va_done, evacuated = sem("v_first_product"), sem("projection_evacuated")
        ks_done, ks_out = sem("k_and_scores_done"), sem("k_and_scores_evacuated")
        turned, post_out, y_out = sem("h_turned"), sem("y_ready"), sem("y_stored")
        num_done, num_out, kv_done, c_ready = (sem(s) for s in (
            "numerator_done", "numerator_read", "state_product_done", "state_ready"))
        d_args, d_exp, p_ready, cc_out = (sem(s) for s in (
            "weights_exponent_ready", "weights_ready", "scores_ready", "context_state_stored"))
        z_ready, g_ready = sem("z_parts_ready"), sem("gate_ready")
        chain = sem("mlstm_dve_chain")
        block = nc.Block()
        block.__enter__()

        def pair(j, n):
            return j * 4 + (PAIR0 + n // 2), n % 2

        def v_tile(j, half):
            return w_o.rearrange("(k p) n -> p k n", p=P)[:, 4 * half:4 * half + 4, ds(j * DV + VCOL, DV)]

        def tile_source(j, n):
            if n in (2, 3):
                return v_tile(j, n - 2)
            if n < 2:
                return in_tile(w_o, j * P + (QCOL, KCOL)[n])
            return in_tile(w_o, j * DV + (OCOL, ZCOL)[n % 2] + (n - 4) // 2 * P)

        def run(eng, body, chained=None):
            body(0, 0, True, False, False)
            body(1, 1, True, True, False)
            if chained:
                chained.start()
            with eng.Fori(1, H // 2 - 1) as m:
                for b in range(2):
                    if chained:
                        chained.turn(m, b)
                    body(m * 2 + b, b, True, True, True)
            if chained:
                chained.stop()
            body(H - 2, 0, True, True, True)
            body(H - 1, 1, True, True, True, last=True)
            body(H, 0, False, True, True)

        @block.sync
        def _(sp):
            sp.dma_start(MK[:], a["causal"]).then_inc(mask_in, 16)

            def context_state(h):
                sp.wait_ge(c_ready, h * 8 + 1)
                with nc.allow_non_contiguous_dma("normalisers, one element per partition"):
                    for d in range(2):
                        sp.dma_start(out["new_C"][0, 0, d, ds(h, 1)].rearrange("h k v -> k (h v)"),
                                     CC[:, d, 0:DV]).then_inc(cc_out, 16)
                        sp.dma_start(out["new_n"][0, 0, d, ds(h, 1)].rearrange("h k -> k h"),
                                     CC[:, d, DV:DV1]).then_inc(cc_out, 16)

            def store_y(h, p):
                sp.wait_ge(post_out, h * 5 + 5)
                sp.dma_start(y_dram[ds(h * 2, 2)].rearrange("b p t -> p b t"),
                             G[:, p, :].rearrange("p (b t) -> p b t", b=2)).then_inc(y_out, 16)

            def body(j, p, project_it, ml, post, last=False):
                if ml:
                    h = j - 1
                    if post:
                        sp.wait_ge(num_done, h * 9)
                    sp.dma_start(DM[:], rows_dram[0, :, ds(h, 1)].rearrange("d h t -> (d h) t").partition_broadcast(P)
                                 ).then_inc(rows_in, 16)
                    sp.dma_start(QW[:], rows_dram[1, :, ds(h, 1)].rearrange("d h t -> (d h) t").partition_broadcast(P)
                                 ).then_inc(carry_in, 16)
                    with nc.allow_non_contiguous_dma("normalisers, one element per partition"):
                        for d in range(2):
                            sp.dma_start(C[:, d, 0:DV], a["state_mlstm_C"][0, 0, d, ds(h, 1)].rearrange("h k v -> k (h v)")
                                         ).then_inc(c_in, 16)
                            sp.dma_start(C[:, d, DV:DV1], a["state_mlstm_n"][0, 0, d, ds(h, 1)].rearrange("h k -> k h")
                                         ).then_inc(c_in, 16)
                for n in (2, 3, None, 4, 5, "context", 6, 7, 8, 9):
                    if n is None:
                        if post:
                            store_y(j - 2, p)
                    elif n == "context":
                        if ml:
                            context_state(j - 1)
                    elif project_it:
                        if n < 8:
                            w_load(sp, *pair(j, n), tile_source(j, n))
                        elif last:
                            w_load(sp, *pair(j, n), out_tile(a["w_out_o"][0], n - 8, 0))
                        else:
                            w_load(sp, *pair(j, n), tile_source(j + 1, n - 8))

            run(sp, body)
            store_y(H - 1, (H - 1) % 2)
            sp.wait_ge(y_out, 16 * H)
            sp.wait_ge(cc_out, 64 * H)
            sp.wait_ge(mask_in, 16)

        @block.tensor
        def _(pe):
            def k_and_scores(h, q, post):
                for r in range(6):
                    t0, t1 = ROUNDS[r % 3]
                    if post and r >= 3:
                        pe.wait_ge(num_out, h * 9)
                    if post and r in (1, 2):
                        pe.wait_ge(c_ready, h * 8)
                    if r == 5:
                        pe.wait_ge(ks_out, h * 6 + 1)
                    for t in range(t0, t1):
                        dst = KS_BANK[r][:, (t - t0) * P:(t - t0 + 1) * P]
                        cols = slice(t * P, (t + 1) * P)
                        if r < 3:
                            ins = pe.transpose(dst, KT[:, q, cols], IDENT[:])
                        else:
                            ins = pe.matmul(dst, KT[:, q, cols], QT[:, q, cols], start=True, stop=True,
                                            skip_group_check=True)
                    ins.then_inc(ks_done, 1)

            def turn_h(h, ks):
                if ks:
                    pe.wait_ge(ks_out, h * 6 + 12)
                pe.wait_ge(num_out, h * 9 + 9)
                for r in range(5):
                    for n in range(4 * r, min(4 * r + 4, 2 * NT)):
                        ins = pe.transpose(BANK[r][:, n % 4 * P:(n % 4 + 1) * P],
                                           HS[:, n % NT, n // NT * P:(n // NT + 1) * P], IDENT[:])
                    ins.then_inc(turned, 1)

            def step(h, q, s, post):
                if s == 0:
                    pe.wait_ge(p_ready, h + 1)
                    pe.wait_ge(ks_out, h * 6 + 6)
                    if post:
                        pe.wait_ge(post_out, h * 5)
                if s == 1:
                    pe.wait_ge(c_in, h * 64 + 64)
                if s < 8:
                    if s:
                        pe.wait_ge(c_ready, h * 8 + s)
                    for d in range(2):
                        t = s if d == 0 or s == 0 else 9 - s
                        ins = pe.matmul(KV[d][:, 0:DV1], KW[:, d, t * P:(t + 1) * P], V[:, q, t, :], start=True, stop=True)
                    ins.then_inc(kv_done, 1)
                else:
                    pe.wait_ge(c_ready, h * 8 + s)
                if s:
                    pe.wait_ge(num_out, h * 9 + s)
                for d in range(2):
                    t = s if d == 0 or s == 0 else 9 - s
                    cols = slice(t * P, (t + 1) * P)
                    ins = pe.matmul(NUM[d][:, 0:DV1], DM[:, d, cols], V[:, q, t, :], start=True, stop=s == 0)
                    if s:
                        ins = pe.matmul(NUM[d][:, 0:DV1], QW[:, d, cols], C[:, d, :], start=False, stop=True)
                ins.then_inc(num_done, 1)

            def values(j, first, last, done):
                for k in range(KC):
                    half, kk = divmod(k, 4)
                    if kk == 0:
                        pair_n, slot = pair(j, 2 + half)
                        pe.wait_ge(w_lo, pair_n * 2 + slot + 1)
                    cols = slice(kk * DV, (kk + 1) * DV)
                    for t in range(first, last):
                        n = t - first
                        dst = PS[:, 0, n // 2, n % 2 * DV:(n % 2 + 1) * DV]
                        for m, (h, w) in enumerate(((HHI, WHI), (HHI, WLO), (HLO, WHI))):
                            ins = pe.matmul(dst, h[:, k, t * P:(t + 1) * P], w[:, half, cols],
                                            start=k == 0 and m == 0 and n % 2 == 0, stop=k == KC - 1 and m == 2,
                                            skip_group_check=True)
                    if done is None and kk == 3:
                        ins.then_inc(w_used, 1)
                if done is not None:
                    ins.then_inc(done, 1)

            def body(j, p, project_it, ml, post, last=False):
                h, q = j - 1, 1 - p

                def job(n):
                    pe.wait_ge(evacuated, j * 8 + n)
                    if n == 2:
                        values(j, 0, 6, va_done)
                    elif n == 3:
                        values(j, 6, 9, None)
                    else:
                        project(pe, *pair(j, n), 0, hhi, hlo)

                if ml:
                    k_and_scores(h, q, post)
                if project_it:
                    job(0)
                if post:
                    turn_h(h - 1, True)
                if project_it:
                    job(1)
                steps = ((0, 1), (2,), (3,), (4,), (5,), (6,), (7, 8))
                for n, some in enumerate(steps):
                    if ml:
                        for s in some:
                            step(h, q, s, post)
                    if project_it and n + 2 < 8:
                        job(n + 2)

            pe.wait_ge(ones_ready, 1)
            run(pe, body)
            turn_h(H - 1, False)

        @block.scalar
        def _(act):
            def body(j, p, project_it, ml, post, last=False):
                if project_it:
                    w_split_hi(act, *pair(j, 1))
                if ml:
                    act.wait_ge(d_args, j)
                    act.activation(DM[:], DM[:], ACT.Exp).then_inc(d_exp, 1)
                if not project_it:
                    return
                group = PS[:, 0, :, 0:JW]
                rows = PS[:, 0].rearrange("p b (t n) -> p (b t) n", n=DV)
                for n in range(8):
                    if n == 2:
                        act.wait_ge(va_done, j + 1)
                        act.activation(V[:, p, 0:6, 0:DV], rows, ACT.Copy).then_inc(evacuated, 1)
                        w_split_hi(act, *pair(j, 4))
                        continue
                    projected(act, *pair(j, n))
                    if n == 0:
                        ins = act.activation(by_bank(QT[:, p, :]), group, ACT.Copy, scale=float(DK) ** -0.5)
                    elif n == 1:
                        ins = act.activation(by_bank(KT[:, p, :]), group, ACT.Copy)
                    elif n == 3:
                        ins = act.activation(V[:, p, 6:9, 0:DV], rows[:, 0:3], ACT.Copy)
                    elif n in (4, 6):
                        act.wait_ge(g_ready, j * 2 + (n - 4) // 2)
                        ins = act.activation(by_bank(TO[:]), group, ACT.Tanh, scale=0.5)
                    else:
                        b = (n - 5) // 2
                        if b == 0 and post:
                            act.wait_ge(y_out, j * 16 - 16)
                        act.activation(by_bank(TZ[:]), group, ACT.Tanh, scale=0.5).then_inc(z_ready, 1)
                        ins = act.activation(by_bank(G[:, p, b * T:(b + 1) * T]), group, ACT.Copy, scale=0.25)
                    ins.then_inc(evacuated, 1)
                    if n != 7:
                        w_split_hi(act, *pair(j, {0: 2, 1: 3, 3: 5, 4: 6, 5: 7, 6: 8}[n]))

            run(act, body)

        @block.vector
        def _(dve):
            ch = Chain(dve, chain)

            def load_scalars(h):
                ch.link(dve.tensor_copy(TK[:], TOK[:, :, :, ds(h, 1), :].rearrange("p q d h c -> p q (d h) c")))
                ch.link(dve.tensor_copy(DC[:], DEC[:, :, ds(h, 1), :].rearrange("p d h c -> p (d h) c")))

            def by_tile(ap):
                return ap.rearrange("p (c n) -> p c n", n=P)

            def prepare(h, q):
                load_scalars(h)
                for r, (t0, t1) in enumerate(ROUNDS):
                    dve.wait_ge(ks_done, h * 6 + r + 1)
                    shape = [P, t1 - t0, P]
                    for d in range(2):
                        ins = dve.tensor_tensor(by_tile(KW[:, d, t0 * P:t1 * P]), by_tile(KS_BANK[r][:, 0:(t1 - t0) * P]),
                                                TK[:, 2, d, t0:t1].unsqueeze(2).to_broadcast(shape), ALU.mult)
                        if d == 0:
                            ch.link(ins)
                    ins.then_inc(ks_out, 1)
                dve.wait_ge(rows_in, h * 16 + 16)
                shape = [P, NT, P]
                for d in range(2):
                    ch.link(dve.tensor_tensor(by_tile(DM[:, d, :]), by_tile(DM[:, d, :]),
                                              TK[:, 0, d, :].unsqueeze(2).to_broadcast(shape), ALU.add))
                    ins = dve.tensor_tensor(by_tile(DM[:, d, :]), by_tile(DM[:, d, :]),
                                            MK[:, d, :].unsqueeze(1).to_broadcast(shape), ALU.add)
                    ch.link(ins)
                dve.sem_inc(d_args, 1)
                dve.wait_ge(carry_in, h * 16 + 16)
                ch.link(dve.tensor_tensor(QW[:], QW[:], QT[:, q, :].unsqueeze(1).to_broadcast([P, 2, T]), ALU.mult))
                dve.wait_ge(d_exp, h + 1)
                for r, (t0, t1) in enumerate(ROUNDS):
                    dve.wait_ge(ks_done, h * 6 + r + 4)
                    w = slice(t0 * P, t1 * P)
                    for d in range(2):
                        ins = dve.tensor_tensor(DM[:, d, w], DM[:, d, w], KS_BANK[3 + r][:, 0:(t1 - t0) * P], ALU.mult)
                        if d == 0:
                            ch.link(ins)
                    ins.then_inc(ks_out, 1)
                dve.wait_ge(ks_out, h * 6 + 6)
                dve.sem_inc(p_ready, 1)

            def finish_y(h, p):
                for r in range(5):
                    dve.wait_ge(turned, h * 5 + r + 1)
                    w = slice(4 * r * P, min(4 * r + 4, 2 * NT) * P)
                    dve.tensor_tensor(G[:, p, w], G[:, p, w], BANK[r][:, 0:w.stop - w.start], ALU.mult).then_inc(post_out, 1)

            def step(h, s, post):
                tiles = (s, s if s == 0 else 9 - s)
                if s < 8:
                    dve.wait_ge(kv_done, h * 8 + s + 1)
                    if s == 0:
                        if post:
                            dve.wait_ge(cc_out, h * 64)
                        ch.link(dve.tensor_copy(CC[:, 0, :], KV[0][:, 0:DV1]))
                        dve.tensor_copy(CC[:, 1, :], KV[1][:, 0:DV1]).then_inc(c_ready, 1)
                dve.wait_ge(num_done, h * 9 + s + 1)
                if 0 < s < 8:
                    for d in range(2):
                        ins = dve.scalar_tensor_tensor(C[:, d, :], C[:, d, :], DC[:, d, tiles[d]:tiles[d] + 1],
                                                       KV[d][:, 0:DV1], ALU.mult, ALU.add)
                        if d == 0:
                            ch.link(ins)
                    ins.then_inc(c_ready, 1)
                den = PS[:, 1, 0:2, DV]
                floor = TK[:, 1].rearrange("p d c -> p (d c)")[:, tiles[0]:NT + tiles[1] + 1:NT + tiles[1] - tiles[0]]
                ch.link(dve.scalar_tensor_tensor(R[:], den, -1.0, floor, ALU.mult, ALU.max))
                ch.link(dve.tensor_tensor(R[:], den, R[:], ALU.max))
                ch.link(dve.reciprocal(R[:], R[:]))
                for d, t in enumerate(tiles):
                    if s > 4 or (s == 0 and d == 1):
                        ins = dve.scalar_tensor_tensor(HS[:, t, :], NUM[d][:, 0:DV], R[:, d:d + 1], HS[:, t, :],
                                                       ALU.mult, ALU.add)
                    else:
                        ins = dve.tensor_scalar(HS[:, t, :], NUM[d][:, 0:DV], R[:, d:d + 1], None, ALU.mult)
                    if d == 0:
                        ch.link(ins)
                ins.then_inc(num_out, 1)

            def gate(j, p, b):
                dve.wait_ge(evacuated, j * 8 + 6 + 2 * b)
                g = G[:, p, b * T:(b + 1) * T]
                ch.link(dve.scalar_tensor_tensor(g, TZ[:], 1.0, g, ALU.add, ALU.mult))
                dve.scalar_tensor_tensor(g, TO[:], 1.0, g, ALU.add, ALU.mult).then_inc(g_ready, 1)

            def body(j, p, project_it, ml, post, last=False):
                h = j - 1

                def split(n):
                    if project_it:
                        w_split_lo(dve, *pair(j, n))

                def steps(*some):
                    if ml:
                        for s in some:
                            step(h, s, post)

                split(1)
                if ml:
                    prepare(h, 1 - p)
                split(2)
                if post:
                    finish_y(h - 1, p)
                split(3)
                steps(0, 1)
                steps(2)
                split(4)
                steps(3)
                split(5)
                steps(4)
                split(6)
                steps(5)
                if project_it:
                    gate(j, p, 0)
                split(7)
                steps(6)
                split(8)
                steps(7, 8)
                if project_it:
                    gate(j, p, 1)

            LINKS = 59

            class Heads:

                def start(self):
                    self.before = ch.n

                def turn(self, m, b):
                    assert b == 0 or ch.n == LINKS, ch.n
                    ch.base, ch.n = m * (2 * LINKS) + (self.before + (b - 2) * LINKS), 0

                def stop(self):
                    assert ch.n == LINKS, ch.n
                    ch.base, ch.n = 0, self.before + 2 * LINKS * (H // 2 - 2)

            dve.memset(V[:, :, :, DV:DV1].rearrange("p a t o -> p a (t o)"), 1.0).then_inc(ones_ready, 1)
            dve.wait_ge(mask_in, 16)
            run(dve, body, Heads())
            finish_y(H - 1, (H - 1) % 2)

        block.__exit__(None, None, None)

    setup()
    lru()
    fourier()
    outputs(0, a["w_out_e"][0], 2 * KC, [in_tile(w_o, 0), in_tile(w_o, D)])
    gates()
    mlstm()
    outputs(1, a["w_out_o"][0], 7 * KC, None)


def consts():
    b, k1, k2 = np.arange(P)[:, None, None], np.arange(8)[None, :, None], np.arange(P)[None, None, :]
    turn = 2 * np.pi * (b * (k1 + 8 * k2) % NLAT) / NLAT
    token = np.stack([np.cos(turn), np.sin(turn)], axis=2)
    turn = 2 * np.pi * (np.arange(P)[:, None] * np.arange(P)[None, :] % P) / P
    channel = np.stack([np.cos(turn), -np.sin(turn)], axis=1) / np.sqrt(NLAT * P)
    t = np.arange(T) % P
    reset = np.where(np.arange(40)[:, None] < 32, t != 0, t != P - 1)
    s, t = np.arange(P)[:, None, None], np.arange(P)[None, None, :]
    hidden = np.concatenate([s > t, s < t], axis=1)
    return {"causal": np.where(hidden, np.float32(-3e38), np.float32(0)), "reset": reset.astype(np.float32), "ident": np.eye(P, dtype=np.float32), "ones": np.ones((P, P), np.float32),
            "token_dft": token.astype(np.float32), "channel_dft": channel.astype(np.float32)}


INS = ["x_prompt", "x_sample", "c", "state_lru", "state_mlstm_C", "state_mlstm_n", "state_mlstm_m", "c_ctx", "w_mod",
       "b_mod", "g_pre", "g_post", "w_in_e", "conv_w", "conv_b", "w_rg", "b_rg", "w_ig", "b_ig", "lru_lambda",
       "w_four", "b_four", "w_out_e", "w_in_o", "b_if", "w_out_o"]
OUTS = [("y_prompt", (1, NCTX, D)), ("y_sample", (1, NLAT, D)), ("new_lru", (1, 1, 2, D)),
        ("new_C", (1, 1, 2, H, 128, 256)), ("new_n", (1, 1, 2, H, 128)), ("new_m", (1, 1, 2, H))]


def kernel(**inputs):
    import concourse.bacc as bacc
    from concourse.bass_utils import run_bass_kernel_spmd

    nc = bacc.Bacc("TRN2", target_bir_lowering=False, num_devices=1)
    arrays = {n: np.ascontiguousarray(inputs[n]) for n in INS} | consts()
    arrays = {f"in_{n}": x for n, x in arrays.items()}
    a = {n[3:]: nc.dram_tensor(n, x.shape, mybir.dt.from_np(x.dtype), kind="ExternalInput").ap()
         for n, x in arrays.items()}
    out = {n: nc.dram_tensor(n, shape, F32, kind="ExternalOutput").ap() for n, shape in OUTS}
    build(nc, a, out)
    r = run_bass_kernel_spmd(nc, [arrays], core_ids=[0])
    return tuple(r.results[0][n] for n, _ in OUTS)
```

```python
import numpy as np

import concourse.bass as bass
from concourse import mybir

F32, F32R = mybir.dt.float32, mybir.dt.float32r
ALU = mybir.AluOpType
ACT = mybir.ActivationFunctionType
ds = bass.ds

P = 128
D = 1024
KC = D // P
NCTX, NLAT = 128, 1024
T = NCTX + NLAT
NT = T // P
NJ, JW = 3, T // 3
H = 8
EPS = 1e-6
GAP = 3
TP = T + GAP
JP = TP // 3
LAT = NCTX + GAP
FFT_A = NLAT // P
TAP, CB, HBR, HBI, NEG, POS, H0 = 0, 4, 5, 6, 7, 8, 9
NPRM = 15


class Chain:

    def __init__(self, eng, sem, base=0):
        self.eng, self.sem, self.base, self.n = eng, sem, base, 0

    def link(self, ins):
        ins.then_inc(self.sem, 1)
        self.n += 1
        self.eng.wait_ge(self.sem, self.base + self.n)


def build(nc, a, out):
    sem = nc.alloc_semaphore
    bottom = [(nc.sbuf_base + 31) // 32 * 32]

    def sb(name, shape, dt=F32, at=None):
        at = bottom if at is None else at
        t = nc.alloc_sbuf_tensor_at(name, list(shape), dt, offset=at[0])
        at[0] += (int(np.prod(shape[1:])) * 4 + 31) // 32 * 32
        assert at[0] <= nc.sbuf_usable_end, (name, at[0])
        return t

    HHI = sb("h_hi", [P, KC, T], F32R)
    HLO = sb("h_lo", [P, KC, T], F32R)
    WRAW = sb("w_raw", [P, 2, KC * P])
    WHI = sb("w_hi", [P, 2, KC * P], F32R)
    WLO = sb("w_lo", [P, 2, KC * P], F32R)
    IDENT = sb("ident", [P, P])
    ONES = sb("ones", [P, P])
    AM = sb("mod_scale", [P, 2, KC, 2])
    SH = sb("mod_shift", [P, 2, KC, 2])
    GP = sb("mod_gate", [P, 2, KC, 2])
    SC = sb("cond_silu", [P, 2, KC])
    BM = sb("b_mod", [P, 2, 24])
    GN = sb("norm_gains", [P, 2, 2, KC])
    ZERO = sb("zeros", [P, 32])
    zone = bottom[0]
    PS = nc.alloc_psum_tensor("psum_groups", [P, 2, 3, 512], F32)
    PX = nc.alloc_psum_tensor("psum_extra", [P, 2, 512], F32)
    y_dram = nc.dram_tensor("y_scratch", (16, P, T), F32).ap()
    x_dram = nc.dram_tensor("x_scratch", (KC, P, T), F32).ap()

    SEGS = ((0, NCTX, 1), (NCTX, T, 0))

    w_loaded = [sem("w_loaded_0"), sem("w_loaded_1")]
    w_hi, w_lo, w_used = sem("w_hi_ready"), sem("w_lo_ready"), sem("w_used")

    def w_load(sp, pair, slot, src):
        if not isinstance(pair, int) or pair >= 1:
            sp.wait_ge(w_lo, pair * 2 + slot - 1)
        sp.dma_start(WRAW[:, slot, :].rearrange("p (k n) -> p k n", k=src.shape[1]), src).then_inc(w_loaded[slot], 16)

    def w_split_hi(act, pair, slot):
        act.wait_ge(w_loaded[slot], (pair + 1) * 16)
        if not isinstance(pair, int) or pair >= 1:
            act.wait_ge(w_used, pair * 2 + slot - 1)
        act.activation(WHI[:, slot, :], WRAW[:, slot, :], ACT.Copy).then_inc(w_hi, 1)

    def w_split_lo(dve, pair, slot):
        dve.wait_ge(w_hi, pair * 2 + slot + 1)
        dve.tensor_tensor(WLO[:, slot, :], WRAW[:, slot, :], WHI[:, slot, :].bitcast(F32), ALU.subtract).then_inc(w_lo, 1)

    def in_tile(w, col):
        return w.rearrange("(k p) n -> p k n", p=P)[:, :, ds(col, P)]

    def project(pe, pair, slot, group, hi, lo, k0=0, start=True, stop=True, ready=None, middle=None):
        pe.wait_ge(w_lo, pair * 2 + slot + 1)
        for k in range(KC):
            if ready:
                ready(k0 + k)
            if middle and k == KC // 2:
                middle()
            for m, (w, h) in enumerate(((WHI, hi), (WHI, lo), (WLO, hi))):
                for j in range(NJ):
                    ins = pe.matmul(PS[:, group, j, 0:JW], w[:, slot, k * P:(k + 1) * P],
                                    h(k0 + k)[:, j * JW:(j + 1) * JW],
                                    start=start and k == 0 and m == 0, stop=stop and k == KC - 1 and m == 2)
        ins.then_inc(w_used, 1)

    def projected(eng, pair, slot):
        eng.wait_ge(w_used, pair * 2 + slot + 1)

    def out_tile(w, half, col):
        return w.rearrange("(h k p) n -> h p k n", h=2, p=P)[half][:, :, ds(col, P)]

    hhi, hlo = (lambda k: HHI[:, k, :]), (lambda k: HLO[:, k, :])

    def by_bank(ap, w=JW):
        return ap.rearrange("p (j n) -> p j n", n=w)

    norm_zone = [zone]
    XT = sb("xT", [P, KC, T], at=norm_zone)
    TMP = sb("norm_tmp", [P, 2, T], at=norm_zone)
    SQ = sb("squares", [P, 2, T], at=norm_zone)
    RSTD = sb("rstd_rows", [96, JW], at=norm_zone)
    sq_ready, sq_used = sem("squares_ready"), sem("squares_summed")
    var_ready, std_ready = sem("variance_ready"), sem("std_ready")
    rstd_ready, rstd_spread = sem("rstd_ready"), sem("rstd_spread")

    def stats_act(act, n, x_of, SQ, x_ready=None):
        for k in range(KC):
            if x_ready:
                act.wait_ge(x_ready, k + 1)
            if k >= 2 or n:
                act.wait_ge(sq_used, KC * n + k - 1)
            act.activation(SQ[:, k % 2, :], x_of(k), ACT.Square).then_inc(sq_ready, 1)
        act.wait_ge(var_ready, n + 1)
        act.activation(RSTD[:], RSTD[:], ACT.Sqrt).then_inc(std_ready, 1)

    def stats_pe(pe, n, SQ, group=0):
        for k in range(KC):
            pe.wait_ge(sq_ready, KC * n + k + 1)
            for j in range(NJ):
                ins = pe.matmul(PX[32 * j:32 * j + 32, 1, 0:JW], ONES[:, 0:32], SQ[:, k % 2, j * JW:(j + 1) * JW],
                                start=k == 0, stop=k == KC - 1)
            ins.then_inc(sq_used, 1)
        pe.wait_ge(rstd_ready, n + 1)
        for j in range(NJ):
            ins = pe.matmul(PS[:, group, j, 0:JW], ONES[32 * j:32 * j + 1, :], RSTD[32 * j:32 * j + 1, :],
                            start=True, stop=True)
        ins.then_inc(rstd_spread, 1)

    def stats_dve(dve, n):
        dve.wait_ge(sq_used, KC * (n + 1))
        dve.tensor_scalar(RSTD[:], PX[0:96, 1, 0:JW], 1.0 / D, EPS, ALU.mult, ALU.add).then_inc(var_ready, 1)
        dve.wait_ge(std_ready, n + 1)
        dve.reciprocal(RSTD[:], RSTD[:]).then_inc(rstd_ready, 1)

    normed, modulated, h_hi, h_lo = sem("x_normed"), sem("h_modulated"), sem("h_hi_ready"), sem("h_lo_ready")

    def modulate(eng, out, x, l, k, c):
        return eng.activation(out, x, ACT.Identity, scale=AM[:, l, k, c:c + 1], bias=SH[:, l, k, c:c + 1])

    def h_dve(dve, l, x_of, TMP):
        dve.wait_ge(rstd_spread, 2 * l + 1)
        for k in range(KC + 1):
            if k < KC:
                if k >= 2:
                    dve.wait_ge(h_lo, KC * l + k - 1)
                dve.tensor_tensor(by_bank(TMP[:, k % 2, :]), by_bank(x_of(k)), PS[:, 0, :, 0:JW],
                                  ALU.mult).then_inc(normed, 1)
            if k:
                dve.wait_ge(h_hi, KC * l + k)
                dve.tensor_tensor(HLO[:, k - 1, :], TMP[:, (k - 1) % 2, :], HHI[:, k - 1, :].bitcast(F32),
                                  ALU.subtract).then_inc(h_lo, 1)

    def h_act(act, l, TMP):
        for k in range(KC):
            act.wait_ge(normed, KC * l + k + 1)
            for t0, t1, c in SEGS:
                modulate(act, TMP[:, k % 2, t0:t1], TMP[:, k % 2, t0:t1], l, k, c).then_inc(modulated, 1)
            act.wait_ge(modulated, 2 * (KC * l + k + 1))
            act.activation(HHI[:, k, :], TMP[:, k % 2, :], ACT.Copy).then_inc(h_hi, 1)

    def setup():
        z = list(norm_zone)
        XS, WS = 4, 4
        XR = sb("x_rows", [P, XS, D], at=z)
        WM = sb("w_mod_rows", [P, WS, 2 * D], at=z)
        CD = sb("cond", [P, 2, KC], at=z)
        MD = sb("mod", [P, 16, 2], at=z)
        const_in, cond_in, gains_in = sem("const_loaded"), sem("cond_loaded"), sem("gains_loaded")
        x_in = [sem(f"x_loaded_{n}") for n in range(XS)]
        wm_in = [sem(f"w_mod_loaded_{n}") for n in range(WS)]
        x_turned, xT_dve, xT_act, x_spilled = (sem(s) for s in ("x_turned", "xT_by_dve", "xT_by_act", "x_spilled"))
        cond_tanh, cond_ready, zero_ready = sem("cond_tanh"), sem("cond_ready"), sem("zeros_ready")
        mod_done, mod_ready, wm_used = sem("mod_summed"), sem("mod_ready"), sem("w_mod_used")
        dve_chain = sem("setup_dve_chain")
        wm_src = a["w_mod"][0].rearrange("(k p) n -> k p n", p=P)
        block = nc.Block()
        block.__enter__()

        @block.sync
        def _(sp):
            def x_rows(t):
                if t >= XS:
                    sp.wait_ge(x_turned, t - XS + 1)
                src = a["x_prompt"][0] if t == 0 else a["x_sample"][0, (t - 1) * P:t * P, :]
                sp.dma_start(XR[:, t % XS, :], src).then_inc(x_in[t % XS], 16)

            sp.dma_start(IDENT[:], a["ident"]).then_inc(const_in, 16)
            for t in range(NT):
                x_rows(t)
            for n in range(KC):
                if n >= WS:
                    sp.wait_ge(wm_used, n - WS + 1)
                sp.dma_start(WM[:, n % WS, :], wm_src[n][:, 0:2 * D]).then_inc(wm_in[n % WS], 16)
            for n in range(2):
                w_load(sp, 0, n, in_tile(a["w_in_e"][0], n * D))
            sp.wait_ge(x_spilled, 16)

        @block.gpsimd
        def _(pool):
            pool.memset(ZERO[:], 0.0).then_inc(zero_ready, 1)

        @block.tensor
        def _(pe):
            pe.wait_ge(const_in, 16)
            for t in range(NT):
                pe.wait_ge(x_in[t % XS], 16 * (t // XS + 1))
                if t >= 2:
                    pe.wait_ge(xT_act if t % 2 else xT_dve, t // 2)
                for k in range(KC):
                    ins = pe.transpose(PS[:, t % 2, k // 4, (k % 4) * P:(k % 4 + 1) * P],
                                       XR[:, t % XS, k * P:(k + 1) * P], IDENT[:])
                ins.then_inc(x_turned, 1)
            pe.wait_ge(const_in, 32)
            stats_pe(pe, 0, SQ, group=1)
            pe.wait_ge(zero_ready, 1)
            pe.wait_ge(cond_ready, 1)
            pe.matmul(PX[:, 0, 0:32], ONES[:], ZERO[:], start=True, stop=False, skip_group_check=True)
            for k in range(KC):
                pe.wait_ge(wm_in[k % WS], 16 * (k // WS + 1))
                for j in range(16):
                    ins = pe.matmul(PX[:, 0, 2 * j:2 * j + 2], WM[:, k % WS, j * P:(j + 1) * P], SC[:, :, k],
                                    start=False, stop=k == KC - 1, skip_group_check=True)
                ins.then_inc(wm_used, 1)
            pe.wait_ge(wm_used, KC)
            pe.sem_inc(mod_done, 1)
            project(pe, 0, 0, 0, hhi, hlo, ready=lambda k: pe.wait_ge(h_lo, k + 1))

        @block.scalar
        def _(act):
            with nc.allow_non_contiguous_dma("vectors, one element per partition"):
                act.dma_start(CD[:, 0, :], a["c"].rearrange("b (k p) -> p (b k)", p=P)).then_inc(cond_in, 16)
                act.dma_start(CD[:, 1, :], a["c_ctx"].rearrange("(k p) -> p k", p=P)).then_inc(cond_in, 16)
                act.dma_start(ONES[:], a["ones"]).then_inc(const_in, 16)
                for l in range(2):
                    act.dma_start(BM[:, l, :], a["b_mod"][l].rearrange("(j p) -> p j", p=P)).then_inc(gains_in, 16)
                    act.dma_start(GN[:, 0, l, :], a["g_pre"][l].rearrange("(k p) -> p k", p=P)).then_inc(gains_in, 16)
                    act.dma_start(GN[:, 1, l, :], a["g_post"][l].rearrange("(k p) -> p k", p=P)).then_inc(gains_in, 16)
            act.wait_ge(cond_in, 32)
            act.activation(SC[:], CD[:], ACT.Tanh, scale=0.5).then_inc(cond_tanh, 1)
            for t in range(1, NT, 2):
                act.wait_ge(x_turned, t + 1)
                act.activation(XT[:, :, t * P:(t + 1) * P],
                               PS[:, 1, 0:2, :].rearrange("p b (k n) -> p (b k) n", n=P), ACT.Copy).then_inc(xT_act, 1)
            act.wait_ge(xT_act, 4)
            act.wait_ge(xT_dve, 5)
            act.dma_start(x_dram.rearrange("k p t -> p k t"), XT[:]).then_inc(x_spilled, 16)
            stats_act(act, 0, lambda k: XT[:, k, :], SQ)
            w_split_hi(act, 0, 0)
            act.wait_ge(mod_ready, 1)
            for k in range(KC):
                act.wait_ge(normed, k + 1)
                if k >= 2:
                    act.wait_ge(h_lo, k - 1)
                for t0, t1, c in SEGS:
                    modulate(act, TMP[:, k % 2, t0:t1], XT[:, k, t0:t1], 0, k, c).then_inc(modulated, 1)
                act.wait_ge(modulated, 2 * (k + 1))
                act.activation(HHI[:, k, :], TMP[:, k % 2, :], ACT.Copy).then_inc(h_hi, 1)

        @block.vector
        def _(dve):
            ch = Chain(dve, dve_chain)
            dve.wait_ge(cond_tanh, 1)
            ch.link(dve.scalar_tensor_tensor(SC[:], SC[:], 1.0, CD[:], ALU.add, ALU.mult))
            dve.tensor_scalar(SC[:], SC[:], 0.5, None, ALU.mult).then_inc(cond_ready, 1)
            for t in range(0, NT, 2):
                dve.wait_ge(x_turned, t + 1)
                dve.tensor_copy(XT[:, :, t * P:(t + 1) * P],
                                PS[:, 0, 0:2, :].rearrange("p b (k n) -> p (b k) n", n=P)).then_inc(xT_dve, 1)
            stats_dve(dve, 0)
            w_split_lo(dve, 0, 0)
            dve.wait_ge(rstd_spread, 1)
            dve.wait_ge(xT_act, 4)
            dve.wait_ge(xT_dve, 5)
            dve.wait_ge(x_spilled, 16)
            for k in range(KC):
                dve.tensor_tensor(by_bank(XT[:, k, :]), by_bank(XT[:, k, :]), PS[:, 1, :, 0:JW], ALU.mult).then_inc(normed, 1)
            dve.wait_ge(mod_done, 1)
            dve.wait_ge(gains_in, 16 * 6)
            ch.link(dve.tensor_tensor(MD[:], PX[:, 0, 0:32].rearrange("p (j c) -> p j c", c=2),
                                      BM[:, 0, 0:16].unsqueeze(2).to_broadcast([P, 16, 2]), ALU.add))
            dve.tensor_copy(SH[:, 0], MD[:, 0:8, :])
            ch.link(dve.tensor_scalar(AM[:, 0], MD[:, 8:16, :], 1.0, None, ALU.add))
            dve.tensor_tensor(AM[:, 0], AM[:, 0], GN[:, 0, 0, :].unsqueeze(2).to_broadcast([P, 8, 2]),
                              ALU.mult).then_inc(mod_ready, 1)
            for k in range(KC):
                dve.wait_ge(h_hi, k + 1)
                dve.tensor_tensor(HLO[:, k, :], TMP[:, k % 2, :], HHI[:, k, :].bitcast(F32), ALU.subtract).then_inc(h_lo, 1)

        block.__exit__(None, None, None)


    def log1p(dve, ch, E, S, S2):
        ch.link(dve.tensor_scalar(S, E, 2.0, None, ALU.add))
        ch.link(dve.reciprocal(S, S))
        ch.link(dve.tensor_tensor(S, S, E, ALU.mult))
        ch.link(dve.tensor_tensor(S2, S, S, ALU.mult))
        ch.link(dve.tensor_scalar(E, S2, 1.0 / 17, None, ALU.mult))
        for m in range(7, 0, -1):
            ch.link(dve.scalar_tensor_tensor(E, E, 1.0 / (2 * m + 1), S2, ALU.add, ALU.mult))
        ch.link(dve.scalar_tensor_tensor(E, E, 1.0, S, ALU.add, ALU.mult))
        ch.link(dve.tensor_scalar(S, E, 2.0, None, ALU.mult))

    def lru():
        z = [zone]
        PRM = sb("lru_params", [P, KC, NPRM], at=z)
        LAM = sb("lru_lambda", [P, 2, KC], at=z)
        LT = sb("lru_softplus", [P, 3, 2 * KC], at=z)
        GW = sb("gate_weights", [P, 4, P], at=z)
        XA = sb("xa_padded", [P, TP + 3], at=z)
        XC = sb("xa_convolved", [P, TP], at=z)
        GZ = sb("za_silu", [P, T], at=z)
        ZH = sb("za_half", [P, T], at=z)
        T1 = sb("gate_r", [P, 2, TP], at=z)
        T2 = sb("gate_i", [P, 2, TP], at=z)
        A = sb("decay", [P, 2, TP], at=z)
        HT = sb("tanh_then_state", [P, 2, TP], at=z)
        YT = sb("lru_y", [P, T], at=z)
        FIN = sb("lru_final", [P, 2, KC], at=z)
        prm_in, gw_in = sem("lru_params_loaded"), sem("gate_weights_loaded")
        mm = sem("lru_products")
        r_out, i_out, z_out, x_out = sem("r_evacuated"), sem("i_evacuated"), sem("za_evacuated"), sem("xa_evacuated")
        pads, conv, gated, squared, var1, root, y_ready, y_out = (sem(s) for s in (
            "pads_zero", "xa_conv_ready", "za_tanh_ready", "decay_ready", "one_minus_a2_ready", "root_ready",
            "lru_y_ready", "lru_y_stored"))
        lam_exp, prm_ready, fin_out = sem("lambda_exp"), sem("lru_params_ready"), sem("lru_final_stored")
        r_tanh = sem("gate_r_read")
        dve_chain = sem("lru_dve_chain")
        s_in = [sem("lru_lam_abs")]
        block = nc.Block()
        block.__enter__()

        @block.gpsimd
        def _(pool):
            def gate_weights(i):
                for n, w in enumerate((a["w_rg"], a["w_ig"])):
                    pool.dma_start(GW[:, 2 * n:2 * n + 2, :], w[0][:, ds(i, 1)].rearrange("d a p n -> p (d a) n")
                                   ).then_inc(gw_in, 16)

            def store_y(i):
                pool.wait_ge(y_ready, i + 1)
                pool.dma_start(y_dram[ds(i, 1)].rearrange("a p t -> p (a t)"), YT[:]).then_inc(y_out, 16)

            gate_weights(0)
            with pool.Fori(0, KC - 1) as i:
                pool.wait_ge(mm, i * 4 + 4)
                gate_weights(i + 1)
                store_y(i)
            store_y(KC - 1)
            pool.wait_ge(y_out, 16 * KC)

        @block.sync
        def _(sp):
            with nc.allow_non_contiguous_dma("vectors, one element per partition"):
                by_channel = "(k p) -> p k"
                for j in range(4):
                    sp.dma_start(PRM[:, :, TAP + j], a["conv_w"][0, j].rearrange(by_channel, p=P)).then_inc(prm_in, 16)
                sp.dma_start(PRM[:, :, CB], a["conv_b"][0].rearrange(by_channel, p=P)).then_inc(prm_in, 16)
                for d in range(2):
                    for col, src in ((HBR, a["b_rg"][0, d]), (HBI, a["b_ig"][0, d]), (H0, a["state_lru"][0, 0, d])):
                        sp.dma_start(PRM[:, :, 5 * d + col], src.rearrange(by_channel, p=P)).then_inc(prm_in, 16)
                    sp.dma_start(LAM[:, d, :], a["lru_lambda"][0, d].rearrange(by_channel, p=P)).then_inc(prm_in, 16)
            with sp.Fori(0, KC - 1) as i:
                w_load(sp, i + 1, 0, in_tile(a["w_in_e"][0], i * P + P))
                w_load(sp, i + 1, 1, in_tile(a["w_in_e"][0], i * P + P + D))
            for slot in range(2):
                w_load(sp, KC, slot, in_tile(a["w_in_e"][0], (2 + slot) * D))
            sp.wait_ge(y_ready, KC)
            with nc.allow_non_contiguous_dma("final states, one element per partition"):
                for d in range(2):
                    sp.dma_start(out["new_lru"][0, 0, d].rearrange("(k p) -> p k", p=P), FIN[:, d, :]).then_inc(fin_out, 16)
            sp.wait_ge(fin_out, 32)

        @block.tensor
        def _(pe):
            def block_of(i, first):
                if not first:
                    pe.wait_ge(r_out, i * 2)
                    project(pe, i, 0, 0, hhi, hlo)
                    pe.wait_ge(i_out, i * 2)
                project(pe, i, 1, 1, hhi, hlo)
                pe.wait_ge(gw_in, i * 32 + 32)
                pe.wait_ge(conv, i + 1)
                for d in range(2):
                    for what in range(2):
                        if what == 0:
                            pe.wait_ge(*((r_out, i * 2 + 1) if d else (x_out, i + 1)))
                        else:
                            pe.wait_ge(*((i_out, i * 2 + 1) if d else (z_out, i + 1)))
                        for j in range(NJ):
                            ins = pe.matmul(PS[:, what, j, 0:JP], GW[:, 2 * what + d, :], XC[:, j * JP:(j + 1) * JP],
                                            start=True, stop=True)
                        ins.then_inc(mm, 1)

            block_of(0, True)
            with pe.Fori(1, KC) as i:
                block_of(i, False)

        def prm(i, col):
            return PRM[:, ds(i, 1), col]

        @block.scalar
        def _(act):
            w_split_hi(act, 0, 1)
            act.wait_ge(prm_in, 16 * 13)
            act.activation(LT[:, 0, :], LAM[:].rearrange("p d k -> p (d k)"), ACT.Abs).then_inc(s_in[0], 1)
            act.wait_ge(s_in[0], 1)
            act.activation(LT[:, 0, :], LT[:, 0, :], ACT.Exp, scale=-1.0).then_inc(lam_exp, 1)
            act.wait_ge(pads, 1)
            act.wait_ge(prm_ready, 1)
            def block_of(i, first):
                projected(act, i, 0)
                if not first:
                    act.wait_ge(conv, i)
                act.activation(XA[:, 2:2 + NCTX], PS[:, 0, 0, 0:NCTX], ACT.Copy)
                act.activation(XA[:, 2 + LAT:2 + JW + GAP], PS[:, 0, 0, NCTX:JW], ACT.Copy)
                act.activation(by_bank(XA[:, 2 + JW + GAP:2 + TP]), PS[:, 0, 1:3, 0:JW], ACT.Copy).then_inc(x_out, 1)
                w_split_hi(act, i + 1, 0)
                projected(act, i, 1)
                if not first:
                    act.wait_ge(y_ready, i)
                act.activation(by_bank(GZ[:]), PS[:, 1, :, 0:JW], ACT.Tanh, scale=0.5)
                act.activation(by_bank(ZH[:]), PS[:, 1, :, 0:JW], ACT.Copy, scale=0.5).then_inc(z_out, 1)
                for d in range(2):
                    act.wait_ge(mm, i * 4 + 1 + 2 * d)
                    act.activation(by_bank(T1[:, d, :], JP), PS[:, 0, :, 0:JP], ACT.Tanh, scale=0.5,
                                   bias=prm(i, HBR + 5 * d)).then_inc(r_out, 1)
                    act.wait_ge(mm, i * 4 + 2 + 2 * d)
                    act.activation(by_bank(T2[:, d, :], JP), PS[:, 1, :, 0:JP], ACT.Tanh, scale=0.5,
                                   bias=prm(i, HBI + 5 * d)).then_inc(i_out, 1)
                    act.wait_ge(r_out, i * 2 + 1 + d)
                    act.activation(A[:, d, :], T1[:, d, :], ACT.Exp, scale=prm(i, NEG + 5 * d),
                                   bias=prm(i, NEG + 5 * d)).then_inc(r_tanh, 1)
                    act.activation(HT[:, d, :], T1[:, d, :], ACT.Tanh, scale=prm(i, POS + 5 * d),
                                   bias=prm(i, POS + 5 * d)).then_inc(r_tanh, 1)
                    act.wait_ge(r_tanh, i * 4 + 2 + 2 * d)
                    act.activation(T1[:, d, :], A[:, d, :], ACT.Square).then_inc(squared, 1)
                w_split_hi(act, i + 1, 1)
                for d in range(2):
                    act.wait_ge(var1, i * 2 + 1 + d)
                    act.activation(T1[:, d, :], T1[:, d, :], ACT.Sqrt, scale=0.25).then_inc(root, 1)

            block_of(0, True)
            with act.Fori(1, KC) as i:
                block_of(i, False)

        @block.vector
        def _(dve):
            ch = Chain(dve, dve_chain)
            dve.memset(XA[:], 0.0).then_inc(pads, 1)
            w_split_lo(dve, 0, 1)
            dve.wait_ge(prm_in, 16 * 13)
            dve.wait_ge(lam_exp, 1)
            log1p(dve, ch, LT[:, 0, :], LT[:, 1, :], LT[:, 2, :])
            lam = LAM[:].rearrange("p d k -> p (d k)")
            ch.link(dve.tensor_scalar(LT[:, 0, :], lam, -1.0, 0.0, ALU.mult, ALU.max))
            ch.link(dve.tensor_tensor(LT[:, 1, :], LT[:, 0, :], LT[:, 1, :], ALU.add))
            for d in range(2):
                sp_d = LT[:, 1, KC * d:KC * d + KC]
                dve.tensor_scalar(PRM[:, :, NEG + 5 * d], sp_d, -4.0, None, ALU.mult)
                dve.tensor_scalar(PRM[:, :, POS + 5 * d], sp_d, 4.0, None, ALU.mult)
                for col in (HBR, HBI):
                    ins = dve.tensor_scalar(PRM[:, :, col + 5 * d], PRM[:, :, col + 5 * d], 0.5, None, ALU.mult)
            ins.then_inc(prm_ready, 1)
            dve.wait_ge(prm_ready, 1)
            before, LINKS = ch.n, 12

            def block_of(i, first):
                dve.wait_ge(x_out, i + 1)
                if not first:
                    dve.wait_ge(mm, i * 4)
                ch.link(dve.tensor_scalar(XC[:], XA[:, 0:TP], prm(i, TAP), prm(i, CB), ALU.mult, ALU.add))
                for j in range(1, 4):
                    ins = dve.scalar_tensor_tensor(XC[:], XA[:, j:j + TP], prm(i, TAP + j), XC[:], ALU.mult, ALU.add)
                    if j < 3:
                        ch.link(ins)
                ins.then_inc(conv, 1)
                w_split_lo(dve, i + 1, 0)
                dve.wait_ge(z_out, i + 1)
                ch.link(dve.scalar_tensor_tensor(GZ[:], GZ[:], 1.0, ZH[:], ALU.add, ALU.mult))
                dve.wait_ge(conv, i + 1)
                for d in range(2):
                    dve.wait_ge(i_out, i * 2 + 1 + d)
                    dve.scalar_tensor_tensor(T2[:, d, :], T2[:, d, :], 1.0, XC[:], ALU.add, ALU.mult)
                    dve.wait_ge(squared, i * 2 + 1 + d)
                    dve.scalar_tensor_tensor(T1[:, d, :], T1[:, d, :], 1.0, HT[:, d, :], ALU.add,
                                             ALU.mult).then_inc(var1, 1)
                w_split_lo(dve, i + 1, 1)
                for d in range(2):
                    dve.wait_ge(root, i * 2 + 1 + d)
                    ch.link(dve.tensor_tensor(T2[:, d, :], T2[:, d, :], T1[:, d, :], ALU.mult))
                    for t0, t1, h0 in ((0, NCTX, 0.0), (LAT, TP, prm(i, H0 + 5 * d))):
                        w = slice(t0, t1) if d == 0 else slice(t1 - 1, None if t0 == 0 else t0 - 1, -1)
                        ins = dve.tensor_tensor_scan(HT[:, d, w], A[:, d, w], T2[:, d, w], h0, op0=ALU.mult, op1=ALU.add)
                    ch.link(ins)
                    dve.tensor_copy(FIN[:, d, ds(i, 1)], HT[:, d, NCTX - 1:NCTX] if d == 0 else HT[:, d, 0:1])
                for n, (t0, t1, p0) in enumerate(((0, NCTX, 0), (NCTX, T, LAT))):
                    ch.link(dve.tensor_tensor(HT[:, 0, p0:p0 + t1 - t0], HT[:, 0, p0:p0 + t1 - t0],
                                              HT[:, 1, p0:p0 + t1 - t0], ALU.add))
                if not first:
                    dve.wait_ge(y_out, i * 16)
                ch.link(dve.tensor_tensor(YT[:, 0:NCTX], HT[:, 0, 0:NCTX], GZ[:, 0:NCTX], ALU.mult))
                ch.link(dve.tensor_tensor(YT[:, NCTX:T], HT[:, 0, LAT:TP], GZ[:, NCTX:T], ALU.mult))
                dve.sem_inc(y_ready, 1)

            block_of(0, True)
            assert ch.n == before + LINKS, ch.n - before
            with dve.Fori(1, KC) as i:
                ch.base, ch.n = before + i * LINKS, 0
                block_of(i, False)

        block.__exit__(None, None, None)

    def fourier():
        z = [zone]
        CH = sb("channel_dft", [P, 2, P], at=z)
        TB = sb("token_dft", [P, 8, 2, P], at=z)
        WF = sb("w_four", [P, 2, P], at=z)
        CW = sb("channel_weights", [P, 2, P], at=z)
        B4 = sb("b_four", [P, KC], at=z)
        XB = sb("xb", [P, T], at=z)
        GZ = sb("zb_silu", [P, T], at=z)
        ZH = sb("zb_half", [P, T], at=z)
        Z = sb("token_major", [P, NT, 2, P], at=z)
        S = sb("butterfly", [P, 2, 4, 2, P], at=z)
        M = sb("butterfly_mid", [P, 4, 2, P], at=z)
        TF = sb("transformed", [P, 8, 2, P], at=z)
        YT = sb("fourier_y", [P, T], at=z)
        WM = sb("w_mod_rest", [P, 4 * D], at=z)
        ACC = sb("mod_by_partition", [P, 2, 4 * D], at=z)
        MD = sb("mod_rest", [P, 32, 2], at=z)
        wm_in, mod_part, mod_done = sem("w_mod_rest_loaded"), sem("mod_rest_added"), sem("mod_rest_summed")
        table_in = sem("tables_loaded")
        wf_in = [sem("w_four_loaded_0"), sem("w_four_loaded_1")]
        cw_done, cw_out = sem("cw_product"), sem("cw_ready")
        f_done, ua_done, ub_done = sem("dft_product"), sem("ua_product"), sem("ub_product")
        xb_out, ua_out, ub_out, zb_out, y_ready, y_out = (sem(s) for s in (
            "xb_ready", "ua_ready", "ub_ready", "zb_ready", "fourier_y_ready", "fourier_y_stored"))
        tf_ready = sem("token_transform_ready")
        dve_chain = sem("fourier_dve_chain")
        half = 1.0 / np.sqrt(2.0)
        block = nc.Block()
        block.__enter__()

        @block.sync
        def _(sp):
            sp.dma_start(CH[:], a["channel_dft"]).then_inc(table_in, 16)
            sp.dma_start(TB[:], a["token_dft"]).then_inc(table_in, 16)
            with nc.allow_non_contiguous_dma("a vector, one element per partition"):
                sp.dma_start(B4[:], a["b_four"][0].rearrange("(k p) -> p k", p=P)).then_inc(table_in, 16)

            def w_mod_rows(k):
                for l, (c0, c1, at) in enumerate(((2 * D, 3 * D, 0), (0, 3 * D, D))):
                    sp.dma_start(WM[:, at:at + c1 - c0],
                                 a["w_mod"][l].rearrange("(k p) n -> k p n", p=P)[ds(k, 1), :, c0:c1].rearrange(
                                     "a p n -> p (a n)")).then_inc(wm_in, 16)

            w_mod_rows(0)
            with sp.Fori(0, KC - 1) as i:
                w_load(sp, i + KC + 1, 0, in_tile(a["w_in_e"][0], i * P + P + 2 * D))
                w_load(sp, i + KC + 1, 1, in_tile(a["w_in_e"][0], i * P + P + 3 * D))
                sp.wait_ge(mod_part, i * 2 + 2)
                w_mod_rows(i + 1)
            for slot in range(2):
                w_load(sp, 2 * KC, slot, out_tile(a["w_out_e"][0], slot, 0))

        @block.gpsimd
        def _(pool):
            for slot in range(2):
                pool.dma_start(WF[:, slot, :], a["w_four"][0, slot]).then_inc(wf_in[slot], 16)

            def store_y(i):
                pool.wait_ge(y_ready, i + 1)
                pool.dma_start(y_dram[ds(i + KC, 1)].rearrange("a p t -> p (a t)"), YT[:]).then_inc(y_out, 16)

            with pool.Fori(0, KC // 2 - 1) as m:
                for slot in range(2):
                    pool.wait_ge(cw_done, m * 2 + 1 + slot)
                    pool.dma_start(WF[:, slot, :], a["w_four"][0][ds(m * 2 + 2 + slot, 1)].rearrange("a p n -> p (a n)")
                                   ).then_inc(wf_in[slot], 16)
                    store_y(m * 2 + slot)
            store_y(KC - 2)
            store_y(KC - 1)
            pool.wait_ge(y_out, 16 * KC)

        @block.tensor
        def _(pe):
            pe.wait_ge(table_in, 48)

            def channel_weights(m, slot):
                pe.wait_ge(wf_in[slot], m * 16 + 16)
                pe.wait_ge(cw_out, m * 2 + slot)
                pe.wait_ge(ub_out, m * 2 + slot)
                for part in range(2):
                    ins = pe.matmul(PX[:, 1, 256 + part * P:256 + (part + 1) * P], CH[:, part, :], WF[:, slot, :],
                                    start=True, stop=True, skip_group_check=True)
                ins.then_inc(cw_done, 1)

            def to_tokens(first, last, bank, done):
                for t in range(first, last):
                    ins = pe.matmul(bank(t - first), XB[:, t * P:(t + 1) * P], CW[:].rearrange("p a n -> p (a n)"),
                                    start=True, stop=True, skip_group_check=True)
                ins.then_inc(done, 1)

            def token_transform(i):
                pe.wait_ge(tf_ready, i + 1)
                pe.wait_ge(zb_out, i + 1)
                for k1 in range(8):
                    for part in range(2):
                        pe.matmul(PS[:, 1, k1 // 4, (k1 % 4) * P:(k1 % 4 + 1) * P], TF[:, k1, part, :],
                                  TB[:, k1, part, :], start=part == 0, stop=part == 1, skip_group_check=True)
                for part in range(2):
                    ins = pe.matmul(PS[:, 1, 2, 0:P], Z[:, 0, part, :], TB[:, 0, part, :],
                                    start=part == 0, stop=part == 1)
                ins.then_inc(f_done, 1)

            def group(i, m, slot, first):
                channel_weights(m, slot)
                if not first:
                    pe.wait_ge(ua_out, i)
                project(pe, i + KC, 0, 0, hhi, hlo)
                if not first:
                    token_transform(i - 1)
                pe.wait_ge(xb_out, i + 1)
                pe.wait_ge(cw_out, m * 2 + slot + 1)
                if not first:
                    pe.wait_ge(ub_out, i)
                to_tokens(0, 6, lambda t: PS[:, 0, t // 2, t % 2 * 256:t % 2 * 256 + 256], ua_done)
                to_tokens(6, 9, lambda t: PX[:, t // 2, t % 2 * 256:t % 2 * 256 + 256], ub_done)
                if not first:
                    pe.wait_ge(y_ready, i)
                project(pe, i + KC, 1, 1, hhi, hlo)

            group(0, 0, 0, True)
            group(1, 0, 1, False)
            with pe.Fori(1, KC // 2) as m:
                for slot in range(2):
                    group(m * 2 + slot, m, slot, False)
            token_transform(KC - 1)
            pe.wait_ge(ua_out, KC)
            pe.wait_ge(mod_part, 2 * KC)
            for j in range(32):
                for c in range(2):
                    ins = pe.matmul(PS[:, 0, 0, 2 * j + c:2 * j + c + 1], ACC[:, c, j * P:(j + 1) * P], ONES[:, 0:1],
                                    start=True, stop=True, skip_group_check=True)
            ins.then_inc(mod_done, 1)

        @block.scalar
        def _(act):
            def group(i, first):
                if not first:
                    w_split_hi(act, i + KC, 1)
                act.wait_ge(cw_done, i + 1)
                if not first:
                    act.wait_ge(ub_done, i)
                act.activation(CW[:].rearrange("p a n -> p (a n)"), PX[:, 1, 256:512], ACT.Copy).then_inc(cw_out, 1)
                projected(act, i + KC, 0)
                act.activation(by_bank(XB[:]), PS[:, 0, :, 0:JW], ACT.Copy).then_inc(xb_out, 1)
                w_split_hi(act, i + KC + 1, 0)
                act.wait_ge(ua_done, i + 1)
                flat = PS[:, 0].rearrange("p b (t r n) -> p (b t) r n", t=2, r=2)
                act.activation(Z[:, 0], flat[:, 0], ACT.Copy, scale=float(np.sqrt(NLAT / NCTX)))
                act.activation(Z[:, 1:6], flat[:, 1:6], ACT.Copy).then_inc(ua_out, 1)
                act.wait_ge(ub_done, i + 1)
                act.activation(Z[:, 6:8], PX[:, 0, :].rearrange("p (t r n) -> p t r n", t=2, r=2), ACT.Copy)
                act.activation(Z[:, 8], PX[:, 1, 0:256].rearrange("p (r n) -> p r n", r=2), ACT.Copy).then_inc(ub_out, 1)
                projected(act, i + KC, 1)
                act.activation(by_bank(GZ[:]), PS[:, 1, :, 0:JW], ACT.Tanh, scale=0.5)
                act.activation(by_bank(ZH[:]), PS[:, 1, :, 0:JW], ACT.Copy, scale=0.5).then_inc(zb_out, 1)

            group(0, True)
            with act.Fori(1, KC) as i:
                group(i, False)

        @block.vector
        def _(dve):
            ch = Chain(dve, dve_chain)

            def tt(o, x, y, op):
                return dve.tensor_tensor(o, x, y, op)

            def eight_points(i):
                add, sub = ALU.add, ALU.subtract
                dve.wait_ge(ub_out, i + 1)
                tt(S[:, 0], Z[:, 1:5], Z[:, 5:9], add)
                ch.link(tt(S[:, 1], Z[:, 1:5], Z[:, 5:9], sub))
                odd = S[:, 1]
                tt(M[:, 0:2], S[:, 0, 0:2], S[:, 0, 2:4], add)
                ch.link(tt(M[:, 2:4], S[:, 0, 0:2], S[:, 0, 2:4], sub))
                tt(TF[:, 0], M[:, 0], M[:, 1], add)
                tt(TF[:, 4], M[:, 0], M[:, 1], sub)
                tt(TF[:, 2, 0], M[:, 2, 0], M[:, 3, 1], add)
                tt(TF[:, 2, 1], M[:, 2, 1], M[:, 3, 0], sub)
                tt(TF[:, 6, 0], M[:, 2, 0], M[:, 3, 1], sub)
                ch.link(tt(TF[:, 6, 1], M[:, 2, 1], M[:, 3, 0], add))
                ch.link(dve.tensor_scalar(odd[:, 1::2], odd[:, 1::2], float(half), None, ALU.mult))
                tt(S[:, 0, 0:2, 0], odd[:, 1::2, 0], odd[:, 1::2, 1], add)
                tt(S[:, 0, 0:2, 1], odd[:, 1::2, 1], odd[:, 1::2, 0], sub)
                tt(M[:, 0, 0], odd[:, 0, 0], odd[:, 2, 1], add)
                tt(M[:, 0, 1], odd[:, 0, 1], odd[:, 2, 0], sub)
                tt(M[:, 2, 0], odd[:, 0, 0], odd[:, 2, 1], sub)
                ch.link(tt(M[:, 2, 1], odd[:, 0, 1], odd[:, 2, 0], add))
                tt(M[:, 1, 0], S[:, 0, 0, 0], S[:, 0, 1, 1], add)
                tt(M[:, 1, 1], S[:, 0, 0, 1], S[:, 0, 1, 0], sub)
                tt(M[:, 3, 0], S[:, 0, 0, 0], S[:, 0, 1, 1], sub)
                ch.link(tt(M[:, 3, 1], S[:, 0, 0, 1], S[:, 0, 1, 0], add))
                tt(TF[:, 1], M[:, 0], M[:, 1], add)
                tt(TF[:, 5], M[:, 0], M[:, 1], sub)
                tt(TF[:, 3, 0], M[:, 2, 0], M[:, 3, 1], add)
                tt(TF[:, 3, 1], M[:, 2, 1], M[:, 3, 0], sub)
                tt(TF[:, 7, 0], M[:, 2, 0], M[:, 3, 1], sub)
                tt(TF[:, 7, 1], M[:, 2, 1], M[:, 3, 0], add).then_inc(tf_ready, 1)

            def add_modulation(i, c):
                dve.wait_ge(wm_in, i * 32 + 32)
                s = SC[:, c, ds(i, 1)]
                if isinstance(i, int) and i == 0:
                    dve.tensor_scalar(ACC[:, c], WM[:], s, None, ALU.mult).then_inc(mod_part, 1)
                else:
                    dve.wait_ge(mod_part, i * 2 - 1 + c)
                    dve.scalar_tensor_tensor(ACC[:, c], WM[:], s, ACC[:, c], ALU.mult, ALU.add).then_inc(mod_part, 1)

            def gate(i):
                dve.wait_ge(zb_out, i + 1)
                ch.link(dve.scalar_tensor_tensor(GZ[:], GZ[:], 1.0, ZH[:], ALU.add, ALU.mult))

            def outputs(i, first):
                dve.wait_ge(f_done, i + 1)
                if not first:
                    dve.wait_ge(y_out, i * 16)
                b4 = B4[:, ds(i, 1)]
                by_k1 = "p (k2 k1) -> p k1 k2"
                dve.scalar_tensor_tensor(YT[:, 0:NCTX], PS[:, 1, 2, 0:P], b4, GZ[:, 0:NCTX], ALU.add, ALU.mult)
                ch.link(dve.scalar_tensor_tensor(
                    YT[:, NCTX:T].rearrange(by_k1, k1=8), PS[:, 1, 0:2, :].rearrange("p b (k n) -> p (b k) n", n=P), b4,
                    GZ[:, NCTX:T].rearrange(by_k1, k1=8), ALU.add, ALU.mult))
                dve.sem_inc(y_ready, 1)

            def group(i):
                if not isinstance(i, int) or i:
                    w_split_lo(dve, i + KC, 1)
                if not isinstance(i, int) or i:
                    outputs(i - 1, isinstance(i, int))
                w_split_lo(dve, i + KC + 1, 0)
                add_modulation(i, 0)
                eight_points(i)
                gate(i)
                add_modulation(i, 1)

            dve.wait_ge(table_in, 48)
            group(0)
            before, LINKS = ch.n, 8
            group(1)
            assert ch.n == before + LINKS, ch.n - before
            with dve.Fori(2, KC) as i:
                ch.base, ch.n = before + (i - 1) * LINKS, 0
                group(i)
            ch.base, ch.n = before + (KC - 1) * LINKS, 0
            outputs(KC - 1, False)
            dve.wait_ge(mod_done, 1)
            mod = PS[:, 0, 0, 0:64].rearrange("p (j c) -> p j c", c=2)
            dve.tensor_tensor(MD[:, 0:8], mod[:, 0:8], BM[:, 0, 16:24].unsqueeze(2).to_broadcast([P, 8, 2]), ALU.add)
            ch.link(dve.tensor_tensor(MD[:, 8:32], mod[:, 8:32], BM[:, 1, :].unsqueeze(2).to_broadcast([P, 24, 2]), ALU.add))
            dve.tensor_copy(SH[:, 1], MD[:, 8:16, :])
            ch.link(dve.tensor_scalar(AM[:, 1], MD[:, 16:24, :], 1.0, None, ALU.add))
            dve.tensor_tensor(AM[:, 1], AM[:, 1], GN[:, 0, 1, :].unsqueeze(2).to_broadcast([P, 8, 2]), ALU.mult)
            for l, at in ((0, 0), (1, 24)):
                dve.tensor_tensor(GP[:, l], MD[:, at:at + 8, :], GN[:, 1, l, :].unsqueeze(2).to_broadcast([P, 8, 2]), ALU.mult)

        block.__exit__(None, None, None)

    def outputs(l, w_out, pair0, next_tiles):
        z = [zone]
        YHI = sb(f"y_hi_{l}", [P, 2 * KC, T], F32R, at=z)
        OUT = sb(f"out_{l}", [P, KC, T], at=z)
        z = list(norm_zone)
        ROWS = sb(f"out_rows_{l}", [P, 2, D], at=z)
        y_in = [sem(f"y_loaded_{l}_{q}") for q in range(4)]
        y_hi, y_lo, out_ready = sem(f"y_hi_ready_{l}"), sem(f"y_lo_ready_{l}"), sem(f"out_ready_{l}")
        x_in, scaled, x_ready, x_out = (sem(f"{s}_{l}") for s in ("residual_loaded", "out_normed", "x_ready", "x_stored"))
        sq_free, turned = sem(f"stats_read_{l}"), sem(f"rows_turned_{l}")
        rows_dve, rows_act = sem(f"rows_by_dve_{l}"), sem(f"rows_by_act_{l}")
        row_out = [sem(f"rows_stored_{l}_0"), sem(f"rows_stored_{l}_1")]
        last = pair0 + KC
        block = nc.Block()
        block.__enter__()

        def ylo(k):
            return (HHI if k < KC else HLO)[:, k % KC, :]

        @block.sync
        def _(sp):
            for q in range(4):
                dst = (HHI if q < 2 else HLO)[:, 4 * (q % 2):4 * (q % 2) + 4, :].bitcast(F32)
                sp.dma_start(dst, y_dram[4 * q:4 * q + 4].rearrange("k p t -> p k t")).then_inc(y_in[q], 16)
            with sp.Fori(0, KC - 1) as o:
                for half in range(2):
                    w_load(sp, o + pair0 + 1, half, out_tile(w_out, half, o * P + P))
            if next_tiles:
                for slot in range(2):
                    w_load(sp, last, slot, next_tiles[slot])
            projected(sp, last - 1, 1)
            sp.dma_start(XT[:], x_dram.rearrange("k p t -> p k t")).then_inc(x_in, 16)
            if l == 0:
                sp.wait_ge(x_ready, KC)
                sp.dma_start(x_dram.rearrange("k p t -> p k t"), XT[:]).then_inc(x_out, 16)
                sp.wait_ge(x_out, 16)
            else:
                for t in range(NT):
                    sp.wait_ge(rows_act if t % 2 else rows_dve, t // 2 + 1)
                    dst = out["y_prompt"][0] if t == 0 else out["y_sample"][0, (t - 1) * P:t * P, :]
                    sp.dma_start(dst, ROWS[:, t % 2, :]).then_inc(row_out[t % 2], 16)
                sp.wait_ge(row_out[0], 16 * 5)
                sp.wait_ge(row_out[1], 16 * 4)

        @block.tensor
        def _(pe):
            def out_block(o, group, free, ready=None):
                if free is not None:
                    pe.wait_ge(out_ready, free)
                for half in range(2):
                    project(pe, o + pair0, half, group, lambda k: YHI[:, k, :], ylo, k0=half * KC,
                            start=half == 0, stop=half == 1, ready=ready)

            out_block(0, 0, None, lambda k: pe.wait_ge(y_lo, k + 1))
            out_block(1, 1, None)
            with pe.Fori(1, KC // 2) as m:
                for b in range(2):
                    out_block(m * 2 + b, b, m * 2 + b - 1)
            stats_pe(pe, 2 * l + 1, SQ)
            if l == 0:
                stats_pe(pe, 2, SQ)
            else:
                for t in range(NT):
                    if t == 0:
                        pe.wait_ge(x_ready, KC)
                    else:
                        if t >= 2:
                            pe.wait_ge(rows_act if t % 2 else rows_dve, t // 2)
                    for k in range(KC):
                        ins = pe.transpose(PS[:, t % 2, k // 4, (k % 4) * P:(k % 4 + 1) * P],
                                           XT[:, k, t * P:(t + 1) * P], IDENT[:])
                    ins.then_inc(turned, 1)

        @block.scalar
        def _(act):
            for k in range(2 * KC):
                if k % 4 == 0:
                    act.wait_ge(y_in[k // 4], 16)
                act.activation(YHI[:, k, :], ylo(k).bitcast(F32), ACT.Copy).then_inc(y_hi, 1)
                if k == 3:
                    w_split_hi(act, pair0, 1)

            def evacuate(o, group):
                projected(act, o + pair0, 1)
                act.activation(OUT[:, ds(o, 1), :].rearrange("p a (j n) -> p (a j) n", n=JW), PS[:, group, :, 0:JW],
                               ACT.Copy).then_inc(out_ready, 1)

            def out_block(o, group):
                w_split_hi(act, o + pair0 + 1, 0)
                w_split_hi(act, o + pair0 + 1, 1)
                evacuate(o, group)

            with act.Fori(0, KC // 2 - 1) as m:
                for b in range(2):
                    out_block(m * 2 + b, b)
            out_block(KC - 2, 0)
            if next_tiles:
                w_split_hi(act, last, 0)
            evacuate(KC - 1, 1)
            act.wait_ge(out_ready, KC)
            stats_act(act, 2 * l + 1, lambda k: OUT[:, k, :], SQ)
            if l == 0:
                stats_act(act, 2, lambda k: XT[:, k, :], SQ, x_ready)
                h_act(act, 1, TMP)
            else:
                for t in range(1, NT, 2):
                    act.wait_ge(turned, t + 1)
                    if t >= 3:
                        act.wait_ge(row_out[1], 16 * (t // 2))
                    act.activation(ROWS[:, 1, :], PS[:, 1, 0:2, :].rearrange("p b n -> p (b n)"),
                                   ACT.Copy).then_inc(rows_act, 1)

        @block.vector
        def _(dve):
            for k in range(2 * KC):
                dve.wait_ge(y_hi, k + 1)
                dve.tensor_tensor(ylo(k), ylo(k).bitcast(F32), YHI[:, k, :].bitcast(F32), ALU.subtract).then_inc(y_lo, 1)
                if k == 3:
                    w_split_lo(dve, pair0, 1)
            with dve.Fori(0, KC - 1) as o:
                for half in range(2):
                    w_split_lo(dve, o + pair0 + 1, half)
            if next_tiles:
                w_split_lo(dve, last, 0)
            stats_dve(dve, 2 * l + 1)
            dve.wait_ge(rstd_spread, 2 * l + 2)
            dve.wait_ge(x_in, 16)
            for k in range(KC + 1):
                if k < KC:
                    dve.tensor_tensor(by_bank(OUT[:, k, :]), by_bank(OUT[:, k, :]), PS[:, 0, :, 0:JW],
                                      ALU.mult).then_inc(scaled, 1)
                if k:
                    dve.wait_ge(scaled, k)
                    for t0, t1, c in SEGS:
                        ins = dve.scalar_tensor_tensor(XT[:, k - 1, t0:t1], OUT[:, k - 1, t0:t1],
                                                       GP[:, l, k - 1, c:c + 1], XT[:, k - 1, t0:t1], ALU.mult, ALU.add)
                    ins.then_inc(x_ready, 1)
            if l == 0:
                stats_dve(dve, 2)
                h_dve(dve, 1, lambda k: XT[:, k, :], TMP)
            else:
                for t in range(0, NT, 2):
                    dve.wait_ge(turned, t + 1)
                    if t >= 2:
                        dve.wait_ge(row_out[0], 16 * (t // 2))
                    dve.tensor_copy(ROWS[:, 0, :], PS[:, 0, 0:2, :].rearrange("p b n -> p (b n)")).then_inc(rows_dve, 1)

        block.__exit__(None, None, None)

    ROWS_N = 40
    head_zone = [zone]
    TOK = sb("token_scalars", [P, 3, 2, H, NT], at=head_zone)
    DEC = sb("chunk_decay", [P, 2, H, NT], at=head_zone)
    rows_dram = nc.dram_tensor("gate_rows", (2, 2, H, T), F32).ap()
    dec_dram = nc.dram_tensor("decay_rows", (2, H, NT), F32).ap()

    def gates():
        z = list(head_zone)
        GWR = sb("gate_w_raw", [P, KC * P], at=z)
        GWH = sb("gate_w_hi", [P, KC * P], F32R, at=z)
        GWL = sb("gate_w_lo", [P, KC * P], F32R, at=z)
        G = sb("gate_products", [P, T], at=z)
        IG, FG, B, A, M, E, S, S2, RST, DEL, WI, WK = (sb("rows_" + n, [ROWS_N, T], at=z) for n in (
            "i", "f", "b", "a", "m", "e", "s", "s2", "reset", "shift", "carry", "keep"))
        BI, BF, M0 = (sb("row_" + n, [ROWS_N, 1], at=z) for n in ("b_i", "b_f", "m0"))
        MP, ME, DR, NM = (sb("chunk_" + n, [ROWS_N, NT], at=z) for n in ("m_before", "m_end", "decay", "m_new"))
        gw_in, small_in, gw_hi, gw_lo, product, rows_sb = (sem(s) for s in (
            "gate_w_loaded", "gate_small_loaded", "gate_w_hi_ready", "gate_w_lo_ready", "gates_product", "gates_in_sbuf"))
        cleared, moved, f_ready, exp_ready, args_ready, exps_ready, neg_ready = (sem(s) for s in (
            "rows_cleared", "rows_moved", "f_rows_ready", "exp_f_ready", "exponents_ready", "exponentials_ready",
            "rows_out_ready"))
        f_abs, turned, stored, m_out, dec_in, act_e = (sem(s) for s in (
            "f_abs_ready", "tokens_turned", "gate_rows_stored", "new_m_stored", "decay_spread", "decay_exp_ready"))
        chain = sem("gates_dve_chain")
        parts = ((0, 0), (1, 32))
        block = nc.Block()
        block.__enter__()

        @block.sync
        def _(sp):
            sp.dma_start(GWR[:].rearrange("p (k n) -> p k n", k=KC),
                         in_tile(a["w_in_o"][0], a["w_in_o"].shape[2] - P)).then_inc(gw_in, 16)
            sp.dma_start(RST[:], a["reset"]).then_inc(small_in, 16)
            sp.wait_ge(cleared, 1)
            with nc.allow_non_contiguous_dma("vectors, one element per partition"):
                for d, r in parts:
                    sp.dma_start(BI[r:r + H, :], a["b_if"][0, d, 0].rearrange("(h o) -> h o", o=1)).then_inc(small_in, 16)
                    sp.dma_start(BF[r:r + H, :], a["b_if"][0, d, 1].rearrange("(h o) -> h o", o=1)).then_inc(small_in, 16)
                    sp.dma_start(M0[r:r + H, :], a["state_mlstm_m"][0, 0, d].rearrange("(h o) -> h o", o=1)
                                 ).then_inc(small_in, 16)
            sp.wait_ge(rows_sb, 1)
            for d, r in parts:
                for n, dst in enumerate((IG, FG)):
                    first = P - 4 * H + (2 * d + n) * H
                    sp.dma_start(dst[r:r + H, :], G[first:first + H, :]).then_inc(moved, 16)
            sp.wait_ge(neg_ready, 1)
            for d, r in parts:
                sp.dma_start(rows_dram[0, d], M[r:r + H, :]).then_inc(stored, 16)
                with nc.allow_non_contiguous_dma("one element per partition"):
                    sp.dma_start(out["new_m"][0, 0, d].rearrange("(h o) -> h o", o=1), NM[r:r + H, 0:1]).then_inc(m_out, 16)
            sp.wait_ge(exps_ready, 4)
            for d, r in parts:
                sp.dma_start(rows_dram[1, d], WI[r:r + H, :]).then_inc(stored, 16)
                sp.dma_start(dec_dram[d], DR[r:r + H, :]).then_inc(stored, 16)
            sp.wait_ge(stored, 16 * 6)
            sp.dma_start(DEC[:].rearrange("p d h c -> p (d h c)"),
                         dec_dram.rearrange("d h c -> (d h c)").partition_broadcast(P)).then_inc(dec_in, 16)
            sp.wait_ge(dec_in, 16)
            sp.wait_ge(m_out, 32)

        @block.tensor
        def _(pe):
            pe.wait_ge(gw_lo, 1)
            for k in range(KC):
                for m, (w, h) in enumerate(((GWH, HHI), (GWH, HLO), (GWL, HHI))):
                    for j in range(NJ):
                        ins = pe.matmul(PS[:, 0, j, 0:JW], w[:, k * P:(k + 1) * P], h[:, k, j * JW:(j + 1) * JW],
                                        start=k == 0 and m == 0, stop=k == KC - 1 and m == 2)
            ins.then_inc(product, 1)
            pe.wait_ge(exps_ready, 4)
            for q, rows in enumerate((A, E, WK)):
                for c in range(NT):
                    ins = pe.transpose(PS[:, 1, q, c * ROWS_N:(c + 1) * ROWS_N], rows[:, c * P:(c + 1) * P],
                                       IDENT[0:ROWS_N, 0:ROWS_N])
            ins.then_inc(turned, 1)

        @block.scalar
        def _(act):
            act.wait_ge(gw_in, 16)
            act.activation(GWH[:], GWR[:], ACT.Copy).then_inc(gw_hi, 1)
            act.wait_ge(product, 1)
            act.activation(by_bank(G[96:128, :]), PS[96:128, 0, :, 0:JW], ACT.Copy).then_inc(rows_sb, 1)
            act.wait_ge(f_ready, 1)
            act.activation(E[:], FG[:], ACT.Abs).then_inc(f_abs, 1)
            act.wait_ge(f_abs, 1)
            act.activation(E[:], E[:], ACT.Exp, scale=-1.0).then_inc(exp_ready, 1)
            act.wait_ge(args_ready, 1)
            act.activation(WI[:], WI[:], ACT.Exp).then_inc(exps_ready, 1)
            act.activation(E[:], S2[:], ACT.Exp, scale=-1.0).then_inc(exps_ready, 1)
            act.activation(WK[:], WK[:], ACT.Exp).then_inc(exps_ready, 1)
            act.activation(DR[:], DR[:], ACT.Exp).then_inc(exps_ready, 1)

        @block.vector
        def _(dve):
            ch = Chain(dve, chain)
            for t in (IG, FG, BI, BF, M0, DEL, M, B):
                ins = dve.memset(t[:], 0.0)
            ch.link(ins)
            dve.sem_inc(cleared, 1)
            dve.wait_ge(gw_hi, 1)
            dve.tensor_tensor(GWL[:], GWR[:], GWH[:].bitcast(F32), ALU.subtract).then_inc(gw_lo, 1)
            dve.wait_ge(moved, 64)
            dve.wait_ge(small_in, 16 * 7)
            dve.tensor_scalar(FG[:], FG[:], BF[:, 0:1], None, ALU.add).then_inc(f_ready, 1)
            ch.link(dve.tensor_scalar(IG[:], IG[:], BI[:, 0:1], None, ALU.add))
            dve.wait_ge(f_ready, 1)
            dve.wait_ge(exp_ready, 1)
            log1p(dve, ch, E[:], S[:], S2[:])
            ch.link(dve.scalar_tensor_tensor(S[:], FG[:], 0.0, S[:], ALU.min, ALU.subtract))
            dve.tensor_tensor_scan(B[0:H, :], RST[0:H, :], S[0:H, :], 0.0, op0=ALU.mult, op1=ALU.add)
            ch.link(dve.tensor_tensor_scan(B[32:40, ::-1], RST[32:40, ::-1], S[32:40, ::-1], 0.0, op0=ALU.mult, op1=ALU.add))
            ch.link(dve.tensor_tensor(A[:], IG[:], B[:], ALU.subtract))
            dve.tensor_copy(DEL[0:H, 256::P], B[0:H, 255:T - 1:P])
            ch.link(dve.tensor_copy(DEL[32:40, 255:T - 1:P], B[32:40, 256::P]))
            for t0, t1 in ((0, NCTX), (NCTX, T)):
                for d, r in parts:
                    w = slice(t0, t1) if d == 0 else slice(t1 - 1, None if t0 == 0 else t0 - 1, -1)
                    first = 0.0 if t0 == 0 else M0[r:r + H, 0:1]
                    ins = dve.tensor_tensor_scan(M[r:r + H, w], DEL[r:r + H, w], A[r:r + H, w], first,
                                                 op0=ALU.add, op1=ALU.max)
            ch.link(ins)
            ch.link(dve.tensor_tensor(S2[:], B[:], M[:], ALU.add))
            ch.link(dve.memset(MP[:], 0.0))
            dve.memset(ME[:], 0.0)
            ch.link(dve.memset(NM[:], 0.0))
            dve.tensor_copy(MP[0:H, 1:2], M0[0:H, :])
            dve.tensor_copy(MP[32:40, 8:9], M0[32:40, :])
            dve.tensor_copy(MP[0:H, 2:9], S2[0:H, 255:T - 1:P])
            dve.tensor_copy(MP[32:40, 1:8], S2[32:40, 256::P])
            dve.tensor_copy(ME[0:H, :], M[0:H, P - 1::P])
            dve.tensor_copy(ME[32:40, :], M[32:40, 0::P])
            dve.tensor_copy(NM[0:H, 0:1], S2[0:H, P - 1:P])
            ch.link(dve.tensor_copy(NM[32:40, 0:1], S2[32:40, 0:1]))
            rows3 = "r (c n) -> r c n"
            spread = [ROWS_N, NT, P]
            dve.tensor_tensor(WI[:].rearrange(rows3, n=P), MP[:].unsqueeze(2).to_broadcast(spread),
                              M[:].rearrange(rows3, n=P), ALU.subtract)
            dve.tensor_tensor(WK[:].rearrange(rows3, n=P), A[:].rearrange(rows3, n=P),
                              ME[:].unsqueeze(2).to_broadcast(spread), ALU.subtract)
            ch.link(dve.tensor_tensor(DR[:], MP[:], ME[:], ALU.subtract))
            dve.sem_inc(args_ready, 1)
            ch.link(dve.tensor_scalar(M[:], M[:], -1.0, None, ALU.mult))
            dve.sem_inc(neg_ready, 1)
            dve.wait_ge(turned, 1)
            for q in range(3):
                for d, r in parts:
                    dve.tensor_copy(TOK[:, q, d], PS[:, 1, q, 0:NT * ROWS_N].rearrange("p (c r) -> p r c", r=ROWS_N)[:, r:r + H, :])

        block.__exit__(None, None, None)

    w_o = a["w_in_o"][0]

    DK, DV = P, 2 * P
    DV1 = DV + 1
    QCOL, KCOL, VCOL, OCOL, ZCOL = 0, D, 2 * D, 4 * D, 6 * D
    PAIR0 = 3 * KC

    def mlstm():
        z = list(head_zone)
        QT = sb("q_t", [P, 2, T], at=z)
        KT = sb("k_t", [P, 2, T], at=z)
        V = sb("v_rows", [P, 2, NT, DV1], at=z)
        G = sb("out_gate", [P, 2, 2 * T], at=z)
        DM = sb("decay_matrix", [P, 2, T], at=z)
        QW = sb("q_carry", [P, 2, T], at=z)
        KW = sb("k_rows", [P, 2, T], at=z)
        HS = sb("h_rows", [P, NT, DV], at=z)
        TO = sb("o_tanh", [P, T], at=z)
        TZ = sb("z_tanh", [P, T], at=z)
        C = sb("state", [P, 2, DV1], at=z)
        CC = sb("context_state", [P, 2, DV1], at=z)
        MK = sb("causal", [P, 2, P], at=z)
        TK = sb("head_scalars", [P, 3, 2, NT], at=z)
        DC = sb("head_decay", [P, 2, NT], at=z)
        R = sb("inverse_den", [P, 2], at=z)

        BANK = [PS[:, 1, 0], PS[:, 1, 1], PS[:, 1, 2], PX[:, 0], PX[:, 1]]
        NUM, KV = BANK[0:2], BANK[3:5]
        KS_BANK = [BANK[2], BANK[3], BANK[4], BANK[0], BANK[1], BANK[2]]
        ROUNDS = [(0, 4), (4, 8), (8, 9)]

        mask_in, ones_ready = sem("causal_loaded"), sem("v_ones_ready")
        rows_in, carry_in, c_in = sem("max_rows_loaded"), sem("carry_rows_loaded"), sem("state_loaded")
        va_done, evacuated = sem("v_first_product"), sem("projection_evacuated")
        ks_done, ks_out = sem("k_and_scores_done"), sem("k_and_scores_evacuated")
        turned, post_out, y_out = sem("h_turned"), sem("y_ready"), sem("y_stored")
        num_done, num_out, kv_done, c_ready = (sem(s) for s in (
            "numerator_done", "numerator_read", "state_product_done", "state_ready"))
        d_args, d_exp, p_ready, cc_out = (sem(s) for s in (
            "weights_exponent_ready", "weights_ready", "scores_ready", "context_state_stored"))
        z_ready, g_ready = sem("z_parts_ready"), sem("gate_ready")
        chain = sem("mlstm_dve_chain")
        block = nc.Block()
        block.__enter__()

        def pair(j, n):
            return j * 4 + (PAIR0 + n // 2), n % 2

        def v_tile(j, half):
            return w_o.rearrange("(k p) n -> p k n", p=P)[:, 4 * half:4 * half + 4, ds(j * DV + VCOL, DV)]

        def tile_source(j, n):
            if n in (2, 3):
                return v_tile(j, n - 2)
            if n < 2:
                return in_tile(w_o, j * P + (QCOL, KCOL)[n])
            return in_tile(w_o, j * DV + (OCOL, ZCOL)[n % 2] + (n - 4) // 2 * P)

        def run(eng, body, chained=None):
            body(0, 0, True, False, False)
            body(1, 1, True, True, False)
            if chained:
                chained.start()
            with eng.Fori(1, H // 2 - 1) as m:
                for b in range(2):
                    if chained:
                        chained.turn(m, b)
                    body(m * 2 + b, b, True, True, True)
            if chained:
                chained.stop()
            body(H - 2, 0, True, True, True)
            body(H - 1, 1, True, True, True, last=True)
            body(H, 0, False, True, True)

        @block.sync
        def _(sp):
            sp.dma_start(MK[:], a["causal"]).then_inc(mask_in, 16)

            def context_state(h):
                sp.wait_ge(c_ready, h * 8 + 1)
                with nc.allow_non_contiguous_dma("normalisers, one element per partition"):
                    for d in range(2):
                        sp.dma_start(out["new_C"][0, 0, d, ds(h, 1)].rearrange("h k v -> k (h v)"),
                                     CC[:, d, 0:DV]).then_inc(cc_out, 16)
                        sp.dma_start(out["new_n"][0, 0, d, ds(h, 1)].rearrange("h k -> k h"),
                                     CC[:, d, DV:DV1]).then_inc(cc_out, 16)

            def store_y(h, p):
                sp.wait_ge(post_out, h * 5 + 5)
                sp.dma_start(y_dram[ds(h * 2, 2)].rearrange("b p t -> p b t"),
                             G[:, p, :].rearrange("p (b t) -> p b t", b=2)).then_inc(y_out, 16)

            def body(j, p, project_it, ml, post, last=False):
                if ml:
                    h = j - 1
                    if post:
                        sp.wait_ge(num_done, h * 9)
                    sp.dma_start(DM[:], rows_dram[0, :, ds(h, 1)].rearrange("d h t -> (d h) t").partition_broadcast(P)
                                 ).then_inc(rows_in, 16)
                    sp.dma_start(QW[:], rows_dram[1, :, ds(h, 1)].rearrange("d h t -> (d h) t").partition_broadcast(P)
                                 ).then_inc(carry_in, 16)
                    with nc.allow_non_contiguous_dma("normalisers, one element per partition"):
                        for d in range(2):
                            sp.dma_start(C[:, d, 0:DV], a["state_mlstm_C"][0, 0, d, ds(h, 1)].rearrange("h k v -> k (h v)")
                                         ).then_inc(c_in, 16)
                            sp.dma_start(C[:, d, DV:DV1], a["state_mlstm_n"][0, 0, d, ds(h, 1)].rearrange("h k -> k h")
                                         ).then_inc(c_in, 16)
                for n in (2, 3, 4, None, 5, "context", 6, 7, 8, 9):
                    if n is None:
                        if post:
                            store_y(j - 2, p)
                    elif n == "context":
                        if ml:
                            context_state(j - 1)
                    elif project_it:
                        if n < 8:
                            w_load(sp, *pair(j, n), tile_source(j, n))
                        elif last:
                            w_load(sp, *pair(j, n), out_tile(a["w_out_o"][0], n - 8, 0))
                        else:
                            w_load(sp, *pair(j, n), tile_source(j + 1, n - 8))

            run(sp, body)
            store_y(H - 1, (H - 1) % 2)
            sp.wait_ge(y_out, 16 * H)
            sp.wait_ge(cc_out, 64 * H)
            sp.wait_ge(mask_in, 16)

        @block.tensor
        def _(pe):
            def k_and_scores(h, q, post, rounds):
                for r in rounds:
                    t0, t1 = ROUNDS[r % 3]
                    if post and r >= 3:
                        pe.wait_ge(num_out, h * 9)
                    if post and r in (1, 2):
                        pe.wait_ge(c_ready, h * 8)
                    if r == 5:
                        pe.wait_ge(ks_out, h * 6 + 1)
                    for t in range(t0, t1):
                        dst = KS_BANK[r][:, (t - t0) * P:(t - t0 + 1) * P]
                        cols = slice(t * P, (t + 1) * P)
                        if r < 3:
                            ins = pe.transpose(dst, KT[:, q, cols], IDENT[:])
                        else:
                            ins = pe.matmul(dst, KT[:, q, cols], QT[:, q, cols], start=True, stop=True,
                                            skip_group_check=True)
                    ins.then_inc(ks_done, 1)

            def turn_h(h, ks):
                if ks:
                    pe.wait_ge(ks_out, h * 6 + 12)
                pe.wait_ge(num_out, h * 9 + 9)
                for r in range(5):
                    for n in range(4 * r, min(4 * r + 4, 2 * NT)):
                        ins = pe.transpose(BANK[r][:, n % 4 * P:(n % 4 + 1) * P],
                                           HS[:, n % NT, n // NT * P:(n // NT + 1) * P], IDENT[:])
                    ins.then_inc(turned, 1)

            def step(h, q, s, post):
                if s == 0:
                    pe.wait_ge(p_ready, h + 1)
                    pe.wait_ge(ks_out, h * 6 + 6)
                    if post:
                        pe.wait_ge(post_out, h * 5)
                if s == 1:
                    pe.wait_ge(c_in, h * 64 + 64)
                if s < 8:
                    if s:
                        pe.wait_ge(c_ready, h * 8 + s)
                    for d in range(2):
                        t = s if d == 0 or s == 0 else 9 - s
                        ins = pe.matmul(KV[d][:, 0:DV1], KW[:, d, t * P:(t + 1) * P], V[:, q, t, :], start=True, stop=True)
                    ins.then_inc(kv_done, 1)
                else:
                    pe.wait_ge(c_ready, h * 8 + s)
                if s:
                    pe.wait_ge(num_out, h * 9 + s)
                for d in range(2):
                    t = s if d == 0 or s == 0 else 9 - s
                    cols = slice(t * P, (t + 1) * P)
                    ins = pe.matmul(NUM[d][:, 0:DV1], DM[:, d, cols], V[:, q, t, :], start=True, stop=s == 0)
                    if s:
                        ins = pe.matmul(NUM[d][:, 0:DV1], QW[:, d, cols], C[:, d, :], start=False, stop=True)
                ins.then_inc(num_done, 1)

            def values(j, first, last, done, middle=None):
                for k in range(KC):
                    half, kk = divmod(k, 4)
                    if kk == 0:
                        pair_n, slot = pair(j, 2 + half)
                        pe.wait_ge(w_lo, pair_n * 2 + slot + 1)
                        if middle and half:
                            middle()
                    cols = slice(kk * DV, (kk + 1) * DV)
                    for t in range(first, last):
                        n = t - first
                        dst = PS[:, 0, n // 2, n % 2 * DV:(n % 2 + 1) * DV]
                        for m, (h, w) in enumerate(((HHI, WHI), (HHI, WLO), (HLO, WHI))):
                            ins = pe.matmul(dst, h[:, k, t * P:(t + 1) * P], w[:, half, cols],
                                            start=k == 0 and m == 0 and n % 2 == 0, stop=k == KC - 1 and m == 2,
                                            skip_group_check=True)
                    if done is None and kk == 3:
                        ins.then_inc(w_used, 1)
                if done is not None:
                    ins.then_inc(done, 1)

            def body(j, p, project_it, ml, post, last=False):
                h, q = j - 1, 1 - p

                def job(n, middle=None):
                    if not project_it:
                        if middle:
                            middle()
                        return
                    if not isinstance(j, int) or j or n:
                        pe.wait_ge(evacuated, j * 8 + n)
                    if n == 2:
                        values(j, 0, 6, va_done, middle)
                    elif n == 3:
                        values(j, 6, 9, None)
                    else:
                        project(pe, *pair(j, n), 0, hhi, hlo, middle=middle)

                def steps(*some):
                    if ml:
                        for s in some:
                            step(h, q, s, post)

                def turn_before():
                    if post:
                        turn_h(h - 1, True)

                job(0)
                if ml:
                    k_and_scores(h, q, post, range(0, 3))
                job(1)
                if ml:
                    k_and_scores(h, q, post, range(3, 6))
                job(2, turn_before)
                steps(0)
                job(3)
                steps(1)
                job(4, lambda: steps(2))
                steps(3)
                job(5, lambda: steps(4))
                steps(5)
                job(6, lambda: steps(6))
                steps(7)
                job(7)
                steps(8)

            pe.wait_ge(ones_ready, 1)
            run(pe, body)
            turn_h(H - 1, False)

        @block.scalar
        def _(act):
            def body(j, p, project_it, ml, post, last=False):
                if project_it:
                    w_split_hi(act, *pair(j, 1))
                def weights():
                    if ml:
                        act.wait_ge(d_args, j)
                        act.activation(DM[:], DM[:], ACT.Exp).then_inc(d_exp, 1)

                if not project_it:
                    weights()
                    return
                group = PS[:, 0, :, 0:JW]
                rows = PS[:, 0].rearrange("p b (t n) -> p (b t) n", n=DV)
                for n in range(8):
                    if n == 2:
                        act.wait_ge(va_done, j + 1)
                        act.activation(V[:, p, 0:6, 0:DV], rows, ACT.Copy).then_inc(evacuated, 1)
                        w_split_hi(act, *pair(j, 4))
                        continue
                    projected(act, *pair(j, n))
                    if n == 0:
                        ins = act.activation(by_bank(QT[:, p, :]), group, ACT.Copy, scale=float(DK) ** -0.5)
                    elif n == 1:
                        ins = act.activation(by_bank(KT[:, p, :]), group, ACT.Copy)
                    elif n == 3:
                        ins = act.activation(V[:, p, 6:9, 0:DV], rows[:, 0:3], ACT.Copy)
                    elif n in (4, 6):
                        act.wait_ge(g_ready, j * 2 + (n - 4) // 2)
                        ins = act.activation(by_bank(TO[:]), group, ACT.Tanh, scale=0.5)
                    else:
                        b = (n - 5) // 2
                        if b == 0 and post:
                            act.wait_ge(y_out, j * 16 - 16)
                        act.activation(by_bank(TZ[:]), group, ACT.Tanh, scale=0.5).then_inc(z_ready, 1)
                        ins = act.activation(by_bank(G[:, p, b * T:(b + 1) * T]), group, ACT.Copy, scale=0.25)
                    ins.then_inc(evacuated, 1)
                    if n != 7:
                        w_split_hi(act, *pair(j, {0: 2, 1: 3, 3: 5, 4: 6, 5: 7, 6: 8}[n]))
                    if n == 0:
                        weights()

            run(act, body)

        @block.vector
        def _(dve):
            ch = Chain(dve, chain)

            def load_scalars(h):
                ch.link(dve.tensor_copy(TK[:], TOK[:, :, :, ds(h, 1), :].rearrange("p q d h c -> p q (d h) c")))
                ch.link(dve.tensor_copy(DC[:], DEC[:, :, ds(h, 1), :].rearrange("p d h c -> p (d h) c")))

            def by_tile(ap):
                return ap.rearrange("p (c n) -> p c n", n=P)

            def prepare(h, q, between):
                load_scalars(h)
                for r, (t0, t1) in enumerate(ROUNDS):
                    dve.wait_ge(ks_done, h * 6 + r + 1)
                    shape = [P, t1 - t0, P]
                    for d in range(2):
                        ins = dve.tensor_tensor(by_tile(KW[:, d, t0 * P:t1 * P]), by_tile(KS_BANK[r][:, 0:(t1 - t0) * P]),
                                                TK[:, 2, d, t0:t1].unsqueeze(2).to_broadcast(shape), ALU.mult)
                        if d == 0:
                            ch.link(ins)
                    ins.then_inc(ks_out, 1)
                dve.wait_ge(rows_in, h * 16 + 16)
                shape = [P, NT, P]
                for d in range(2):
                    ch.link(dve.tensor_tensor(by_tile(DM[:, d, :]), by_tile(DM[:, d, :]),
                                              TK[:, 0, d, :].unsqueeze(2).to_broadcast(shape), ALU.add))
                    ins = dve.tensor_tensor(by_tile(DM[:, d, :]), by_tile(DM[:, d, :]),
                                            MK[:, d, :].unsqueeze(1).to_broadcast(shape), ALU.add)
                    ch.link(ins)
                dve.sem_inc(d_args, 1)
                between()
                dve.wait_ge(carry_in, h * 16 + 16)
                ch.link(dve.tensor_tensor(QW[:], QW[:], QT[:, q, :].unsqueeze(1).to_broadcast([P, 2, T]), ALU.mult))
                dve.wait_ge(d_exp, h + 1)
                for r, (t0, t1) in enumerate(ROUNDS):
                    dve.wait_ge(ks_done, h * 6 + r + 4)
                    w = slice(t0 * P, t1 * P)
                    for d in range(2):
                        ins = dve.tensor_tensor(DM[:, d, w], DM[:, d, w], KS_BANK[3 + r][:, 0:(t1 - t0) * P], ALU.mult)
                        if d == 0:
                            ch.link(ins)
                    ins.then_inc(ks_out, 1)
                dve.wait_ge(ks_out, h * 6 + 6)
                dve.sem_inc(p_ready, 1)

            def finish_y(h, p):
                for r in range(5):
                    dve.wait_ge(turned, h * 5 + r + 1)
                    w = slice(4 * r * P, min(4 * r + 4, 2 * NT) * P)
                    dve.tensor_tensor(G[:, p, w], G[:, p, w], BANK[r][:, 0:w.stop - w.start], ALU.mult).then_inc(post_out, 1)

            def step(h, s, post):
                tiles = (s, s if s == 0 else 9 - s)
                if s < 8:
                    dve.wait_ge(kv_done, h * 8 + s + 1)
                    if s == 0:
                        if post:
                            dve.wait_ge(cc_out, h * 64)
                        ch.link(dve.tensor_copy(CC[:, 0, :], KV[0][:, 0:DV1]))
                        dve.tensor_copy(CC[:, 1, :], KV[1][:, 0:DV1]).then_inc(c_ready, 1)
                dve.wait_ge(num_done, h * 9 + s + 1)
                if 0 < s < 8:
                    for d in range(2):
                        ins = dve.scalar_tensor_tensor(C[:, d, :], C[:, d, :], DC[:, d, tiles[d]:tiles[d] + 1],
                                                       KV[d][:, 0:DV1], ALU.mult, ALU.add)
                        if d == 0:
                            ch.link(ins)
                    ins.then_inc(c_ready, 1)
                den = PS[:, 1, 0:2, DV]
                floor = TK[:, 1].rearrange("p d c -> p (d c)")[:, tiles[0]:NT + tiles[1] + 1:NT + tiles[1] - tiles[0]]
                ch.link(dve.scalar_tensor_tensor(R[:], den, -1.0, floor, ALU.mult, ALU.max))
                ch.link(dve.tensor_tensor(R[:], den, R[:], ALU.max))
                ch.link(dve.reciprocal(R[:], R[:]))
                for d, t in enumerate(tiles):
                    if s > 4 or (s == 0 and d == 1):
                        ins = dve.scalar_tensor_tensor(HS[:, t, :], NUM[d][:, 0:DV], R[:, d:d + 1], HS[:, t, :],
                                                       ALU.mult, ALU.add)
                    else:
                        ins = dve.tensor_scalar(HS[:, t, :], NUM[d][:, 0:DV], R[:, d:d + 1], None, ALU.mult)
                    if d == 0:
                        ch.link(ins)
                ins.then_inc(num_out, 1)

            def gate(j, p, b):
                dve.wait_ge(evacuated, j * 8 + 6 + 2 * b)
                g = G[:, p, b * T:(b + 1) * T]
                ch.link(dve.scalar_tensor_tensor(g, TZ[:], 1.0, g, ALU.add, ALU.mult))
                dve.scalar_tensor_tensor(g, TO[:], 1.0, g, ALU.add, ALU.mult).then_inc(g_ready, 1)

            def body(j, p, project_it, ml, post, last=False):
                h = j - 1

                def split(n):
                    if project_it:
                        w_split_lo(dve, *pair(j, n))

                def steps(*some):
                    if ml:
                        for s in some:
                            step(h, s, post)

                split(1)
                if ml:
                    prepare(h, 1 - p, lambda: split(2))
                else:
                    split(2)
                split(3)
                if post:
                    finish_y(h - 1, p)
                steps(0)
                split(4)
                steps(1)
                split(5)
                steps(2, 3)
                split(6)
                steps(4, 5)
                split(7)
                if project_it:
                    gate(j, p, 0)
                steps(6, 7)
                split(8)
                steps(8)
                if project_it:
                    gate(j, p, 1)

            LINKS = 59

            class Heads:

                def start(self):
                    self.before = ch.n

                def turn(self, m, b):
                    assert b == 0 or ch.n == LINKS, ch.n
                    ch.base, ch.n = m * (2 * LINKS) + (self.before + (b - 2) * LINKS), 0

                def stop(self):
                    assert ch.n == LINKS, ch.n
                    ch.base, ch.n = 0, self.before + 2 * LINKS * (H // 2 - 2)

            dve.memset(V[:, :, :, DV:DV1].rearrange("p a t o -> p a (t o)"), 1.0).then_inc(ones_ready, 1)
            dve.wait_ge(mask_in, 16)
            run(dve, body, Heads())
            finish_y(H - 1, (H - 1) % 2)

        block.__exit__(None, None, None)

    setup()
    lru()
    fourier()
    outputs(0, a["w_out_e"][0], 2 * KC, [in_tile(w_o, 0), in_tile(w_o, D)])
    gates()
    mlstm()
    outputs(1, a["w_out_o"][0], 7 * KC, None)


def consts():
    b, k1, k2 = np.arange(P)[:, None, None], np.arange(8)[None, :, None], np.arange(P)[None, None, :]
    turn = 2 * np.pi * (b * (k1 + 8 * k2) % NLAT) / NLAT
    token = np.stack([np.cos(turn), np.sin(turn)], axis=2)
    turn = 2 * np.pi * (np.arange(P)[:, None] * np.arange(P)[None, :] % P) / P
    channel = np.stack([np.cos(turn), -np.sin(turn)], axis=1) / np.sqrt(NLAT * P)
    t = np.arange(T) % P
    reset = np.where(np.arange(40)[:, None] < 32, t != 0, t != P - 1)
    s, t = np.arange(P)[:, None, None], np.arange(P)[None, None, :]
    hidden = np.concatenate([s > t, s < t], axis=1)
    return {"causal": np.where(hidden, np.float32(-3e38), np.float32(0)), "reset": reset.astype(np.float32), "ident": np.eye(P, dtype=np.float32), "ones": np.ones((P, P), np.float32),
            "token_dft": token.astype(np.float32), "channel_dft": channel.astype(np.float32)}


INS = ["x_prompt", "x_sample", "c", "state_lru", "state_mlstm_C", "state_mlstm_n", "state_mlstm_m", "c_ctx", "w_mod",
       "b_mod", "g_pre", "g_post", "w_in_e", "conv_w", "conv_b", "w_rg", "b_rg", "w_ig", "b_ig", "lru_lambda",
       "w_four", "b_four", "w_out_e", "w_in_o", "b_if", "w_out_o"]
OUTS = [("y_prompt", (1, NCTX, D)), ("y_sample", (1, NLAT, D)), ("new_lru", (1, 1, 2, D)),
        ("new_C", (1, 1, 2, H, 128, 256)), ("new_n", (1, 1, 2, H, 128)), ("new_m", (1, 1, 2, H))]


def kernel(**inputs):
    import concourse.bacc as bacc
    from concourse.bass_utils import run_bass_kernel_spmd

    nc = bacc.Bacc("TRN2", target_bir_lowering=False, num_devices=1)
    arrays = {n: np.ascontiguousarray(inputs[n]) for n in INS} | consts()
    arrays = {f"in_{n}": x for n, x in arrays.items()}
    a = {n[3:]: nc.dram_tensor(n, x.shape, mybir.dt.from_np(x.dtype), kind="ExternalInput").ap()
         for n, x in arrays.items()}
    out = {n: nc.dram_tensor(n, shape, F32, kind="ExternalOutput").ap() for n, shape in OUTS}
    build(nc, a, out)
    r = run_bass_kernel_spmd(nc, [arrays], core_ids=[0])
    return tuple(r.results[0][n] for n, _ in OUTS)
```

```python
import numpy as np

import concourse.bass as bass
from concourse import mybir

F32, F32R = mybir.dt.float32, mybir.dt.float32r
ALU = mybir.AluOpType
ACT = mybir.ActivationFunctionType
ds = bass.ds

P = 128
D = 1024
KC = D // P
NCTX, NLAT = 128, 1024
T = NCTX + NLAT
NT = T // P
NJ, JW = 3, T // 3
H = 8
EPS = 1e-6
GAP = 3
TP = T + GAP
JP = TP // 3
LAT = NCTX + GAP
TAP, CB, HBR, HBI, NEG, POS, H0 = 0, 4, 5, 6, 7, 8, 9
NPRM = 15


class Chain:

    def __init__(self, eng, sem, base=0):
        self.eng, self.sem, self.base, self.n = eng, sem, base, 0

    def link(self, ins):
        ins.then_inc(self.sem, 1)
        self.n += 1
        self.eng.wait_ge(self.sem, self.base + self.n)


def build(nc, a, out):
    sem = nc.alloc_semaphore
    bottom = [(nc.sbuf_base + 31) // 32 * 32]

    def sb(name, shape, dt=F32, at=None):
        at = bottom if at is None else at
        t = nc.alloc_sbuf_tensor_at(name, list(shape), dt, offset=at[0])
        at[0] += (int(np.prod(shape[1:])) * 4 + 31) // 32 * 32
        assert at[0] <= nc.sbuf_usable_end, (name, at[0])
        return t

    h_at = bottom[0]
    HHI = sb("h_hi", [P, KC, T], F32R)
    h_lo_at = bottom[0]
    HLO = sb("h_lo", [P, KC, T], F32R)
    WRAW = sb("w_raw", [P, 2, KC * P])
    WHI = sb("w_hi", [P, 2, KC * P], F32R)
    WLO = sb("w_lo", [P, 2, KC * P], F32R)
    IDENT = sb("ident", [P, P])
    ONES = sb("ones", [P, P])
    AM = sb("mod_scale", [P, 2, KC, 2])
    SH = sb("mod_shift", [P, 2, KC, 2])
    GP = sb("mod_gate", [P, 2, KC, 2])
    SC = sb("cond_silu", [P, 2, KC])
    BM = sb("b_mod", [P, 2, 24])
    GN = sb("norm_gains", [P, 2, 2, KC])
    PRM = sb("lru_params", [P, KC, NPRM])
    LAM = sb("lru_lambda", [P, 2, KC])
    prm_in = sem("lru_params_loaded")
    zone = bottom[0]
    PS = nc.alloc_psum_tensor("psum_groups", [P, 2, 3, 512], F32)
    PX = nc.alloc_psum_tensor("psum_extra", [P, 2, 512], F32)
    y_dram = nc.dram_tensor("y_scratch", (16, P, T), F32).ap()
    x_dram = nc.dram_tensor("x_scratch", (KC, P, T), F32).ap()

    SEGS = ((0, NCTX, 1), (NCTX, T, 0))

    w_loaded = [sem("w_loaded_0"), sem("w_loaded_1")]
    w_hi, w_lo, w_used = sem("w_hi_ready"), sem("w_lo_ready"), sem("w_used")

    def w_load(sp, pair, slot, src):
        if not isinstance(pair, int) or pair >= 1:
            sp.wait_ge(w_lo, pair * 2 + slot - 1)
        sp.dma_start(WRAW[:, slot, :].rearrange("p (k n) -> p k n", k=src.shape[1]), src).then_inc(w_loaded[slot], 16)

    def w_split_hi(act, pair, slot):
        act.wait_ge(w_loaded[slot], (pair + 1) * 16)
        if not isinstance(pair, int) or pair >= 1:
            act.wait_ge(w_used, pair * 2 + slot - 1)
        act.activation(WHI[:, slot, :], WRAW[:, slot, :], ACT.Copy).then_inc(w_hi, 1)

    def w_split_lo(dve, pair, slot):
        dve.wait_ge(w_hi, pair * 2 + slot + 1)
        dve.tensor_tensor(WLO[:, slot, :], WRAW[:, slot, :], WHI[:, slot, :].bitcast(F32), ALU.subtract).then_inc(w_lo, 1)

    def in_tile(w, col):
        return w.rearrange("(k p) n -> p k n", p=P)[:, :, ds(col, P)]

    def project(pe, pair, slot, group, hi, lo, k0=0, start=True, stop=True, ready=None, middle=None):
        pe.wait_ge(w_lo, pair * 2 + slot + 1)
        for k in range(KC):
            if ready:
                ready(k0 + k)
            if middle and k == KC // 2:
                middle()
            for m, (w, h) in enumerate(((WHI, hi), (WHI, lo), (WLO, hi))):
                for j in range(NJ):
                    ins = pe.matmul(PS[:, group, j, 0:JW], w[:, slot, k * P:(k + 1) * P],
                                    h(k0 + k)[:, j * JW:(j + 1) * JW],
                                    start=start and k == 0 and m == 0, stop=stop and k == KC - 1 and m == 2)
        ins.then_inc(w_used, 1)

    def projected(eng, pair, slot):
        eng.wait_ge(w_used, pair * 2 + slot + 1)

    def out_tile(w, half, col):
        return w.rearrange("(h k p) n -> h p k n", h=2, p=P)[half][:, :, ds(col, P)]

    hhi, hlo = (lambda k: HHI[:, k, :]), (lambda k: HLO[:, k, :])

    def by_bank(ap, w=JW):
        return ap.rearrange("p (j n) -> p j n", n=w)

    y_in = [sem(f"y_loaded_{k}") for k in range(KC)]

    def load_y(sp, n):
        dst = (HHI if 2 * n < KC else HLO)[:, 2 * n % KC:2 * n % KC + 2, :].bitcast(F32)
        sp.dma_start(dst, y_dram[2 * n:2 * n + 2].rearrange("k p t -> p k t")).then_inc(y_in[n], 16)

    norm_zone = [zone]
    XT = sb("xT", [P, KC, T], at=norm_zone)
    TMP = sb("norm_tmp", [P, 2, T], at=norm_zone)
    SQ = sb("squares", [P, 2, T], at=norm_zone)
    RSTD = sb("rstd_rows", [96, JW], at=norm_zone)
    sq_ready, sq_used = sem("squares_ready"), sem("squares_summed")
    var_ready, std_ready = sem("variance_ready"), sem("std_ready")
    rstd_ready, rstd_spread = sem("rstd_ready"), sem("rstd_spread")

    def squares_act(act, m, x_of, x_ready=None):
        for k in range(KC):
            if x_ready:
                x_ready(act, k)
            if k >= 2 or m:
                act.wait_ge(sq_used, KC * m + k - 1)
            act.activation(SQ[:, k % 2, :], x_of(k), ACT.Square).then_inc(sq_ready, 1)

    def root_act(act, n):
        act.wait_ge(var_ready, n + 1)
        act.activation(RSTD[:], RSTD[:], ACT.Sqrt).then_inc(std_ready, 1)

    def squares_pe(pe, m):
        for k in range(KC):
            pe.wait_ge(sq_ready, KC * m + k + 1)
            for j in range(NJ):
                ins = pe.matmul(PX[32 * j:32 * j + 32, 1, 0:JW], ONES[:, 0:32], SQ[:, k % 2, j * JW:(j + 1) * JW],
                                start=k == 0, stop=k == KC - 1)
            ins.then_inc(sq_used, 1)

    def spread_pe(pe, n, group=0):
        pe.wait_ge(rstd_ready, n + 1)
        for j in range(NJ):
            ins = pe.matmul(PS[:, group, j, 0:JW], ONES[32 * j:32 * j + 1, :], RSTD[32 * j:32 * j + 1, :],
                            start=True, stop=True)
        ins.then_inc(rstd_spread, 1)

    def stats_dve(dve, n, used, count):
        dve.wait_ge(used, count)
        dve.tensor_scalar(RSTD[:], PX[0:96, 1, 0:JW], 1.0 / D, EPS, ALU.mult, ALU.add).then_inc(var_ready, 1)
        dve.wait_ge(std_ready, n + 1)
        dve.reciprocal(RSTD[:], RSTD[:]).then_inc(rstd_ready, 1)

    normed, modulated, h_hi, h_lo = sem("x_normed"), sem("h_modulated"), sem("h_hi_ready"), sem("h_lo_ready")

    def modulate(eng, out, x, l, k, c):
        return eng.activation(out, x, ACT.Identity, scale=AM[:, l, k, c:c + 1], bias=SH[:, l, k, c:c + 1])

    def h_dve(dve, l, x_of, TMP):
        dve.wait_ge(rstd_spread, 2 * l + 1)
        for k in range(KC + 1):
            if k < KC:
                if k >= 2:
                    dve.wait_ge(h_lo, KC * l + k - 1)
                dve.tensor_tensor(by_bank(TMP[:, k % 2, :]), by_bank(x_of(k)), PS[:, 0, :, 0:JW],
                                  ALU.mult).then_inc(normed, 1)
            if k:
                dve.wait_ge(h_hi, KC * l + k)
                dve.tensor_tensor(HLO[:, k - 1, :], TMP[:, (k - 1) % 2, :], HHI[:, k - 1, :].bitcast(F32),
                                  ALU.subtract).then_inc(h_lo, 1)

    def h_act(act, l, TMP):
        for k in range(KC):
            act.wait_ge(normed, KC * l + k + 1)
            for t0, t1, c in SEGS:
                modulate(act, TMP[:, k % 2, t0:t1], TMP[:, k % 2, t0:t1], l, k, c).then_inc(modulated, 1)
            act.wait_ge(modulated, 2 * (KC * l + k + 1))
            act.activation(HHI[:, k, :], TMP[:, k % 2, :], ACT.Copy).then_inc(h_hi, 1)

    def setup():
        z = list(norm_zone)
        XS, WS = 4, 4
        XR = sb("x_rows", [P, XS, D], at=z)
        WM = sb("w_mod_rows", [P, WS, 2 * D], at=z)
        CD = sb("cond", [P, 2, KC], at=z)
        ZERO = sb("zeros", [P, 32], at=z)
        BY_PE, BY_DVE = (3, 7), (0, 1, 2, 4, 5, 6)
        ACC = sb("mod_sums", [P, 2, 2 * D], at=[h_at])
        XN = sb("x_normed", [P, KC, T], at=[h_lo_at])
        wm_added = sem("w_mod_added")
        MD = sb("mod", [P, 16, 2], at=z)
        const_in, cond_in, gains_in = sem("const_loaded"), sem("cond_loaded"), sem("gains_loaded")
        x_in = [sem(f"x_loaded_{n}") for n in range(XS)]
        wm_in = [sem(f"w_mod_loaded_{n}") for n in range(WS)]
        x_turned, xT_dve, xT_act, x_spilled = (sem(s) for s in ("x_turned", "xT_by_dve", "xT_by_act", "x_spilled"))
        cond_tanh, cond_ready, zero_ready = sem("cond_tanh"), sem("cond_ready"), sem("zeros_ready")
        mod_done, mod_ready, wm_used = sem("mod_summed"), sem("mod_ready"), sem("w_mod_used")
        dve_chain = sem("setup_dve_chain")
        wm_src = a["w_mod"][0].rearrange("(k p) n -> k p n", p=P)
        block = nc.Block()
        block.__enter__()

        @block.sync
        def _(sp):
            def x_rows(t):
                if t >= XS:
                    sp.wait_ge(x_turned, t - XS + 1)
                src = a["x_prompt"][0] if t == 0 else a["x_sample"][0, (t - 1) * P:t * P, :]
                sp.dma_start(XR[:, t % XS, :], src).then_inc(x_in[t % XS], 16)

            sp.dma_start(IDENT[:], a["ident"]).then_inc(const_in, 16)
            for t in range(NT):
                x_rows(t)
            for n in range(KC):
                if n >= WS:
                    m = n - WS
                    sp.wait_ge(*((wm_used, BY_PE.index(m) + 1) if m in BY_PE else (wm_added, 2 * BY_DVE.index(m) + 2)))
                sp.dma_start(WM[:, n % WS, :], wm_src[n][:, 0:2 * D]).then_inc(wm_in[n % WS], 16)
            for n in range(2):
                w_load(sp, 0, n, in_tile(a["w_in_e"][0], n * D))
            sp.wait_ge(xT_dve, 5)
            sp.wait_ge(xT_act, 4)
            sp.dma_start(x_dram.rearrange("k p t -> p k t"), XT[:]).then_inc(x_spilled, 16)
            with nc.allow_non_contiguous_dma("vectors, one element per partition"):
                by_channel = "(k p) -> p k"
                for j in range(4):
                    sp.dma_start(PRM[:, :, TAP + j], a["conv_w"][0, j].rearrange(by_channel, p=P)).then_inc(prm_in, 16)
                sp.dma_start(PRM[:, :, CB], a["conv_b"][0].rearrange(by_channel, p=P)).then_inc(prm_in, 16)
                for d in range(2):
                    for col, src in ((HBR, a["b_rg"][0, d]), (HBI, a["b_ig"][0, d]), (H0, a["state_lru"][0, 0, d])):
                        sp.dma_start(PRM[:, :, 5 * d + col], src.rearrange(by_channel, p=P)).then_inc(prm_in, 16)
                    sp.dma_start(LAM[:, d, :], a["lru_lambda"][0, d].rearrange(by_channel, p=P)).then_inc(prm_in, 16)
            sp.wait_ge(x_spilled, 16)

        @block.gpsimd
        def _(pool):
            pool.memset(ZERO[:], 0.0).then_inc(zero_ready, 1)

        @block.tensor
        def _(pe):
            pe.wait_ge(const_in, 16)
            for t in range(NT):
                pe.wait_ge(x_in[t % XS], 16 * (t // XS + 1))
                if t >= 2:
                    pe.wait_ge(xT_act if t % 2 else xT_dve, t // 2)
                for k in range(KC):
                    ins = pe.transpose(PS[:, t % 2, k // 4, (k % 4) * P:(k % 4 + 1) * P],
                                       XR[:, t % XS, k * P:(k + 1) * P], IDENT[:])
                ins.then_inc(x_turned, 1)
            pe.wait_ge(const_in, 32)
            squares_pe(pe, 0)
            spread_pe(pe, 0, group=1)
            pe.wait_ge(zero_ready, 1)
            pe.wait_ge(cond_ready, 1)
            pe.matmul(PX[:, 0, 0:32], ONES[:], ZERO[:], start=True, stop=False, skip_group_check=True)
            for k in BY_PE:
                pe.wait_ge(wm_in[k % WS], 16 * (k // WS + 1))
                for j in range(16):
                    ins = pe.matmul(PX[:, 0, 2 * j:2 * j + 2], WM[:, k % WS, j * P:(j + 1) * P], SC[:, :, k],
                                    start=False, stop=False, skip_group_check=True)
                ins.then_inc(wm_used, 1)
            for c in range(2):
                pe.wait_ge(wm_added, 2 * len(BY_DVE) - 1 + c)
                for j in range(16):
                    ins = pe.matmul(PX[:, 0, 2 * j + c:2 * j + c + 1], ACC[:, c, j * P:(j + 1) * P], ONES[:, 0:1],
                                    start=False, stop=True, skip_group_check=True)
            ins.then_inc(mod_done, 1)
            project(pe, 0, 0, 0, hhi, hlo, ready=lambda k: pe.wait_ge(h_lo, k + 1))

        @block.scalar
        def _(act):
            with nc.allow_non_contiguous_dma("vectors, one element per partition"):
                act.dma_start(CD[:, 0, :], a["c"].rearrange("b (k p) -> p (b k)", p=P)).then_inc(cond_in, 16)
                act.dma_start(CD[:, 1, :], a["c_ctx"].rearrange("(k p) -> p k", p=P)).then_inc(cond_in, 16)
                act.dma_start(ONES[:], a["ones"]).then_inc(const_in, 16)
                for l in range(2):
                    act.dma_start(BM[:, l, :], a["b_mod"][l].rearrange("(j p) -> p j", p=P)).then_inc(gains_in, 16)
                    act.dma_start(GN[:, 0, l, :], a["g_pre"][l].rearrange("(k p) -> p k", p=P)).then_inc(gains_in, 16)
                    act.dma_start(GN[:, 1, l, :], a["g_post"][l].rearrange("(k p) -> p k", p=P)).then_inc(gains_in, 16)
            act.wait_ge(cond_in, 32)
            act.activation(SC[:], CD[:], ACT.Tanh, scale=0.5).then_inc(cond_tanh, 1)
            for t in range(1, NT, 2):
                act.wait_ge(x_turned, t + 1)
                act.activation(XT[:, :, t * P:(t + 1) * P],
                               PS[:, 1, 0:2, :].rearrange("p b (k n) -> p (b k) n", n=P), ACT.Copy).then_inc(xT_act, 1)
            act.wait_ge(xT_act, 4)
            act.wait_ge(xT_dve, 5)
            squares_act(act, 0, lambda k: XT[:, k, :])
            root_act(act, 0)
            w_split_hi(act, 0, 0)
            act.wait_ge(mod_ready, 1)
            for k in range(KC):
                act.wait_ge(normed, k + 1)
                if k >= 2:
                    act.wait_ge(h_lo, k - 1)
                if k % 2 == 0:
                    for t0, t1, c in SEGS:
                        modulate(act, TMP[:, 0, t0:t1], XN[:, k, t0:t1], 0, k, c).then_inc(modulated, 1)
                act.wait_ge(modulated, 2 * (k + 1))
                act.activation(HHI[:, k, :], TMP[:, k % 2, :], ACT.Copy).then_inc(h_hi, 1)

        @block.vector
        def _(dve):
            ch = Chain(dve, dve_chain)
            dve.wait_ge(cond_tanh, 1)
            ch.link(dve.scalar_tensor_tensor(SC[:], SC[:], 1.0, CD[:], ALU.add, ALU.mult))
            dve.tensor_scalar(SC[:], SC[:], 0.5, None, ALU.mult).then_inc(cond_ready, 1)
            for t in range(0, NT, 2):
                dve.wait_ge(x_turned, t + 1)
                dve.tensor_copy(XT[:, :, t * P:(t + 1) * P],
                                PS[:, 0, 0:2, :].rearrange("p b (k n) -> p (b k) n", n=P)).then_inc(xT_dve, 1)
            for n, k in enumerate(BY_DVE):
                if n == 2:
                    stats_dve(dve, 0, sq_used, KC)
                dve.wait_ge(wm_in[k % WS], 16 * (k // WS + 1))
                for c in range(2):
                    s = SC[:, c, k:k + 1]
                    if n == 0:
                        if c == 0:
                            dve.wait_ge(cond_ready, 1)
                        dve.tensor_scalar(ACC[:, c], WM[:, k % WS], s, None, ALU.mult).then_inc(wm_added, 1)
                    else:
                        dve.wait_ge(wm_added, 2 * n - 1 + c)
                        dve.scalar_tensor_tensor(ACC[:, c], WM[:, k % WS], s, ACC[:, c], ALU.mult, ALU.add
                                                 ).then_inc(wm_added, 1)
            w_split_lo(dve, 0, 0)
            dve.wait_ge(rstd_spread, 1)
            dve.wait_ge(xT_act, 4)
            dve.wait_ge(xT_dve, 5)
            for k in range(KC):
                dve.tensor_tensor(by_bank(XN[:, k, :]), by_bank(XT[:, k, :]), PS[:, 1, :, 0:JW], ALU.mult).then_inc(normed, 1)
            dve.wait_ge(mod_done, 1)
            dve.wait_ge(gains_in, 16 * 6)
            ch.link(dve.tensor_tensor(MD[:], PX[:, 0, 0:32].rearrange("p (j c) -> p j c", c=2),
                                      BM[:, 0, 0:16].unsqueeze(2).to_broadcast([P, 16, 2]), ALU.add))
            dve.tensor_copy(SH[:, 0], MD[:, 0:8, :])
            ch.link(dve.tensor_scalar(AM[:, 0], MD[:, 8:16, :], 1.0, None, ALU.add))
            dve.tensor_tensor(AM[:, 0], AM[:, 0], GN[:, 0, 0, :].unsqueeze(2).to_broadcast([P, 8, 2]),
                              ALU.mult).then_inc(mod_ready, 1)
            dve.wait_ge(mod_ready, 1)
            for k in range(KC):
                if k % 2 == 0:
                    if k:
                        dve.wait_ge(h_lo, k)
                    dve.wait_ge(modulated, 2 * (k + 1))
                    for t0, t1, c in SEGS:
                        dve.tensor_scalar(TMP[:, 1, t0:t1], XN[:, k + 1, t0:t1], AM[:, 0, k + 1, c:c + 1],
                                          SH[:, 0, k + 1, c:c + 1], ALU.mult, ALU.add).then_inc(modulated, 1)
                dve.wait_ge(h_hi, k + 1)
                dve.tensor_tensor(HLO[:, k, :], TMP[:, k % 2, :], HHI[:, k, :].bitcast(F32), ALU.subtract).then_inc(h_lo, 1)

        block.__exit__(None, None, None)


    def log1p(dve, ch, E, S, S2, between=None):
        ch.link(dve.tensor_scalar(S, E, 2.0, None, ALU.add))
        ch.link(dve.reciprocal(S, S))
        ch.link(dve.tensor_tensor(S, S, E, ALU.mult))
        ch.link(dve.tensor_tensor(S2, S, S, ALU.mult))
        ch.link(dve.tensor_scalar(E, S2, 1.0 / 17, None, ALU.mult))
        for m in range(7, 0, -1):
            ch.link(dve.scalar_tensor_tensor(E, E, 1.0 / (2 * m + 1), S2, ALU.add, ALU.mult))
            if between:
                between(m)
        ch.link(dve.scalar_tensor_tensor(E, E, 1.0, S, ALU.add, ALU.mult))
        ch.link(dve.tensor_scalar(S, E, 2.0, None, ALU.mult))

    mix_zone = [zone]
    GZ = sb("z_silu", [P, T], at=mix_zone)
    ZH = sb("z_half", [P, T], at=mix_zone)
    YT = sb("mixed_y", [P, T], at=mix_zone)
    FIN = sb("lru_final", [P, 2, KC], at=mix_zone)
    CH = sb("channel_dft", [P, 2, P], at=mix_zone)
    TB = sb("token_dft", [P, 8, 2, P], at=mix_zone)
    WF = sb("w_four", [P, 2, P], at=mix_zone)
    B4 = sb("b_four", [P, KC], at=mix_zone)
    four_only = 4 * (T + NT * 2 * P + 12 * 2 * P + 8 * 2 * P + 2 * P) + 128
    lru_zone = [(mix_zone[0] + four_only + 31) // 32 * 32]
    r_out, i_out, lru_y_ready, lru_y_out = (sem(s) for s in (
        "r_evacuated", "i_evacuated", "lru_y_ready", "lru_y_stored"))
    table_in = sem("tables_loaded")
    wf_in = [sem("w_four_loaded_0"), sem("w_four_loaded_1")]

    def lru():
        z = list(lru_zone)
        LT = sb("lru_softplus", [P, 3, 2 * KC], at=z)
        GW = sb("gate_weights", [P, 4, P], at=z)
        XA = sb("xa_padded", [P, TP + 3], at=z)
        XC = sb("xa_convolved", [P, TP], at=z)
        T1 = sb("gate_r", [P, 2, TP], at=z)
        T2 = sb("gate_i", [P, 2, TP], at=z)
        A = sb("decay", [P, 2, TP], at=z)
        HT = sb("tanh_then_state", [P, 2, TP], at=z)
        gw_in = sem("gate_weights_loaded")
        mm = sem("lru_products")
        z_out, x_out = sem("za_evacuated"), sem("xa_evacuated")
        pads, conv, squared, var1, root = (sem(s) for s in (
            "pads_zero", "xa_conv_ready", "decay_ready", "one_minus_a2_ready", "root_ready"))
        y_ready, y_out = lru_y_ready, lru_y_out
        lam_exp, prm_ready, fin_out = sem("lambda_exp"), sem("lru_params_ready"), sem("lru_final_stored")
        scanned, summed, summed_ctx = sem("states_ready"), sem("states_added"), sem("context_y_ready")
        r_tanh, lam_abs = sem("gate_r_read"), sem("lambda_abs")
        dve_chain = sem("lru_dve_chain")

        def on_gpsimd(pool):
            def gate_weights(i):
                for n, w in enumerate((a["w_rg"], a["w_ig"])):
                    pool.dma_start(GW[:, 2 * n:2 * n + 2, :], w[0][:, ds(i, 1)].rearrange("d a p n -> p (d a) n")
                                   ).then_inc(gw_in, 16)

            def finish_y(i, first):
                parts = ((0, NCTX, 0), (NCTX, T, LAT))
                pool.wait_ge(scanned, i + 1)
                for t0, t1, p0 in parts:
                    both = HT[:, 0, p0:p0 + t1 - t0]
                    pool.tensor_tensor(both, both, HT[:, 1, p0:p0 + t1 - t0], ALU.add).then_inc(summed, 1)
                pool.wait_ge(summed, i * 2 + 2)
                if not first:
                    pool.wait_ge(y_out, i * 16)
                for t0, t1, p0 in parts:
                    ins = pool.tensor_tensor(YT[:, t0:t1], HT[:, 0, p0:p0 + t1 - t0], GZ[:, t0:t1], ALU.mult)
                    if t0 == 0:
                        ins.then_inc(summed_ctx, 1)
                ins.then_inc(y_ready, 1)
                pool.wait_ge(summed_ctx, i + 1)
                pool.wait_ge(y_ready, i + 1)
                pool.dma_start(y_dram[ds(i, 1)].rearrange("a p t -> p (a t)"), YT[:]).then_inc(y_out, 16)

            gate_weights(0)
            for slot in range(2):
                pool.dma_start(WF[:, slot, :], a["w_four"][0, slot]).then_inc(wf_in[slot], 16)

            def block_of(i, first):
                pool.wait_ge(mm, i * 4 + 4)
                gate_weights(i + 1)
                finish_y(i, first)

            block_of(0, True)
            with pool.Fori(1, KC - 1) as i:
                block_of(i, False)
            finish_y(KC - 1, False)
            with nc.allow_non_contiguous_dma("final states, one element per partition"):
                for d in range(2):
                    pool.dma_start(out["new_lru"][0, 0, d].rearrange("(k p) -> p k", p=P), FIN[:, d, :]).then_inc(fin_out, 16)
            pool.wait_ge(y_out, 16 * KC)
            pool.wait_ge(fin_out, 32)

        def on_sync(sp):
            with nc.allow_non_contiguous_dma("a vector, one element per partition"):
                sp.dma_start(B4[:], a["b_four"][0].rearrange("(k p) -> p k", p=P)).then_inc(table_in, 16)
            sp.dma_start(CH[:], a["channel_dft"]).then_inc(table_in, 16)
            sp.dma_start(TB[:], a["token_dft"]).then_inc(table_in, 16)
            with sp.Fori(0, KC - 1) as i:
                w_load(sp, i + 1, 0, in_tile(a["w_in_e"][0], i * P + P))
                w_load(sp, i + 1, 1, in_tile(a["w_in_e"][0], i * P + P + D))
            for slot in range(2):
                w_load(sp, KC, slot, in_tile(a["w_in_e"][0], (2 + slot) * D))

        def on_tensor(pe):
            def block_of(i, first):
                if not first:
                    pe.wait_ge(r_out, i * 2)
                    project(pe, i, 0, 0, hhi, hlo)
                    pe.wait_ge(i_out, i * 2)
                project(pe, i, 1, 1, hhi, hlo)
                pe.wait_ge(gw_in, i * 32 + 32)
                pe.wait_ge(conv, i + 1)
                for d in range(2):
                    for what in range(2):
                        if what == 0:
                            pe.wait_ge(*((r_out, i * 2 + 1) if d else (x_out, i + 1)))
                        else:
                            pe.wait_ge(*((i_out, i * 2 + 1) if d else (z_out, i + 1)))
                        for j in range(NJ):
                            ins = pe.matmul(PS[:, what, j, 0:JP], GW[:, 2 * what + d, :], XC[:, j * JP:(j + 1) * JP],
                                            start=True, stop=True)
                        ins.then_inc(mm, 1)

            block_of(0, True)
            with pe.Fori(1, KC) as i:
                block_of(i, False)

        def prm(i, col):
            return PRM[:, ds(i, 1), col]

        def on_scalar(act):
            w_split_hi(act, 0, 1)
            act.wait_ge(prm_in, 16 * 13)
            act.activation(LT[:, 0, :], LAM[:].rearrange("p d k -> p (d k)"), ACT.Abs).then_inc(lam_abs, 1)
            act.wait_ge(lam_abs, 1)
            act.activation(LT[:, 0, :], LT[:, 0, :], ACT.Exp, scale=-1.0).then_inc(lam_exp, 1)
            act.wait_ge(pads, 1)
            act.wait_ge(prm_ready, 1)
            def block_of(i, first):
                projected(act, i, 0)
                if not first:
                    act.wait_ge(conv, i)
                act.activation(XA[:, 2:2 + NCTX], PS[:, 0, 0, 0:NCTX], ACT.Copy)
                act.activation(XA[:, 2 + LAT:2 + JW + GAP], PS[:, 0, 0, NCTX:JW], ACT.Copy)
                act.activation(by_bank(XA[:, 2 + JW + GAP:2 + TP]), PS[:, 0, 1:3, 0:JW], ACT.Copy).then_inc(x_out, 1)
                w_split_hi(act, i + 1, 0)
                projected(act, i, 1)
                if not first:
                    act.wait_ge(y_ready, i)
                act.activation(by_bank(GZ[:]), PS[:, 1, :, 0:JW], ACT.Tanh, scale=0.5)
                act.activation(by_bank(ZH[:]), PS[:, 1, :, 0:JW], ACT.Copy, scale=0.5).then_inc(z_out, 1)

                def gates_out(d):
                    act.wait_ge(mm, i * 4 + 1 + 2 * d)
                    act.activation(by_bank(T1[:, d, :], JP), PS[:, 0, :, 0:JP], ACT.Tanh, scale=0.5,
                                   bias=prm(i, HBR + 5 * d)).then_inc(r_out, 1)
                    act.wait_ge(mm, i * 4 + 2 + 2 * d)
                    act.activation(by_bank(T2[:, d, :], JP), PS[:, 1, :, 0:JP], ACT.Tanh, scale=0.5,
                                   bias=prm(i, HBI + 5 * d)).then_inc(i_out, 1)

                def decay(d):
                    act.wait_ge(r_out, i * 2 + 1 + d)
                    act.activation(A[:, d, :], T1[:, d, :], ACT.Exp, scale=prm(i, NEG + 5 * d),
                                   bias=prm(i, NEG + 5 * d)).then_inc(r_tanh, 1)

                def decay_squared(d):
                    act.activation(HT[:, d, :], T1[:, d, :], ACT.Tanh, scale=prm(i, POS + 5 * d),
                                   bias=prm(i, POS + 5 * d)).then_inc(r_tanh, 1)
                    act.wait_ge(r_tanh, i * 4 + 2 + 2 * d)
                    act.activation(T1[:, d, :], A[:, d, :], ACT.Square).then_inc(squared, 1)

                gates_out(0)
                decay(0)
                gates_out(1)
                decay_squared(0)
                decay(1)
                decay_squared(1)
                w_split_hi(act, i + 1, 1)
                for d in range(2):
                    act.wait_ge(var1, i * 2 + 1 + d)
                    act.activation(T1[:, d, :], T1[:, d, :], ACT.Sqrt, scale=0.25).then_inc(root, 1)

            block_of(0, True)
            with act.Fori(1, KC) as i:
                block_of(i, False)

        def on_vector(dve):
            ch = Chain(dve, dve_chain)
            dve.memset(XA[:], 0.0).then_inc(pads, 1)
            w_split_lo(dve, 0, 1)
            dve.wait_ge(prm_in, 16 * 13)
            dve.wait_ge(lam_exp, 1)
            log1p(dve, ch, LT[:, 0, :], LT[:, 1, :], LT[:, 2, :])
            lam = LAM[:].rearrange("p d k -> p (d k)")
            ch.link(dve.tensor_scalar(LT[:, 0, :], lam, -1.0, 0.0, ALU.mult, ALU.max))
            ch.link(dve.tensor_tensor(LT[:, 1, :], LT[:, 0, :], LT[:, 1, :], ALU.add))
            for d in range(2):
                sp_d = LT[:, 1, KC * d:KC * d + KC]
                dve.tensor_scalar(PRM[:, :, NEG + 5 * d], sp_d, -4.0, None, ALU.mult)
                dve.tensor_scalar(PRM[:, :, POS + 5 * d], sp_d, 4.0, None, ALU.mult)
                for col in (HBR, HBI):
                    ins = dve.tensor_scalar(PRM[:, :, col + 5 * d], PRM[:, :, col + 5 * d], 0.5, None, ALU.mult)
            ins.then_inc(prm_ready, 1)
            dve.wait_ge(prm_ready, 1)

            def convolve(i, first=False):
                dve.wait_ge(x_out, i + 1)
                if not first:
                    dve.wait_ge(mm, i * 4)
                ch.link(dve.tensor_scalar(XC[:], XA[:, 0:TP], prm(i, TAP), prm(i, CB), ALU.mult, ALU.add))
                for j in range(1, 4):
                    ins = dve.scalar_tensor_tensor(XC[:], XA[:, j:j + TP], prm(i, TAP + j), XC[:], ALU.mult, ALU.add)
                    if j < 3:
                        ch.link(ins)
                ins.then_inc(conv, 1)

            convolve(0, first=True)
            before, LINKS = ch.n, 8

            def block_of(i, first, last=False):
                w_split_lo(dve, i + 1, 0)
                dve.wait_ge(z_out, i + 1)
                ch.link(dve.scalar_tensor_tensor(GZ[:], GZ[:], 1.0, ZH[:], ALU.add, ALU.mult))
                dve.wait_ge(conv, i + 1)
                for d in range(2):
                    dve.wait_ge(i_out, i * 2 + 1 + d)
                    dve.scalar_tensor_tensor(T2[:, d, :], T2[:, d, :], 1.0, XC[:], ALU.add, ALU.mult)
                    dve.wait_ge(squared, i * 2 + 1 + d)
                    dve.scalar_tensor_tensor(T1[:, d, :], T1[:, d, :], 1.0, HT[:, d, :], ALU.add,
                                             ALU.mult).then_inc(var1, 1)
                w_split_lo(dve, i + 1, 1)
                for d in range(2):
                    dve.wait_ge(root, i * 2 + 1 + d)
                    ch.link(dve.tensor_tensor(T2[:, d, :], T2[:, d, :], T1[:, d, :], ALU.mult))
                    for t0, t1, h0 in ((0, NCTX, 0.0), (LAT, TP, prm(i, H0 + 5 * d))):
                        w = slice(t0, t1) if d == 0 else slice(t1 - 1, None if t0 == 0 else t0 - 1, -1)
                        ins = dve.tensor_tensor_scan(HT[:, d, w], A[:, d, w], T2[:, d, w], h0, op0=ALU.mult, op1=ALU.add)
                    ch.link(ins)
                    ins = dve.tensor_copy(FIN[:, d, ds(i, 1)], HT[:, d, NCTX - 1:NCTX] if d == 0 else HT[:, d, 0:1])
                ins.then_inc(scanned, 1)
                if not last:
                    convolve(i + 1)

            block_of(0, True)
            assert ch.n == before + LINKS, ch.n - before
            with dve.Fori(1, KC - 1) as i:
                ch.base, ch.n = before + i * LINKS, 0
                block_of(i, False)
            ch.base, ch.n = before + (KC - 1) * LINKS, 0
            block_of(KC - 1, False, last=True)

        return {"sync": on_sync, "gpsimd": on_gpsimd, "tensor": on_tensor, "scalar": on_scalar, "vector": on_vector}

    def fourier():
        z = list(mix_zone)
        CW = sb("channel_weights", [P, 2, P], at=z)
        XB = sb("xb", [P, T], at=z)
        Z = sb("token_major", [P, NT, 2, P], at=z)
        S = sb("butterfly", [P, 2, 4, 2, P], at=z)
        M = sb("butterfly_mid", [P, 4, 2, P], at=z)
        TF = sb("transformed", [P, 8, 2, P], at=z)
        assert z[0] <= lru_zone[0]
        z = list(lru_zone)
        WM = sb("w_mod_rest", [P, 4 * D], at=z)
        ACC = sb("mod_by_partition", [P, 2, 4 * D], at=z)
        MD = sb("mod_rest", [P, 32, 2], at=z)
        wm_in, mod_part, mod_done = sem("w_mod_rest_loaded"), sem("mod_rest_added"), sem("mod_rest_summed")
        cw_done, cw_out = sem("cw_product"), sem("cw_ready")
        f_done, ua_done, ub_done = sem("dft_product"), sem("ua_product"), sem("ub_product")
        xb_out, ua_out, ub_out, zb_out, y_ready, y_out = (sem(s) for s in (
            "xb_ready", "ua_ready", "ub_ready", "zb_ready", "fourier_y_ready", "fourier_y_stored"))
        tf_ready = sem("token_transform_ready")
        dve_chain = sem("fourier_dve_chain")
        half = 1.0 / np.sqrt(2.0)

        def on_sync(sp):

            def w_mod_rows(k):
                for l, (c0, c1, at) in enumerate(((2 * D, 3 * D, 0), (0, 3 * D, D))):
                    sp.dma_start(WM[:, at:at + c1 - c0],
                                 a["w_mod"][l].rearrange("(k p) n -> k p n", p=P)[ds(k, 1), :, c0:c1].rearrange(
                                     "a p n -> p (a n)")).then_inc(wm_in, 16)

            for slot in range(2):
                w_load(sp, KC + 1, slot, in_tile(a["w_in_e"][0], P + (2 + slot) * D))
            sp.wait_ge(lru_y_ready, KC)
            w_mod_rows(0)
            sp.wait_ge(mod_part, 2)
            w_mod_rows(1)
            with sp.Fori(1, KC - 1) as i:
                w_load(sp, i + KC + 1, 0, in_tile(a["w_in_e"][0], i * P + P + 2 * D))
                w_load(sp, i + KC + 1, 1, in_tile(a["w_in_e"][0], i * P + P + 3 * D))
                sp.wait_ge(mod_part, i * 2 + 2)
                w_mod_rows(i + 1)
            for slot in range(2):
                w_load(sp, 2 * KC, slot, out_tile(a["w_out_e"][0], slot, 0))
            projected(sp, 2 * KC - 1, 1)
            for n in range(KC):
                sp.wait_ge(*((lru_y_out, 16 * KC) if n < KC // 2 else (y_out, 16 * (2 * n - KC + 2))))
                load_y(sp, n)

        def on_gpsimd(pool):
            def store_y(i):
                pool.wait_ge(y_ready, i + 1)
                pool.dma_start(y_dram[ds(i + KC, 1)].rearrange("a p t -> p (a t)"), YT[:]).then_inc(y_out, 16)

            with pool.Fori(0, KC // 2 - 1) as m:
                for slot in range(2):
                    pool.wait_ge(cw_done, m * 2 + 1 + slot)
                    pool.dma_start(WF[:, slot, :], a["w_four"][0][ds(m * 2 + 2 + slot, 1)].rearrange("a p n -> p (a n)")
                                   ).then_inc(wf_in[slot], 16)
                    store_y(m * 2 + slot)
            store_y(KC - 2)
            store_y(KC - 1)
            pool.wait_ge(y_out, 16 * KC)

        def on_tensor(pe):
            pe.wait_ge(table_in, 48)

            def channel_weights(m, slot):
                pe.wait_ge(wf_in[slot], m * 16 + 16)
                pe.wait_ge(cw_out, m * 2 + slot)
                pe.wait_ge(ub_out, m * 2 + slot)
                for part in range(2):
                    ins = pe.matmul(PX[:, 1, 256 + part * P:256 + (part + 1) * P], CH[:, part, :], WF[:, slot, :],
                                    start=True, stop=True, skip_group_check=True)
                ins.then_inc(cw_done, 1)

            def to_tokens(first, last, bank, done):
                for t in range(first, last):
                    ins = pe.matmul(bank(t - first), XB[:, t * P:(t + 1) * P], CW[:].rearrange("p a n -> p (a n)"),
                                    start=True, stop=True, skip_group_check=True)
                ins.then_inc(done, 1)

            def token_transform(i):
                pe.wait_ge(tf_ready, i + 1)
                pe.wait_ge(zb_out, i + 1)
                for k1 in range(8):
                    for part in range(2):
                        pe.matmul(PS[:, 1, k1 // 4, (k1 % 4) * P:(k1 % 4 + 1) * P], TF[:, k1, part, :],
                                  TB[:, k1, part, :], start=part == 0, stop=part == 1, skip_group_check=True)
                for part in range(2):
                    ins = pe.matmul(PS[:, 1, 2, 0:P], Z[:, 0, part, :], TB[:, 0, part, :],
                                    start=part == 0, stop=part == 1)
                ins.then_inc(f_done, 1)

            def group(i, m, slot, first):
                channel_weights(m, slot)
                if first:
                    pe.wait_ge(r_out, 2 * KC)
                else:
                    pe.wait_ge(ua_out, i)
                project(pe, i + KC, 0, 0, hhi, hlo)
                if not first:
                    token_transform(i - 1)
                pe.wait_ge(xb_out, i + 1)
                pe.wait_ge(cw_out, m * 2 + slot + 1)
                if not first:
                    pe.wait_ge(ub_out, i)
                to_tokens(0, 6, lambda t: PS[:, 0, t // 2, t % 2 * 256:t % 2 * 256 + 256], ua_done)
                to_tokens(6, 9, lambda t: PX[:, t // 2, t % 2 * 256:t % 2 * 256 + 256], ub_done)
                if first:
                    pe.wait_ge(i_out, 2 * KC)
                else:
                    pe.wait_ge(y_ready, i)
                project(pe, i + KC, 1, 1, hhi, hlo)

            group(0, 0, 0, True)
            group(1, 0, 1, False)
            with pe.Fori(1, KC // 2) as m:
                for slot in range(2):
                    group(m * 2 + slot, m, slot, False)
            pe.wait_ge(ua_out, KC)
            for c in range(2):
                if c:
                    token_transform(KC - 1)
                pe.wait_ge(mod_part, 2 * KC - 1 + c)
                for j in range(32):
                    ins = pe.matmul(PS[:, 0, 0, 2 * j + c:2 * j + c + 1], ACC[:, c, j * P:(j + 1) * P], ONES[:, 0:1],
                                    start=True, stop=True, skip_group_check=True)
            ins.then_inc(mod_done, 1)

        def on_scalar(act):
            def group(i, first):
                if not first:
                    w_split_hi(act, i + KC, 1)
                act.wait_ge(cw_done, i + 1)
                if not first:
                    act.wait_ge(ub_done, i)
                act.activation(CW[:].rearrange("p a n -> p (a n)"), PX[:, 1, 256:512], ACT.Copy).then_inc(cw_out, 1)
                projected(act, i + KC, 0)
                act.activation(by_bank(XB[:]), PS[:, 0, :, 0:JW], ACT.Copy).then_inc(xb_out, 1)
                w_split_hi(act, i + KC + 1, 0)
                act.wait_ge(ua_done, i + 1)
                flat = PS[:, 0].rearrange("p b (t r n) -> p (b t) r n", t=2, r=2)
                act.activation(Z[:, 0], flat[:, 0], ACT.Copy, scale=float(np.sqrt(NLAT / NCTX)))
                act.activation(Z[:, 1:6], flat[:, 1:6], ACT.Copy).then_inc(ua_out, 1)
                act.wait_ge(ub_done, i + 1)
                act.activation(Z[:, 6:8], PX[:, 0, :].rearrange("p (t r n) -> p t r n", t=2, r=2), ACT.Copy)
                act.activation(Z[:, 8], PX[:, 1, 0:256].rearrange("p (r n) -> p r n", r=2), ACT.Copy).then_inc(ub_out, 1)
                projected(act, i + KC, 1)
                if first:
                    act.wait_ge(lru_y_ready, KC)
                act.activation(by_bank(GZ[:]), PS[:, 1, :, 0:JW], ACT.Tanh, scale=0.5)
                act.activation(by_bank(ZH[:]), PS[:, 1, :, 0:JW], ACT.Copy, scale=0.5).then_inc(zb_out, 1)

            group(0, True)
            with act.Fori(1, KC) as i:
                group(i, False)

        def on_vector(dve):
            ch = Chain(dve, dve_chain)

            def tt(o, x, y, op):
                return dve.tensor_tensor(o, x, y, op)

            def eight_points(i):
                add, sub = ALU.add, ALU.subtract
                dve.wait_ge(ub_out, i + 1)
                tt(S[:, 0], Z[:, 1:5], Z[:, 5:9], add)
                ch.link(tt(S[:, 1], Z[:, 1:5], Z[:, 5:9], sub))
                odd = S[:, 1]
                tt(M[:, 0:2], S[:, 0, 0:2], S[:, 0, 2:4], add)
                ch.link(tt(M[:, 2:4], S[:, 0, 0:2], S[:, 0, 2:4], sub))
                tt(TF[:, 0], M[:, 0], M[:, 1], add)
                tt(TF[:, 4], M[:, 0], M[:, 1], sub)
                tt(TF[:, 2, 0], M[:, 2, 0], M[:, 3, 1], add)
                tt(TF[:, 2, 1], M[:, 2, 1], M[:, 3, 0], sub)
                tt(TF[:, 6, 0], M[:, 2, 0], M[:, 3, 1], sub)
                ch.link(tt(TF[:, 6, 1], M[:, 2, 1], M[:, 3, 0], add))
                ch.link(dve.tensor_scalar(odd[:, 1::2], odd[:, 1::2], float(half), None, ALU.mult))
                tt(S[:, 0, 0:2, 0], odd[:, 1::2, 0], odd[:, 1::2, 1], add)
                tt(S[:, 0, 0:2, 1], odd[:, 1::2, 1], odd[:, 1::2, 0], sub)
                tt(M[:, 0, 0], odd[:, 0, 0], odd[:, 2, 1], add)
                tt(M[:, 0, 1], odd[:, 0, 1], odd[:, 2, 0], sub)
                tt(M[:, 2, 0], odd[:, 0, 0], odd[:, 2, 1], sub)
                ch.link(tt(M[:, 2, 1], odd[:, 0, 1], odd[:, 2, 0], add))
                tt(M[:, 1, 0], S[:, 0, 0, 0], S[:, 0, 1, 1], add)
                tt(M[:, 1, 1], S[:, 0, 0, 1], S[:, 0, 1, 0], sub)
                tt(M[:, 3, 0], S[:, 0, 0, 0], S[:, 0, 1, 1], sub)
                ch.link(tt(M[:, 3, 1], S[:, 0, 0, 1], S[:, 0, 1, 0], add))
                tt(TF[:, 1], M[:, 0], M[:, 1], add)
                tt(TF[:, 5], M[:, 0], M[:, 1], sub)
                tt(TF[:, 3, 0], M[:, 2, 0], M[:, 3, 1], add)
                tt(TF[:, 3, 1], M[:, 2, 1], M[:, 3, 0], sub)
                tt(TF[:, 7, 0], M[:, 2, 0], M[:, 3, 1], sub)
                tt(TF[:, 7, 1], M[:, 2, 1], M[:, 3, 0], add).then_inc(tf_ready, 1)

            def add_modulation(i, c):
                dve.wait_ge(wm_in, i * 32 + 32)
                s = SC[:, c, ds(i, 1)]
                if isinstance(i, int) and i == 0:
                    dve.tensor_scalar(ACC[:, c], WM[:], s, None, ALU.mult).then_inc(mod_part, 1)
                else:
                    dve.wait_ge(mod_part, i * 2 - 1 + c)
                    dve.scalar_tensor_tensor(ACC[:, c], WM[:], s, ACC[:, c], ALU.mult, ALU.add).then_inc(mod_part, 1)

            def gate(i):
                dve.wait_ge(zb_out, i + 1)
                ch.link(dve.scalar_tensor_tensor(GZ[:], GZ[:], 1.0, ZH[:], ALU.add, ALU.mult))

            def outputs(i, first):
                dve.wait_ge(f_done, i + 1)
                if first:
                    dve.wait_ge(lru_y_out, KC * 16)
                else:
                    dve.wait_ge(y_out, i * 16)
                b4 = B4[:, ds(i, 1)]
                by_k1 = "p (k2 k1) -> p k1 k2"
                dve.scalar_tensor_tensor(YT[:, 0:NCTX], PS[:, 1, 2, 0:P], b4, GZ[:, 0:NCTX], ALU.add, ALU.mult)
                ch.link(dve.scalar_tensor_tensor(
                    YT[:, NCTX:T].rearrange(by_k1, k1=8), PS[:, 1, 0:2, :].rearrange("p b (k n) -> p (b k) n", n=P), b4,
                    GZ[:, NCTX:T].rearrange(by_k1, k1=8), ALU.add, ALU.mult))
                dve.sem_inc(y_ready, 1)

            def group(i, last=False):
                if not isinstance(i, int) or i:
                    w_split_lo(dve, i + KC, 1)
                if not isinstance(i, int) or i:
                    outputs(i - 1, isinstance(i, int) and i == 1)
                w_split_lo(dve, i + KC + 1, 0)
                add_modulation(i, 0)
                if last:
                    add_modulation(i, 1)
                eight_points(i)
                gate(i)
                if not last:
                    add_modulation(i, 1)

            dve.wait_ge(table_in, 48)
            group(0)
            before, LINKS = ch.n, 8
            group(1)
            assert ch.n == before + LINKS, ch.n - before
            with dve.Fori(2, KC - 1) as i:
                ch.base, ch.n = before + (i - 1) * LINKS, 0
                group(i)
            ch.base, ch.n = 0, before + (KC - 2) * LINKS
            group(KC - 1, last=True)
            outputs(KC - 1, False)
            dve.wait_ge(mod_done, 1)
            mod = PS[:, 0, 0, 0:64].rearrange("p (j c) -> p j c", c=2)
            dve.tensor_tensor(MD[:, 0:8], mod[:, 0:8], BM[:, 0, 16:24].unsqueeze(2).to_broadcast([P, 8, 2]), ALU.add)
            ch.link(dve.tensor_tensor(MD[:, 8:32], mod[:, 8:32], BM[:, 1, :].unsqueeze(2).to_broadcast([P, 24, 2]), ALU.add))
            dve.tensor_copy(SH[:, 1], MD[:, 8:16, :])
            ch.link(dve.tensor_scalar(AM[:, 1], MD[:, 16:24, :], 1.0, None, ALU.add))
            dve.tensor_tensor(AM[:, 1], AM[:, 1], GN[:, 0, 1, :].unsqueeze(2).to_broadcast([P, 8, 2]), ALU.mult)
            for l, at in ((0, 0), (1, 24)):
                dve.tensor_tensor(GP[:, l], MD[:, at:at + 8, :], GN[:, 1, l, :].unsqueeze(2).to_broadcast([P, 8, 2]), ALU.mult)

        return {"sync": on_sync, "gpsimd": on_gpsimd, "tensor": on_tensor, "scalar": on_scalar, "vector": on_vector}

    def mix():
        phases = [lru(), fourier()]
        with nc.Block() as block:
            @block.sync
            def _(sp):
                for phase in phases:
                    phase["sync"](sp)

            @block.gpsimd
            def _(pool):
                for phase in phases:
                    phase["gpsimd"](pool)

            @block.tensor
            def _(pe):
                for phase in phases:
                    phase["tensor"](pe)

            @block.scalar
            def _(act):
                for phase in phases:
                    phase["scalar"](act)

            @block.vector
            def _(dve):
                for phase in phases:
                    phase["vector"](dve)

    gate_zone = [zone + 2 * KC * T * 4 - 3 * KC * P * 4]
    GWR = sb("gate_w_raw", [P, KC * P], at=gate_zone)
    GWH = sb("gate_w_hi", [P, KC * P], F32R, at=gate_zone)
    GWL = sb("gate_w_lo", [P, KC * P], F32R, at=gate_zone)
    assert norm_zone[0] <= gate_zone[0] - 3 * KC * P * 4
    gw_in, gw_hi, gw_lo, gates_done = sem("gate_w_loaded"), sem("gate_w_hi_ready"), sem("gate_w_lo_ready"), sem("gates_product")

    def outputs(l, w_out, pair0, next_tiles, y_stored=None):
        z = [zone]
        YHI = sb(f"y_hi_{l}", [P, 2 * KC, T], F32R, at=z)
        OUT = sb(f"out_{l}", [P, KC, T], at=z)
        PIECE = sb(f"out_squares_{l}", [P, JW], at=z)
        z = list(norm_zone)
        SLOTS = 4
        POOL_CHUNKS = (2, 4, 6) if l == 0 else ()
        if l == 1:
            ROWS = sb("out_rows", [P, SLOTS, D], at=z)
            row_out = [sem(f"rows_stored_{n}") for n in range(SLOTS)]
            turned, rows_ready = sem("rows_turned"), sem("rows_ready")
        x_by_pool = sem(f"x_ready_by_pool_{l}")
        BY_POOL = KC - 4
        piece_ready, piece_used = sem(f"out_squares_ready_{l}"), sem(f"out_squares_summed_{l}")
        y_hi, y_lo, out_ready = sem(f"y_hi_ready_{l}"), sem(f"y_lo_ready_{l}"), sem(f"out_ready_{l}")
        x_in, scaled, x_ready, x_out = (sem(f"{s}_{l}") for s in ("residual_loaded", "out_normed", "x_ready", "x_stored"))
        last = pair0 + KC
        block = nc.Block()
        block.__enter__()

        def chunk_ready(eng, k):
            if k in POOL_CHUNKS:
                eng.wait_ge(x_by_pool, POOL_CHUNKS.index(k) + 1)
            else:
                eng.wait_ge(x_ready, k + 1 - sum(n < k for n in POOL_CHUNKS))

        def ylo(k):
            return (HHI if k < KC else HLO)[:, k % KC, :]

        @block.sync
        def _(sp):
            if y_stored:
                sp.wait_ge(y_stored, 16 * H)
                load_y(sp, KC - 1)
            with sp.Fori(0, KC - 1) as o:
                for half in range(2):
                    w_load(sp, o + pair0 + 1, half, out_tile(w_out, half, o * P + P))
            if next_tiles:
                for slot in range(2):
                    w_load(sp, last, slot, next_tiles[slot])
            projected(sp, last - 1, 0)
            sp.dma_start(XT[:], x_dram.rearrange("k p t -> p k t")).then_inc(x_in, 16)
            if l == 0:
                projected(sp, last - 1, 1)
                sp.dma_start(GWR[:].rearrange("p (k n) -> p k n", k=KC),
                             in_tile(a["w_in_o"][0], a["w_in_o"].shape[2] - P)).then_inc(gw_in, 16)
                for k in (KC - 2, KC - 1):
                    chunk_ready(sp, k)
                sp.dma_start(x_dram.rearrange("k p t -> p k t"), XT[:]).then_inc(x_out, 16)
                sp.wait_ge(x_out, 16)
            else:
                for t in range(NT):
                    sp.wait_ge(rows_ready, t + 1)
                    dst = out["y_prompt"][0] if t == 0 else out["y_sample"][0, (t - 1) * P:t * P, :]
                    sp.dma_start(dst, ROWS[:, t % SLOTS, :]).then_inc(row_out[t % SLOTS], 16)
                for n in range(SLOTS):
                    sp.wait_ge(row_out[n], 16 * ((NT - n - 1) // SLOTS + 1))

        def place(t):
            return PX[:] if t % 2 else PS[:, 1, 0:2, :]

        @block.gpsimd
        def _(pool):
            for k in POOL_CHUNKS:
                pool.wait_ge(scaled, k + 1)
                pool.tensor_tensor(XT[:, k, :], OUT[:, k, :], XT[:, k, :], ALU.add).then_inc(x_by_pool, 1)
            if l == 1:
                for j in range(NJ):
                    for k in range(BY_POOL, KC):
                        pool.wait_ge(scaled, j * KC + k - BY_POOL + 1)
                        w = slice(j * JW, (j + 1) * JW)
                        pool.tensor_tensor(XT[:, k, w], OUT[:, k, w], XT[:, k, w], ALU.add).then_inc(x_by_pool, 1)

        @block.tensor
        def _(pe):
            def add_squares(o, j, start=False, stop=False):
                pe.wait_ge(piece_ready, o * NJ + (j + 1))
                pe.matmul(PX[32 * j:32 * j + 32, 1, 0:JW], ONES[:, 0:32], PIECE[:], start=start, stop=stop
                          ).then_inc(piece_used, 1)

            def out_block(o, group, free, ready=None, squares=True, first=False):
                if free is not None:
                    pe.wait_ge(out_ready, free)
                for half in range(2):
                    project(pe, o + pair0, half, group, lambda k: YHI[:, k, :], ylo, k0=half * KC,
                            start=half == 0, stop=half == 1, ready=ready,
                            middle=(lambda: add_squares(o - 1, 2 * half, start=first)) if squares else None)
                    if squares and half == 0:
                        add_squares(o - 1, 1, start=first)

            out_block(0, 0, None, lambda k: pe.wait_ge(y_lo, k + 1), squares=False)
            out_block(1, 1, None, first=True)
            with pe.Fori(1, KC // 2) as m:
                for b in range(2):
                    out_block(m * 2 + b, b, m * 2 + b - 1)
            for j in range(NJ):
                add_squares(KC - 1, j, stop=True)
            spread_pe(pe, 2 * l + 1)
            if l == 0:
                squares_pe(pe, 1)
                spread_pe(pe, 2)
                pe.wait_ge(gw_lo, 1)
                for k in range(KC):
                    pe.wait_ge(h_lo, KC + k + 1)
                    for m, (w, h) in enumerate(((GWH, HHI), (GWH, HLO), (GWL, HHI))):
                        for j in range(NJ):
                            ins = pe.matmul(PS[:, 1, j, 0:JW], w[:, k * P:(k + 1) * P], h[:, k, j * JW:(j + 1) * JW],
                                            start=k == 0 and m == 0, stop=k == KC - 1 and m == 2)
                ins.then_inc(gates_done, 1)
            else:
                for t in range(NT):
                    if t % NJ == 0:
                        pe.wait_ge(x_ready, BY_POOL * (t // NJ + 1))
                        pe.wait_ge(x_by_pool, (KC - BY_POOL) * (t // NJ + 1))
                    if t >= 2:
                        pe.wait_ge(rows_ready, t - 1)
                    for k in range(KC):
                        ins = pe.transpose(place(t)[:, k // 4, (k % 4) * P:(k % 4 + 1) * P],
                                           XT[:, k, t * P:(t + 1) * P], IDENT[:])
                    ins.then_inc(turned, 1)

        @block.scalar
        def _(act):
            for k in range(2 * KC):
                if k == 4 and y_stored:
                    act.wait_ge(y_stored, 16 * H)
                if k % 2 == 0:
                    act.wait_ge(y_in[k // 2], 16 * (l + 1))
                act.activation(YHI[:, k, :], ylo(k).bitcast(F32), ACT.Copy).then_inc(y_hi, 1)
                if k == 3:
                    w_split_hi(act, pair0, 1)

            def evacuate(o, group):
                projected(act, o + pair0, 1)
                def gated(t0, t1, src, c):
                    return act.activation(OUT[:, ds(o, 1), t0:t1].rearrange("p a (j n) -> p (a j) n", n=min(JW, t1 - t0)),
                                          src, ACT.Copy, scale=GP[:, l, ds(o, 1), c:c + 1].rearrange("p a c -> p (a c)"))

                gated(0, NCTX, PS[:, group, 0:1, 0:NCTX], 1)
                gated(NCTX, JW, PS[:, group, 0:1, NCTX:JW], 0)
                gated(JW, T, PS[:, group, 1:NJ, 0:JW], 0).then_inc(out_ready, 1)
                for j in range(NJ):
                    if j or not isinstance(o, int) or o:
                        act.wait_ge(piece_used, o * NJ + j)
                    act.activation(PIECE[:], PS[:, group, j, 0:JW], ACT.Square).then_inc(piece_ready, 1)

            def out_block(o, group):
                w_split_hi(act, o + pair0 + 1, 0)
                w_split_hi(act, o + pair0 + 1, 1)
                evacuate(o, group)

            for b in range(2):
                out_block(b, b)
            with act.Fori(1, KC // 2 - 1) as m:
                for b in range(2):
                    out_block(m * 2 + b, b)
            out_block(KC - 2, 0)
            if next_tiles:
                w_split_hi(act, last, 0)
            evacuate(KC - 1, 1)
            root_act(act, 2 * l + 1)
            if l == 0:
                act.wait_ge(gw_in, 16)
                act.activation(GWH[:], GWR[:], ACT.Copy).then_inc(gw_hi, 1)
                squares_act(act, 1, lambda k: XT[:, k, :], chunk_ready)
                root_act(act, 2)
                h_act(act, 1, TMP)
            else:
                for t in range(NT):
                    act.wait_ge(turned, t + 1)
                    if t >= SLOTS:
                        act.wait_ge(row_out[t % SLOTS], 16 * (t // SLOTS))
                    act.activation(ROWS[:, t % SLOTS, :], place(t).rearrange("p b n -> p (b n)"),
                                   ACT.Copy).then_inc(rows_ready, 1)

        @block.vector
        def _(dve):
            for k in range(2 * KC):
                dve.wait_ge(y_hi, k + 1)
                dve.tensor_tensor(ylo(k), ylo(k).bitcast(F32), YHI[:, k, :].bitcast(F32), ALU.subtract).then_inc(y_lo, 1)
                if k == 3:
                    w_split_lo(dve, pair0, 1)
            with dve.Fori(0, KC - 1) as o:
                for half in range(2):
                    w_split_lo(dve, o + pair0 + 1, half)
            if next_tiles:
                w_split_lo(dve, last, 0)
            stats_dve(dve, 2 * l + 1, piece_used, KC * NJ)
            dve.wait_ge(rstd_spread, 2 * l + 2)
            dve.wait_ge(x_in, 16)
            dve.wait_ge(out_ready, KC)
            if l == 0:
                for k in range(KC + 1):
                    if k < KC:
                        dve.tensor_tensor(by_bank(OUT[:, k, :]), by_bank(OUT[:, k, :]), PS[:, 0, :, 0:JW],
                                          ALU.mult).then_inc(scaled, 1)
                    if k and k - 1 not in POOL_CHUNKS:
                        dve.wait_ge(scaled, k)
                        dve.tensor_tensor(XT[:, k - 1, :], OUT[:, k - 1, :], XT[:, k - 1, :], ALU.add).then_inc(x_ready, 1)
                dve.wait_ge(gw_hi, 1)
                dve.tensor_tensor(GWL[:], GWR[:], GWH[:].bitcast(F32), ALU.subtract).then_inc(gw_lo, 1)
                stats_dve(dve, 2, sq_used, 2 * KC)
                dve.wait_ge(x_by_pool, len(POOL_CHUNKS))
                h_dve(dve, 1, lambda k: XT[:, k, :], TMP)
            else:
                for j in range(NJ):
                    w = slice(j * JW, (j + 1) * JW)
                    for k in (*range(BY_POOL, KC), *range(BY_POOL)):
                        dve.tensor_tensor(OUT[:, k, w], OUT[:, k, w], PS[:, 0, j, 0:JW], ALU.mult).then_inc(scaled, 1)
                    for k in range(BY_POOL):
                        dve.wait_ge(scaled, j * KC + KC - BY_POOL + k + 1)
                        dve.tensor_tensor(XT[:, k, w], OUT[:, k, w], XT[:, k, w], ALU.add).then_inc(x_ready, 1)

        block.__exit__(None, None, None)

    w_o = a["w_in_o"][0]

    DK, DV = P, 2 * P
    DV1 = DV + 1
    QCOL, KCOL, VCOL, OCOL, ZCOL = 0, D, 2 * D, 4 * D, 6 * D
    PAIR0 = 3 * KC
    ROWS_N = 40
    rows_dram = nc.dram_tensor("gate_rows", (2, 2, H, T), F32).ap()
    dec_dram = nc.dram_tensor("decay_rows", (2, H, NT), F32).ap()

    mlstm_y_out = sem("y_stored")

    def mlstm():
        z = [zone]
        TOK = sb("token_scalars", [P, 3, 2, H, NT], at=z)
        DEC = sb("chunk_decay", [P, 2, H, NT], at=z)
        by_parity = [(sb(f"q_t_{p}", [P, T], at=z), sb(f"k_t_{p}", [P, T], at=z)) for p in range(1)]
        V0 = sb("v_rows_0", [P, NT, DV1], at=z)
        G = sb("out_gate", [P, 2 * T], at=z)
        TO = sb("o_tanh", [P, T], at=z)
        TZ = sb("z_tanh", [P, T], at=z)
        DM0 = sb("decay_matrix_0", [P, 2, T], at=z)
        C = sb("state", [P, 2, DV1], at=z)
        MK = sb("causal", [P, 2, P], at=z)
        TK = sb("head_scalars", [P, 3, 2, NT], at=z)
        DC = sb("head_decay", [P, 2, NT], at=z)
        TA = sb("next_head_a", [P, 2, NT], at=z)
        R = sb("inverse_den", [P, 2], at=z)
        BI, BF, M0 = (sb("row_" + n, [ROWS_N, 1], at=z) for n in ("b_i", "b_f", "m0"))
        MP, ME, DR, NM = (sb("chunk_" + n, [ROWS_N, NT], at=z) for n in ("m_before", "m_end", "decay", "m_new"))
        GP_ROWS = sb("gate_products", [P, T], at=list(z))
        V1 = sb("v_rows_1", [P, NT, DV1], at=z)
        by_parity.append((sb("q_t_1", [P, T], at=z), sb("k_t_1", [P, T], at=z)))
        rows_z = [max(z[0], zone + 2 * KC * T * 4)]
        DM1 = sb("decay_matrix_1", [P, 2, T], at=z)
        QW = sb("q_carry", [P, 2, T], at=z)
        KW = sb("k_rows", [P, 2, T], at=z)
        HS = sb("h_rows", [P, NT, DV], at=z)
        CC = sb("context_state", [P, 2, DV1], at=z)
        QT, KT = ([t[n] for t in by_parity] for n in range(2))
        V = [V0, V1]
        DM = [DM0, DM1]
        IG, FG, E, S, S2, RST, M = (sb("rows_" + n, [ROWS_N, T], at=rows_z) for n in (
            "i", "f", "e", "s", "s2", "reset", "m"))
        WI, WK, B, DEL, A = IG, FG, E, S, RST
        parts = ((0, 0), (1, 32))

        small_in, rows_sb = sem("gate_small_loaded"), sem("gates_in_sbuf")
        cleared, moved, f_ready, exp_ready, args_ready, exps_ready, neg_ready = (sem(s) for s in (
            "rows_cleared", "rows_moved", "f_rows_ready", "exp_f_ready", "exponents_ready", "exponentials_ready",
            "max_rows_ready"))
        f_abs, tok_turned, tok_ready, m_stored, stored, m_out, dec_in = (sem(s) for s in (
            "f_abs_ready", "tokens_turned", "token_scalars_ready", "max_rows_stored", "gate_rows_stored", "new_m_stored",
            "decay_spread"))

        BANK = [PS[:, 1, 0], PS[:, 1, 1], PS[:, 1, 2], PX[:, 0], PX[:, 1]]
        NUM, KV = BANK[0:2], BANK[3:5]
        KS_BANK = [BANK[2], BANK[3], BANK[4], BANK[0], BANK[1], BANK[2]]
        ROUNDS = [(0, 4), (4, 8), (8, 9)]

        mask_in, ones_ready = sem("causal_loaded"), sem("v_ones_ready")
        rows_in, carry_in, c_in = sem("max_rows_loaded"), sem("carry_rows_loaded"), sem("state_loaded")
        va_done, evacuated = sem("v_first_product"), sem("projection_evacuated")
        ks_done, ks_out = sem("k_and_scores_done"), sem("k_and_scores_evacuated")
        turned, post_out = sem("h_turned"), sem("y_ready")
        y_out = mlstm_y_out
        num_done, num_out, kv_done, c_ready = (sem(s) for s in (
            "numerator_done", "numerator_read", "state_product_done", "state_ready"))
        d_args, d_exp, p_ready, cc_out = (sem(s) for s in (
            "weights_exponent_ready", "weights_ready", "scores_ready", "context_state_stored"))
        g_ready = sem("gate_ready")
        chain = sem("mlstm_dve_chain")
        block = nc.Block()
        block.__enter__()

        def pair(j, n):
            if isinstance(j, int) and j in (0, H):
                return (PAIR0 if j == 0 else j * 4 + (PAIR0 - 4)) + n // 2, n % 2
            return j * 4 + (PAIR0 - 2 + n // 2), n % 2

        def jobs(j):
            return range(4) if isinstance(j, int) and j == 0 else range(4, 8) if isinstance(j, int) and j == H else range(8)

        def before(j, n):
            if isinstance(j, int) and j in (0, H):
                return n if j == 0 else j * 8 - 8 + n
            return j * 8 + (n - 4)

        def v_tile(j, half):
            return w_o.rearrange("(k p) n -> p k n", p=P)[:, 4 * half:4 * half + 4, ds(j * DV + VCOL, DV)]

        def tile_source(j, n):
            last = jobs(j)[-1]
            if n > last:
                if isinstance(j, int) and j == H:
                    return out_tile(a["w_out_o"][0], n - 8, 0)
                return tile_source(j + 1, n - last - 1 + (4 if isinstance(j, int) and j == H - 1 else 0))
            if n in (2, 3):
                return v_tile(j, n - 2)
            if n < 2:
                return in_tile(w_o, j * P + (QCOL, KCOL)[n])
            return in_tile(w_o, j * DV + ((OCOL, ZCOL)[n % 2] + (n - 4) // 2 * P - DV))

        def run(eng, body, chained=None):
            body(0, 0, True, False, False)
            body(1, 1, True, True, False)
            if chained:
                chained.start()
            with eng.Fori(1, H // 2 - 1) as m:
                for b in range(2):
                    if chained:
                        chained.turn(m, b)
                    body(m * 2 + b, b, True, True, True)
            if chained:
                chained.stop()
            body(H - 2, 0, True, True, True)
            body(H - 1, 1, True, True, True)
            body(H, 0, False, True, True)

        @block.sync
        def _(sp):
            sp.dma_start(MK[:], a["causal"]).then_inc(mask_in, 16)
            sp.dma_start(RST[:], a["reset"]).then_inc(small_in, 16)
            sp.wait_ge(cleared, 1)
            with nc.allow_non_contiguous_dma("vectors, one element per partition"):
                for d, r in parts:
                    sp.dma_start(BI[r:r + H, :], a["b_if"][0, d, 0].rearrange("(h o) -> h o", o=1)).then_inc(small_in, 16)
                    sp.dma_start(BF[r:r + H, :], a["b_if"][0, d, 1].rearrange("(h o) -> h o", o=1)).then_inc(small_in, 16)
                    sp.dma_start(M0[r:r + H, :], a["state_mlstm_m"][0, 0, d].rearrange("(h o) -> h o", o=1)
                                 ).then_inc(small_in, 16)
            sp.wait_ge(rows_sb, 1)
            for d, r in parts:
                for n, dst in enumerate((IG, FG)):
                    first = P - 4 * H + (2 * d + n) * H
                    sp.dma_start(dst[r:r + H, :], GP_ROWS[first:first + H, :]).then_inc(moved, 16)

            def context_state(h):
                sp.wait_ge(c_ready, h * 8 + 1)
                with nc.allow_non_contiguous_dma("normalisers, one element per partition"):
                    for d in range(2):
                        sp.dma_start(out["new_C"][0, 0, d, ds(h, 1)].rearrange("h k v -> k (h v)"),
                                     CC[:, d, 0:DV]).then_inc(cc_out, 16)
                        sp.dma_start(out["new_n"][0, 0, d, ds(h, 1)].rearrange("h k -> k h"),
                                     CC[:, d, DV:DV1]).then_inc(cc_out, 16)

            def store_y(h):
                sp.wait_ge(post_out, h * 5 + 5)
                sp.dma_start(y_dram[ds(h * 2, 2)].rearrange("b p t -> p b t"),
                             G[:].rearrange("p (b t) -> p b t", b=2)).then_inc(y_out, 16)

            def load_weights_of(j, p, after=None, count=0):
                if after:
                    sp.wait_ge(after, count)
                sp.dma_start(DM[p][:], rows_dram[0, :, ds(j, 1)].rearrange("d h t -> (d h) t").partition_broadcast(P)
                             ).then_inc(rows_in, 16)

            def body(j, p, qkv, ml, post):
                h = j - 1
                if post:
                    sp.wait_ge(num_done, h * 9)
                if ml and not post:
                    for n in (2, 3):
                        w_load(sp, *pair(j, n), tile_source(j, n))
                    load_weights_of(h, 0, m_stored, 32)
                    sp.wait_ge(d_args, 1)
                    sp.wait_ge(stored, 64)
                if ml:
                    sp.dma_start(QW[:], rows_dram[1, :, ds(h, 1)].rearrange("d h t -> (d h) t").partition_broadcast(P)
                                 ).then_inc(carry_in, 16)
                    with nc.allow_non_contiguous_dma("normalisers, one element per partition"):
                        for d in range(2):
                            sp.dma_start(C[:, d, 0:DV], a["state_mlstm_C"][0, 0, d, ds(h, 1)].rearrange("h k v -> k (h v)")
                                         ).then_inc(c_in, 16)
                            sp.dma_start(C[:, d, DV:DV1], a["state_mlstm_n"][0, 0, d, ds(h, 1)].rearrange("h k -> k h")
                                         ).then_inc(c_in, 16)
                if qkv and ml:
                    load_weights_of(j, p)
                first = jobs(j)[0] + (4 if ml and not post else 2)
                for n in range(first, jobs(j)[-1] + 3):
                    w_load(sp, *pair(j, n), tile_source(j, n))
                    if post and n == max(first, 4):
                        store_y(h - 1)
                    if ml and n == max(first, 5):
                        context_state(h)

            run(sp, body)
            projected(sp, 7 * KC - 1, 1)
            sp.wait_ge(y_out, 16 * (H - 1))
            for n in range(H - 1):
                load_y(sp, n)
            store_y(H - 1)
            sp.wait_ge(cc_out, 64 * H)

        @block.gpsimd
        def _(pool):
            pool.wait_ge(neg_ready, 1)
            for d, r in parts:
                pool.dma_start(rows_dram[0, d], M[r:r + H, :]).then_inc(m_stored, 16)
            with nc.allow_non_contiguous_dma("one element per partition"):
                for d, r in parts:
                    pool.dma_start(out["new_m"][0, 0, d].rearrange("(h o) -> h o", o=1), NM[r:r + H, 0:1]).then_inc(m_out, 16)
            pool.wait_ge(exps_ready, 4)
            for d, r in parts:
                pool.dma_start(rows_dram[1, d], WI[r:r + H, :]).then_inc(stored, 16)
                pool.dma_start(dec_dram[d], DR[r:r + H, :]).then_inc(stored, 16)
            pool.wait_ge(stored, 64)
            pool.dma_start(DEC[:].rearrange("p d h c -> p (d h c)"),
                           dec_dram.rearrange("d h c -> (d h c)").partition_broadcast(P)).then_inc(dec_in, 16)
            pool.wait_ge(dec_in, 16)
            pool.wait_ge(m_out, 32)

        @block.tensor
        def _(pe):
            def gates_to_tokens():
                pe.wait_ge(exps_ready, 4)
                for n, rows in enumerate((A, E, WK)):
                    for c in range(NT):
                        ins = pe.transpose(PS[:, 1, n, c * ROWS_N:(c + 1) * ROWS_N], rows[:, c * P:(c + 1) * P],
                                           IDENT[0:ROWS_N, 0:ROWS_N])
                ins.then_inc(tok_turned, 1)
                pe.wait_ge(tok_ready, 1)

            def k_and_scores(h, q, post, rounds):
                for r in rounds:
                    t0, t1 = ROUNDS[r % 3]
                    if post and r >= 3:
                        pe.wait_ge(num_out, h * 9)
                    if post and r in (1, 2):
                        pe.wait_ge(c_ready, h * 8)
                    if r == 5:
                        pe.wait_ge(ks_out, h * 6 + 1)
                    for t in range(t0, t1):
                        dst = KS_BANK[r][:, (t - t0) * P:(t - t0 + 1) * P]
                        cols = slice(t * P, (t + 1) * P)
                        if r < 3:
                            ins = pe.transpose(dst, KT[q][:, cols], IDENT[:])
                        else:
                            ins = pe.matmul(dst, KT[q][:, cols], QT[q][:, cols], start=True, stop=True,
                                            skip_group_check=True)
                    ins.then_inc(ks_done, 1)

            def turn_h(h, ks):
                if ks:
                    pe.wait_ge(ks_out, h * 6 + 12)
                pe.wait_ge(num_out, h * 9 + 9)
                for r in range(5):
                    for n in range(4 * r, min(4 * r + 4, 2 * NT)):
                        ins = pe.transpose(BANK[r][:, n % 4 * P:(n % 4 + 1) * P],
                                           HS[:, n % NT, n // NT * P:(n // NT + 1) * P], IDENT[:])
                    ins.then_inc(turned, 1)

            def step(h, q, s, post):
                if s == 0:
                    if not post:
                        pe.wait_ge(ones_ready, 1)
                    pe.wait_ge(p_ready, h + 1)
                    pe.wait_ge(ks_out, h * 6 + 6)
                    if post:
                        pe.wait_ge(post_out, h * 5)
                if s == 1:
                    pe.wait_ge(c_in, h * 64 + 64)
                if s < 8:
                    if s:
                        pe.wait_ge(c_ready, h * 8 + s)
                    for d in range(2):
                        t = s if d == 0 or s == 0 else 9 - s
                        ins = pe.matmul(KV[d][:, 0:DV1], KW[:, d, t * P:(t + 1) * P], V[q][:, t, :], start=True, stop=True)
                    ins.then_inc(kv_done, 1)
                else:
                    pe.wait_ge(c_ready, h * 8 + s)
                if s:
                    pe.wait_ge(num_out, h * 9 + s)
                for d in range(2):
                    t = s if d == 0 or s == 0 else 9 - s
                    cols = slice(t * P, (t + 1) * P)
                    ins = pe.matmul(NUM[d][:, 0:DV1], DM[q][:, d, cols], V[q][:, t, :], start=True, stop=s == 0)
                    if s:
                        ins = pe.matmul(NUM[d][:, 0:DV1], QW[:, d, cols], C[:, d, :], start=False, stop=True)
                ins.then_inc(num_done, 1)

            def values(j, first, last, done, middle=None):
                for k in range(KC):
                    half, kk = divmod(k, 4)
                    if kk == 0:
                        pair_n, slot = pair(j, 2 + half)
                        pe.wait_ge(w_lo, pair_n * 2 + slot + 1)
                        if middle and half:
                            middle()
                    cols = slice(kk * DV, (kk + 1) * DV)
                    for t in range(first, last):
                        n = t - first
                        dst = PS[:, 0, n // 2, n % 2 * DV:(n % 2 + 1) * DV]
                        for m, (h, w) in enumerate(((HHI, WHI), (HHI, WLO), (HLO, WHI))):
                            ins = pe.matmul(dst, h[:, k, t * P:(t + 1) * P], w[:, half, cols],
                                            start=k == 0 and m == 0 and n % 2 == 0, stop=k == KC - 1 and m == 2,
                                            skip_group_check=True)
                    if done is None and kk == 3:
                        ins.then_inc(w_used, 1)
                if done is not None:
                    ins.then_inc(done, 1)

            def body(j, p, qkv, ml, post):
                h, q = j - 1, 1 - p

                def job(n, middle=None):
                    if n not in jobs(j):
                        return
                    if not isinstance(j, int) or j or n:
                        pe.wait_ge(evacuated, before(j, n))
                    if n == 2:
                        values(j, 0, 6, va_done, middle)
                    elif n == 3:
                        values(j, 6, 9, None)
                    else:
                        project(pe, *pair(j, n), 0, hhi, hlo, middle=middle)

                def steps(*some):
                    if ml:
                        for s in some:
                            step(h, q, s, post)

                def turn_before():
                    if post:
                        turn_h(h - 1, True)

                job(0)
                if ml and not post:
                    gates_to_tokens()
                if ml:
                    k_and_scores(h, q, post, range(0, 3))
                job(1)
                if ml:
                    k_and_scores(h, q, post, range(3, 6))
                if qkv:
                    job(2, turn_before)
                    steps(0)
                    job(3)
                    steps(1)
                    job(4, lambda: steps(2))
                    steps(3)
                    job(5, lambda: steps(4))
                    steps(5)
                    job(6, lambda: steps(6))
                    steps(7)
                    job(7)
                    steps(8)
                else:
                    job(4, turn_before)
                    steps(0)
                    job(5, lambda: steps(1))
                    steps(2)
                    job(6, lambda: steps(3))
                    steps(4)
                    job(7, lambda: steps(5))
                    steps(6, 7, 8)

            run(pe, body)
            turn_h(H - 1, False)

        @block.scalar
        def _(act):
            group = PS[:, 0, :, 0:JW]
            rows = PS[:, 0].rearrange("p b (t n) -> p (b t) n", n=DV)

            def weights(j, p):
                act.wait_ge(d_args, j + 1)
                act.activation(DM[p][:], DM[p][:], ACT.Exp).then_inc(d_exp, 1)

            def body(j, p, qkv, ml, post):
                h = j - 1
                w_split_hi(act, *pair(j, jobs(j)[0] + 1))
                if not ml:
                    act.wait_ge(f_ready, 1)
                    act.activation(E[:], FG[:], ACT.Abs).then_inc(f_abs, 1)
                    act.wait_ge(f_abs, 1)
                    act.activation(E[:], E[:], ACT.Exp, scale=-1.0).then_inc(exp_ready, 1)
                elif not post:
                    act.wait_ge(args_ready, 1)
                    act.activation(WI[:], WI[:], ACT.Exp).then_inc(exps_ready, 1)
                    act.activation(E[:], S2[:], ACT.Exp, scale=-1.0).then_inc(exps_ready, 1)
                    act.activation(WK[:], WK[:], ACT.Exp).then_inc(exps_ready, 1)
                    act.activation(DR[:], DR[:], ACT.Exp).then_inc(exps_ready, 1)
                for n in jobs(j):
                    if n == 2:
                        act.wait_ge(va_done, j + 1)
                    else:
                        projected(act, *pair(j, n))
                    if n == 0:
                        ins = act.activation(by_bank(QT[p][:]), group, ACT.Copy, scale=float(DK) ** -0.5)
                    elif n == 1:
                        ins = act.activation(by_bank(KT[p][:]), group, ACT.Copy)
                    elif n == 2:
                        ins = act.activation(V[p][:, 0:6, 0:DV], rows, ACT.Copy)
                    elif n == 3:
                        ins = act.activation(V[p][:, 6:9, 0:DV], rows[:, 0:3], ACT.Copy)
                    elif n in (4, 6):
                        if post or n == 6:
                            act.wait_ge(g_ready, j * 2 + ((n - 4) // 2 - 2))
                        ins = act.activation(by_bank(TO[:]), group, ACT.Tanh, scale=0.5)
                    else:
                        b = (n - 5) // 2
                        if b == 0 and post:
                            act.wait_ge(y_out, j * 16 - 16)
                        act.activation(by_bank(TZ[:]), group, ACT.Tanh, scale=0.5)
                        ins = act.activation(by_bank(G[:, b * T:(b + 1) * T]), group, ACT.Copy, scale=0.25)
                    ins.then_inc(evacuated, 1)
                    if n < jobs(j)[-1]:
                        w_split_hi(act, *pair(j, n + 2))
                    if n == 0 and ml and not post:
                        weights(h, 1 - p)
                    if qkv and ml and n == 6:
                        weights(j, p)

            act.activation(by_bank(GP_ROWS[96:128, :]), PS[96:128, 1, :, 0:JW], ACT.Copy).then_inc(rows_sb, 1)
            run(act, body)

        @block.vector
        def _(dve):
            ch = Chain(dve, chain)

            def by_tile(ap):
                return ap.rearrange("p (c n) -> p c n", n=P)

            def forget_gates(between):
                dve.wait_ge(moved, 64)
                dve.wait_ge(small_in, 16 * 7)
                dve.tensor_scalar(FG[:], FG[:], BF[:, 0:1], None, ALU.add).then_inc(f_ready, 1)
                ch.link(dve.tensor_scalar(IG[:], IG[:], BI[:, 0:1], None, ALU.add))
                dve.wait_ge(f_ready, 1)
                dve.wait_ge(exp_ready, 1)
                log1p(dve, ch, E[:], S[:], S2[:], between)
                ch.link(dve.scalar_tensor_tensor(S[:], FG[:], 0.0, S[:], ALU.min, ALU.subtract))
                dve.tensor_tensor_scan(B[0:H, :], RST[0:H, :], S[0:H, :], 0.0, op0=ALU.mult, op1=ALU.add)
                ch.link(dve.tensor_tensor_scan(B[32:40, ::-1], RST[32:40, ::-1], S[32:40, ::-1], 0.0, op0=ALU.mult,
                                               op1=ALU.add))
                ch.link(dve.memset(DEL[:], 0.0))
                ch.link(dve.tensor_tensor(A[:], IG[:], B[:], ALU.subtract))
                dve.tensor_copy(DEL[0:H, 256::P], B[0:H, 255:T - 1:P])
                ch.link(dve.tensor_copy(DEL[32:40, 255:T - 1:P], B[32:40, 256::P]))
                for t0, t1 in ((0, NCTX), (NCTX, T)):
                    for d, r in parts:
                        w = slice(t0, t1) if d == 0 else slice(t1 - 1, None if t0 == 0 else t0 - 1, -1)
                        first = 0.0 if t0 == 0 else M0[r:r + H, 0:1]
                        ins = dve.tensor_tensor_scan(M[r:r + H, w], DEL[r:r + H, w], A[r:r + H, w], first,
                                                     op0=ALU.add, op1=ALU.max)
                ch.link(ins)
                ch.link(dve.tensor_tensor(S2[:], B[:], M[:], ALU.add))
                dve.tensor_copy(MP[0:H, 1:2], M0[0:H, :])
                dve.tensor_copy(MP[32:40, 8:9], M0[32:40, :])
                dve.tensor_copy(MP[0:H, 2:9], S2[0:H, 255:T - 1:P])
                dve.tensor_copy(MP[32:40, 1:8], S2[32:40, 256::P])
                dve.tensor_copy(ME[0:H, :], M[0:H, P - 1::P])
                dve.tensor_copy(ME[32:40, :], M[32:40, 0::P])
                dve.tensor_copy(NM[0:H, 0:1], S2[0:H, P - 1:P])
                ch.link(dve.tensor_copy(NM[32:40, 0:1], S2[32:40, 0:1]))
                rows3 = "r (c n) -> r c n"
                spread = [ROWS_N, NT, P]
                dve.tensor_tensor(WI[:].rearrange(rows3, n=P), MP[:].unsqueeze(2).to_broadcast(spread),
                                  M[:].rearrange(rows3, n=P), ALU.subtract)
                dve.tensor_tensor(WK[:].rearrange(rows3, n=P), A[:].rearrange(rows3, n=P),
                                  ME[:].unsqueeze(2).to_broadcast(spread), ALU.subtract)
                ch.link(dve.tensor_tensor(DR[:], MP[:], ME[:], ALU.subtract))
                dve.sem_inc(args_ready, 1)
                ch.link(dve.tensor_scalar(M[:], M[:], -1.0, None, ALU.mult))
                dve.sem_inc(neg_ready, 1)

            def token_scalars():
                dve.wait_ge(tok_turned, 1)
                for n in range(3):
                    for d, r in parts:
                        ins = dve.tensor_copy(TOK[:, n, d], PS[:, 1, n, 0:NT * ROWS_N].rearrange(
                            "p (c r) -> p r c", r=ROWS_N)[:, r:r + H, :])
                ch.link(ins)
                dve.sem_inc(tok_ready, 1)
                dve.wait_ge(dec_in, 16)

            def exponents(j, p):
                dve.wait_ge(rows_in, j * 16 + 16)
                ch.link(dve.tensor_copy(TA[:], TOK[:, 0, :, ds(j, 1), :].rearrange("p d h c -> p (d h) c")))
                shape = [P, NT, P]
                for d in range(2):
                    dm = by_tile(DM[p][:, d, :])
                    ch.link(dve.tensor_tensor(dm, dm, TA[:, d, :].unsqueeze(2).to_broadcast(shape), ALU.add))
                    ch.link(dve.tensor_tensor(dm, dm, MK[:, d, :].unsqueeze(1).to_broadcast(shape), ALU.add))
                dve.sem_inc(d_args, 1)

            def weigh_k(h):
                ch.link(dve.tensor_copy(TK[:], TOK[:, :, :, ds(h, 1), :].rearrange("p q d h c -> p q (d h) c")))
                ch.link(dve.tensor_copy(DC[:], DEC[:, :, ds(h, 1), :].rearrange("p d h c -> p (d h) c")))
                for r, (t0, t1) in enumerate(ROUNDS):
                    dve.wait_ge(ks_done, h * 6 + r + 1)
                    shape = [P, t1 - t0, P]
                    for d in range(2):
                        ins = dve.tensor_tensor(by_tile(KW[:, d, t0 * P:t1 * P]), by_tile(KS_BANK[r][:, 0:(t1 - t0) * P]),
                                                TK[:, 2, d, t0:t1].unsqueeze(2).to_broadcast(shape), ALU.mult)
                        if d == 0:
                            ch.link(ins)
                    ins.then_inc(ks_out, 1)

            def weigh_scores(h, q):
                dve.wait_ge(d_exp, h + 1)
                for r, (t0, t1) in enumerate(ROUNDS):
                    dve.wait_ge(ks_done, h * 6 + r + 4)
                    w = slice(t0 * P, t1 * P)
                    for d in range(2):
                        ins = dve.tensor_tensor(DM[q][:, d, w], DM[q][:, d, w], KS_BANK[3 + r][:, 0:(t1 - t0) * P], ALU.mult)
                        if d == 0:
                            ch.link(ins)
                    ins.then_inc(ks_out, 1)
                dve.wait_ge(carry_in, h * 16 + 16)
                ch.link(dve.tensor_tensor(QW[:], QW[:], QT[q][:].unsqueeze(1).to_broadcast([P, 2, T]), ALU.mult))
                dve.wait_ge(ks_out, h * 6 + 6)
                dve.sem_inc(p_ready, 1)

            def finish_y(h):
                for r in range(5):
                    dve.wait_ge(turned, h * 5 + r + 1)
                    w = slice(4 * r * P, min(4 * r + 4, 2 * NT) * P)
                    dve.tensor_tensor(G[:, w], G[:, w], BANK[r][:, 0:w.stop - w.start], ALU.mult).then_inc(post_out, 1)

            def step(h, s, post):
                tiles = (s, s if s == 0 else 9 - s)
                if s < 8:
                    dve.wait_ge(kv_done, h * 8 + s + 1)
                    if s == 0:
                        if post:
                            dve.wait_ge(cc_out, h * 64)
                        ch.link(dve.tensor_copy(CC[:, 0, :], KV[0][:, 0:DV1]))
                        dve.tensor_copy(CC[:, 1, :], KV[1][:, 0:DV1]).then_inc(c_ready, 1)
                dve.wait_ge(num_done, h * 9 + s + 1)
                if 0 < s < 8:
                    for d in range(2):
                        ins = dve.scalar_tensor_tensor(C[:, d, :], C[:, d, :], DC[:, d, tiles[d]:tiles[d] + 1],
                                                       KV[d][:, 0:DV1], ALU.mult, ALU.add)
                        if d == 0:
                            ch.link(ins)
                    ins.then_inc(c_ready, 1)
                den = PS[:, 1, 0:2, DV]
                floor = TK[:, 1].rearrange("p d c -> p (d c)")[:, tiles[0]:NT + tiles[1] + 1:NT + tiles[1] - tiles[0]]
                ch.link(dve.scalar_tensor_tensor(R[:], den, -1.0, floor, ALU.mult, ALU.max))
                ch.link(dve.tensor_tensor(R[:], den, R[:], ALU.max))
                ch.link(dve.reciprocal(R[:], R[:]))
                for d, t in enumerate(tiles):
                    if s > 4 or (s == 0 and d == 1):
                        ins = dve.scalar_tensor_tensor(HS[:, t, :], NUM[d][:, 0:DV], R[:, d:d + 1], HS[:, t, :],
                                                       ALU.mult, ALU.add)
                    else:
                        ins = dve.tensor_scalar(HS[:, t, :], NUM[d][:, 0:DV], R[:, d:d + 1], None, ALU.mult)
                    if d == 0:
                        ch.link(ins)
                ins.then_inc(num_out, 1)

            def gate(j, b):
                dve.wait_ge(evacuated, before(j, 6 + 2 * b))
                g = G[:, b * T:(b + 1) * T]
                ch.link(dve.scalar_tensor_tensor(g, TZ[:], 1.0, g, ALU.add, ALU.mult))
                dve.scalar_tensor_tensor(g, TO[:], 1.0, g, ALU.add, ALU.mult).then_inc(g_ready, 1)

            def body(j, p, qkv, ml, post):
                h, q = j - 1, 1 - p

                def split(n):
                    w_split_lo(dve, *pair(j, n))

                def steps(*some):
                    for s in some:
                        step(h, s, post)

                if not ml:
                    split(1)
                    forget_gates(lambda m: split(2) if m == 6 else split(3) if m == 2 else None)
                    split(4)
                elif qkv:
                    split(1)
                    if not post:
                        token_scalars()
                        exponents(h, q)
                        dve.memset(V[1][:, :, DV:DV1].rearrange("p t o -> p (t o)"), 1.0).then_inc(ones_ready, 1)
                    weigh_k(h)
                    split(2)
                    weigh_scores(h, q)
                    split(3)
                    if post:
                        finish_y(h - 1)
                    steps(0)
                    split(4)
                    steps(1)
                    split(5)
                    steps(2, 3)
                    split(6)
                    steps(4, 5)
                    split(7)
                    gate(j, 0)
                    steps(6, 7)
                    split(8)
                    exponents(j, p)
                    steps(8)
                    gate(j, 1)
                else:
                    split(5)
                    weigh_k(h)
                    weigh_scores(h, q)
                    finish_y(h - 1)
                    steps(0)
                    split(6)
                    steps(1, 2)
                    split(7)
                    gate(j, 0)
                    steps(3, 4)
                    split(8)
                    steps(5, 6)
                    gate(j, 1)
                    steps(7, 8)

            LINKS = 60

            class Heads:

                def start(self):
                    self.before = ch.n

                def turn(self, m, b):
                    assert b == 0 or ch.n == LINKS, ch.n
                    ch.base, ch.n = m * (2 * LINKS) + (self.before + (b - 2) * LINKS), 0

                def stop(self):
                    assert ch.n == LINKS, ch.n
                    ch.base, ch.n = 0, self.before + 2 * LINKS * (H // 2 - 2)

            dve.memset(V[0][:, :, DV:DV1].rearrange("p t o -> p (t o)"), 1.0)
            for t in (IG, FG, BI, BF, M0, M, MP, ME, NM):
                ins = dve.memset(t[:], 0.0)
            ch.link(ins)
            dve.sem_inc(cleared, 1)
            dve.wait_ge(mask_in, 16)
            run(dve, body, Heads())
            finish_y(H - 1)

        block.__exit__(None, None, None)

    setup()
    mix()
    outputs(0, a["w_out_e"][0], 2 * KC, [in_tile(w_o, 0), in_tile(w_o, D)])
    mlstm()
    outputs(1, a["w_out_o"][0], 7 * KC, None, y_stored=mlstm_y_out)


def consts():
    b, k1, k2 = np.arange(P)[:, None, None], np.arange(8)[None, :, None], np.arange(P)[None, None, :]
    turn = 2 * np.pi * (b * (k1 + 8 * k2) % NLAT) / NLAT
    token = np.stack([np.cos(turn), np.sin(turn)], axis=2)
    turn = 2 * np.pi * (np.arange(P)[:, None] * np.arange(P)[None, :] % P) / P
    channel = np.stack([np.cos(turn), -np.sin(turn)], axis=1) / np.sqrt(NLAT * P)
    t = np.arange(T) % P
    reset = np.where(np.arange(40)[:, None] < 32, t != 0, t != P - 1)
    s, t = np.arange(P)[:, None, None], np.arange(P)[None, None, :]
    hidden = np.concatenate([s > t, s < t], axis=1)
    return {"causal": np.where(hidden, np.float32(-3e38), np.float32(0)), "reset": reset.astype(np.float32), "ident": np.eye(P, dtype=np.float32), "ones": np.ones((P, P), np.float32),
            "token_dft": token.astype(np.float32), "channel_dft": channel.astype(np.float32)}


INS = ["x_prompt", "x_sample", "c", "state_lru", "state_mlstm_C", "state_mlstm_n", "state_mlstm_m", "c_ctx", "w_mod",
       "b_mod", "g_pre", "g_post", "w_in_e", "conv_w", "conv_b", "w_rg", "b_rg", "w_ig", "b_ig", "lru_lambda",
       "w_four", "b_four", "w_out_e", "w_in_o", "b_if", "w_out_o"]
OUTS = [("y_prompt", (1, NCTX, D)), ("y_sample", (1, NLAT, D)), ("new_lru", (1, 1, 2, D)),
        ("new_C", (1, 1, 2, H, 128, 256)), ("new_n", (1, 1, 2, H, 128)), ("new_m", (1, 1, 2, H))]


def kernel(**inputs):
    import concourse.bacc as bacc
    from concourse.bass_utils import run_bass_kernel_spmd

    nc = bacc.Bacc("TRN2", target_bir_lowering=False, num_devices=1)
    arrays = {n: np.ascontiguousarray(inputs[n]) for n in INS} | consts()
    arrays = {f"in_{n}": x for n, x in arrays.items()}
    a = {n[3:]: nc.dram_tensor(n, x.shape, mybir.dt.from_np(x.dtype), kind="ExternalInput").ap()
         for n, x in arrays.items()}
    out = {n: nc.dram_tensor(n, shape, F32, kind="ExternalOutput").ap() for n, shape in OUTS}
    build(nc, a, out)
    r = run_bass_kernel_spmd(nc, [arrays], core_ids=[0])
    return tuple(r.results[0][n] for n, _ in OUTS)
```
